# Optimizing a Trainium2 kernel written in Bass

```python
import jax, jax.numpy as jnp
from jax import lax
import numpy as np
import math

D_MODEL = 1024
BATCH = 1
SEQ = 1024
DEPTH = 1

MIX_WIDTH = D_MODEL
SB_HEADS = 8
SB_HEAD_DIM = 64
SB_WIDTH = SB_HEADS * SB_HEAD_DIM
SB_SCALE = SB_HEAD_DIM ** -0.5
MLA_HEADS = 4
QK_NOPE = 128
QK_ROPE = 64
V_DIM = 128
Q_LORA = 256
KV_LORA = 128
MLA_WIDTH = MLA_HEADS * V_DIM
MLA_SCALE = (QK_NOPE + QK_ROPE) ** -0.5
ROPE_BASE = 10000.0
IN_COLS = 3 * SB_WIDTH + Q_LORA + KV_LORA + QK_ROPE
D_FF = 4 * D_MODEL
BLOCK_Q = 128
NORM_EPS = 1e-6


def rmsnorm(x, g):
    xf = x.astype(jnp.float32)
    y = xf * lax.rsqrt(jnp.mean(jnp.square(xf), axis=-1, keepdims=True) + NORM_EPS)
    return (y * g.astype(jnp.float32)).astype(x.dtype)

def rope_tables(positions):
    half = QK_ROPE // 2
    inv_freq = ROPE_BASE ** (-jnp.arange(half, dtype=jnp.float32) / half)
    ang = positions.astype(jnp.float32)[..., None] * inv_freq
    return jnp.cos(ang), jnp.sin(ang)

def apply_rope(x, cos, sin):
    half = QK_ROPE // 2
    xf = x.astype(jnp.float32)
    x1, x2 = xf[..., :half], xf[..., half:]
    out = jnp.concatenate([x1 * cos - x2 * sin, x2 * cos + x1 * sin], axis=-1)
    return out.astype(x.dtype)

def stick_breaking_block(q_blk, k_pre, v_pre, t0):
    n_q, n_k = q_blk.shape[1], k_pre.shape[1]
    z = jnp.einsum('bqhd,bkhd->bhqk', q_blk, k_pre).astype(jnp.float32) * SB_SCALE
    t_idx = t0 + jnp.arange(n_q)
    s_idx = jnp.arange(n_k)
    strict = s_idx[None, :] < t_idx[:, None]
    sp = jnp.where(strict, jax.nn.softplus(z), 0.0)
    excl = lax.cumsum(sp, axis=3, reverse=True) - sp
    log_a = jax.nn.log_sigmoid(z) - excl
    a = jnp.where(strict, jnp.exp(log_a), 0.0)
    return jnp.einsum('bhqk,bkhd->bqhd', a.astype(v_pre.dtype), v_pre)

def mla_block(qn_blk, qr_blk, kn_pre, kr_pre, v_pre, t0):
    n_q, n_k = qn_blk.shape[1], kn_pre.shape[1]
    s = (jnp.einsum('bqhd,bkhd->bhqk', qn_blk, kn_pre)
         + jnp.einsum('bqhr,bkr->bhqk', qr_blk, kr_pre)).astype(jnp.float32) * MLA_SCALE
    t_idx = t0 + jnp.arange(n_q)
    s_idx = jnp.arange(n_k)
    causal = s_idx[None, :] <= t_idx[:, None]
    s = jnp.where(causal, s, jnp.finfo(jnp.float32).min)
    p = jax.nn.softmax(s, axis=-1)
    return jnp.einsum('bhqk,bkhd->bqhd', p.astype(v_pre.dtype), v_pre)

def first_inputs(seed: int = 0) -> dict:
    key = jax.random.key(seed)
    ks = jax.random.split(key, 16)

    def w(k, shape, fan_in):
        return jax.random.normal(k, shape, jnp.float32) * fan_in ** -0.5

    def g(k, shape):
        return 1.0 + 0.01 * jax.random.normal(k, shape, jnp.float32)

    return {
        'x': jax.random.normal(ks[0], (BATCH, SEQ, D_MODEL), jnp.float32),
        'positions': jnp.broadcast_to(jnp.arange(SEQ, dtype=jnp.int32), (BATCH, SEQ)),
        'attn_norm_g': g(ks[1], (DEPTH, D_MODEL)),
        'w_in': w(ks[2], (DEPTH, D_MODEL, IN_COLS), D_MODEL),
        'q_a_norm_g': g(ks[3], (DEPTH, Q_LORA)),
        'w_q_b': w(ks[4], (DEPTH, Q_LORA, MLA_HEADS * (QK_NOPE + QK_ROPE)), Q_LORA),
        'kv_a_norm_g': g(ks[5], (DEPTH, KV_LORA)),
        'w_kv_b': w(ks[6], (DEPTH, KV_LORA, MLA_HEADS * (QK_NOPE + V_DIM)), KV_LORA),
        'sb_out_norm_g': g(ks[7], (DEPTH, SB_WIDTH)),
        'mla_out_norm_g': g(ks[8], (DEPTH, MLA_WIDTH)),
        'w_o': w(ks[9], (DEPTH, MIX_WIDTH, D_MODEL), MIX_WIDTH),
        'mlp_norm_g': g(ks[10], (DEPTH, D_MODEL)),
        'w_up': w(ks[11], (DEPTH, D_MODEL, D_FF), D_MODEL),
        'w_down': w(ks[12], (DEPTH, D_FF, D_MODEL), D_FF),
        'final_norm_g': g(ks[13], (D_MODEL,)),
    }

def first_block(x, positions, attn_norm_g, w_in, q_a_norm_g, w_q_b, kv_a_norm_g, w_kv_b,
              sb_out_norm_g, mla_out_norm_g, w_o, mlp_norm_g, w_up, w_down, final_norm_g):
    bsz, seq = x.shape[0], x.shape[1]
    n_blocks = seq // BLOCK_Q
    cos, sin = rope_tables(positions)
    splits = [SB_WIDTH, 2 * SB_WIDTH, 3 * SB_WIDTH, 3 * SB_WIDTH + Q_LORA,
              3 * SB_WIDTH + Q_LORA + KV_LORA]
    h = x
    for l in range(DEPTH):
        u = rmsnorm(h, attn_norm_g[l])
        proj = jnp.einsum('bsd,de->bse', u, w_in[l])
        q_sb, k_sb, v_sb, c_q, c_kv, k_rope = jnp.split(proj, splits, axis=-1)
        q_sb = q_sb.reshape(bsz, seq, SB_HEADS, SB_HEAD_DIM)
        k_sb = k_sb.reshape(bsz, seq, SB_HEADS, SB_HEAD_DIM)
        v_sb = v_sb.reshape(bsz, seq, SB_HEADS, SB_HEAD_DIM)
        q_m = jnp.einsum('bsr,re->bse', rmsnorm(c_q, q_a_norm_g[l]), w_q_b[l])
        q_m = q_m.reshape(bsz, seq, MLA_HEADS, QK_NOPE + QK_ROPE)
        q_nope = q_m[..., :QK_NOPE]
        q_rope = apply_rope(q_m[..., QK_NOPE:], cos[:, :, None, :], sin[:, :, None, :])
        kv = jnp.einsum('bsr,re->bse', rmsnorm(c_kv, kv_a_norm_g[l]), w_kv_b[l])
        kv = kv.reshape(bsz, seq, MLA_HEADS, QK_NOPE + V_DIM)
        k_nope, v_m = kv[..., :QK_NOPE], kv[..., QK_NOPE:]
        k_rope = apply_rope(k_rope, cos, sin)
        sb_outs, mla_outs = [], []
        for i in range(n_blocks):
            t0 = i * BLOCK_Q
            t1 = t0 + BLOCK_Q
            sb_outs.append(stick_breaking_block(q_sb[:, t0:t1], k_sb[:, :t1], v_sb[:, :t1], t0))
            mla_outs.append(mla_block(q_nope[:, t0:t1], q_rope[:, t0:t1], k_nope[:, :t1],
                                      k_rope[:, :t1], v_m[:, :t1], t0))
        o_sb = jnp.concatenate(sb_outs, axis=1).reshape(bsz, seq, SB_WIDTH)
        o_mla = jnp.concatenate(mla_outs, axis=1).reshape(bsz, seq, MLA_WIDTH)
        mixed = jnp.concatenate([rmsnorm(o_sb, sb_out_norm_g[l]),
                                 rmsnorm(o_mla, mla_out_norm_g[l])], axis=-1)
        h = h + jnp.einsum('bse,ed->bsd', mixed, w_o[l])
        v = rmsnorm(h, mlp_norm_g[l])
        hid = jnp.square(jax.nn.relu(jnp.einsum('bsd,df->bsf', v, w_up[l])))
        h = h + jnp.einsum('bsf,fd->bsd', hid, w_down[l])
    return rmsnorm(h, final_norm_g)


_first_inputs = first_inputs


def first_inputs(seed=0):
    import zlib

    import numpy as np

    out = dict(_first_inputs(seed))
    spreads = {}
    factors = {'attn_norm_g': 5.217,
     'q_a_norm_g': 8.0,
     'kv_a_norm_g': 5.423,
     'sb_out_norm_g': 8.0,
     'mla_out_norm_g': 8.0,
     'mlp_norm_g': 7.71,
     'final_norm_g': 5.481}
    for name, (base, spread) in spreads.items():
        noise = np.random.default_rng([zlib.crc32(name.encode()), seed]).standard_normal(out[name].shape)
        drawn = base * np.exp(spread * noise) if base else spread * noise
        out[name] = __import__('jax').numpy.asarray(drawn.astype(out[name].dtype))
    for name, factor in factors.items():
        out[name] = (out[name] * factor).astype(out[name].dtype)
    return out


_narrow_inputs = first_inputs


def first_inputs(seed=0):

    out = dict(_narrow_inputs(seed))
    wider = {'sb_out_norm_g': 7.93, 'mla_out_norm_g': 8.21, 'mlp_norm_g': 5.71, 'final_norm_g': 6.14}
    for name, times in wider.items():
        mean = out[name].mean()
        out[name] = (mean + times * (out[name] - mean)).astype(out[name].dtype)
    return out


MEM_LEN = 256
BRANCH_WIDTH = 512
N_BRANCHES = 5
GDN_HEADS = 4
GDN_HEAD_DIM = 128
GDN_CONV = 4
GDN_CHUNK = 64
CONF_WIDTH = 31
SWA_Q_HEADS = 8
SWA_KV_HEADS = 2
SWA_HEAD_DIM = 64
WINDOW = 128
REL_BUCKETS = 32
REL_MAX_DIST = 128
LRU_BLOCKS = 8
LRU_BLOCK_W = BRANCH_WIDTH // LRU_BLOCKS
LRU_CONV = 4
LRU_C = 8.0
XATTN_HEADS = 4
XATTN_HEAD_DIM = BRANCH_WIDTH // XATTN_HEADS

SPLIT_SIZES = (3 * BRANCH_WIDTH, BRANCH_WIDTH, GDN_HEADS, GDN_HEADS,
               2 * BRANCH_WIDTH, BRANCH_WIDTH,
               SWA_Q_HEADS * SWA_HEAD_DIM, 2 * SWA_KV_HEADS * SWA_HEAD_DIM, BRANCH_WIDTH,
               BRANCH_WIDTH, BRANCH_WIDTH,
               XATTN_HEADS * XATTN_HEAD_DIM, BRANCH_WIDTH,
               N_BRANCHES * D_MODEL)
IN_COLS_2 = sum(SPLIT_SIZES)


def _rms_norm(x, g):
    xf = x.astype(jnp.float32)
    y = xf * lax.rsqrt(jnp.mean(xf * xf, axis=-1, keepdims=True) + NORM_EPS)
    return (y * g.astype(jnp.float32)).astype(x.dtype)

def _layer_norm(x, g, b):
    xf = x.astype(jnp.float32)
    mu = jnp.mean(xf, axis=-1, keepdims=True)
    var = jnp.mean(jnp.square(xf - mu), axis=-1, keepdims=True)
    y = (xf - mu) * lax.rsqrt(var + NORM_EPS)
    return (y * g.astype(jnp.float32) + b.astype(jnp.float32)).astype(x.dtype)

def _l2_norm(x):
    return x * lax.rsqrt(jnp.sum(x * x, axis=-1, keepdims=True) + NORM_EPS)

def _causal_dwconv(x, w, b=None):
    K, C = w.shape
    y = lax.conv_general_dilated(x, w[:, None, :].astype(x.dtype), window_strides=(1,),
                                 padding=((K - 1, 0),), dimension_numbers=('NWC', 'WIO', 'NWC'),
                                 feature_group_count=C)
    if b is not None:
        y = y + b.astype(x.dtype)
    return y

def _gated_delta_rule(q, k, v, g, beta):
    B, S, H, DK = q.shape
    DV = v.shape[-1]
    C = GDN_CHUNK
    N = S // C

    def chunks(t):
        return jnp.swapaxes(t.reshape((B, N, C, H) + t.shape[3:]), 2, 3)

    qc, kc, vc, gc, bc = (chunks(t) for t in (q, k, v, g, beta))
    G = jnp.cumsum(gc, axis=-1)
    idx = jnp.arange(C)
    tril = idx[:, None] >= idx[None, :]
    strict = idx[:, None] > idx[None, :]
    L = jnp.exp(jnp.where(tril, G[..., :, None] - G[..., None, :], -jnp.inf))
    kb = kc * bc[..., None]
    A = jnp.where(strict, jnp.einsum('bnhid,bnhjd->bnhij', kb, kc) * L, 0.0)
    rhs = jnp.concatenate([vc * bc[..., None], kb * jnp.exp(G)[..., None]], axis=-1)
    sol = lax.linalg.triangular_solve(A + jnp.eye(C, dtype=A.dtype), rhs, left_side=True, lower=True)
    u, w = sol[..., :DV], sol[..., DV:]
    attn = jnp.einsum('bnhid,bnhjd->bnhij', qc, kc) * L
    q_dec = qc * jnp.exp(G)[..., None]
    k_dec = kc * jnp.exp(G[..., -1:] - G)[..., None]
    chunk_decay = jnp.exp(G[..., -1])

    def step(state, inp):
        u_n, w_n, attn_n, qd_n, kd_n, cd_n = inp
        v_new = u_n - jnp.einsum('bhck,bhkv->bhcv', w_n, state)
        o = jnp.einsum('bhck,bhkv->bhcv', qd_n, state) + jnp.einsum('bhij,bhjv->bhiv', attn_n, v_new)
        state = state * cd_n[..., None, None] + jnp.einsum('bhck,bhcv->bhkv', kd_n, v_new)
        return state, o

    xs = tuple(jnp.moveaxis(t, 1, 0) for t in (u, w, attn, q_dec, k_dec, chunk_decay))
    s0 = jnp.zeros((B, H, DK, DV), q.dtype)
    _, o = lax.scan(step, s0, xs)
    o = jnp.moveaxis(o, 0, 1)
    return jnp.swapaxes(o, 2, 3).reshape(B, S, H, DV)

def _t5_bucket(dist):
    n = np.maximum(dist, 0)
    max_exact = REL_BUCKETS // 2
    large = max_exact + (np.log(np.maximum(n, 1) / max_exact) / np.log(REL_MAX_DIST / max_exact)
                         * (REL_BUCKETS - max_exact)).astype(np.int32)
    large = np.minimum(large, REL_BUCKETS - 1)
    return np.where(n < max_exact, n, large).astype(np.int32)

def _swa_sinks(q, k, v, sinks, band_bias):
    B, S, HQ, hd = q.shape
    HKV = k.shape[2]
    G = HQ // HKV
    W = WINDOW
    N = S // W
    qb = q.reshape(B, N, W, HKV, G, hd)

    def band(t):
        tb = t.reshape(B, N, W, HKV, hd)
        prev = jnp.pad(tb, ((0, 0), (1, 0), (0, 0), (0, 0), (0, 0)))[:, :-1]
        return jnp.concatenate([prev, tb], axis=2)

    kb, vb = band(k), band(v)
    s = jnp.einsum('bniKgd,bnjKd->bnKgij', qb, kb).astype(jnp.float32) * (hd ** -0.5)
    s = s + band_bias.astype(jnp.float32).reshape(1, 1, HKV, G, W, 2 * W)
    i = jnp.arange(W)[:, None]
    j = jnp.arange(2 * W)[None, :]
    dist = i + W - j
    valid = (dist >= 0) & (dist < W)
    valid = valid[None] & ((jnp.arange(N)[:, None, None] > 0) | (j >= W)[None])
    s = jnp.where(valid[None, :, None, None], s, -jnp.inf)
    sink = sinks.astype(jnp.float32).reshape(1, 1, HKV, G, 1, 1)
    m = jnp.maximum(jnp.max(s, axis=-1, keepdims=True), sink)
    p = jnp.exp(s - m)
    p = p / (jnp.sum(p, axis=-1, keepdims=True) + jnp.exp(sink - m))
    o = jnp.einsum('bnKgij,bnjKd->bniKgd', p.astype(v.dtype), vb)
    return o.reshape(B, S, HQ, hd)

def _rglru(x, w_a, b_a, w_x, b_x, lam):
    B, S, W = x.shape
    xf = x.astype(jnp.float32)
    xb = xf.reshape(B, S, LRU_BLOCKS, LRU_BLOCK_W)
    r = jax.nn.sigmoid(jnp.einsum('bsnc,ncd->bsnd', xb, w_a.astype(jnp.float32)).reshape(B, S, W) + b_a)
    ig = jax.nn.sigmoid(jnp.einsum('bsnc,ncd->bsnd', xb, w_x.astype(jnp.float32)).reshape(B, S, W) + b_x)
    log_a = -LRU_C * r * jax.nn.softplus(-lam.astype(jnp.float32))
    a = jnp.exp(log_a)
    bterm = jnp.sqrt(-jnp.expm1(2.0 * log_a)) * (ig * xf)

    def combine(left, right):
        a1, b1 = left
        a2, b2 = right
        return a1 * a2, a2 * b1 + b2

    _, h = lax.associative_scan(combine, (a, bterm), axis=1)
    return h.astype(x.dtype)

def _hybrid_mixer(h, mem, w_in, b_in, a_conv_w, a_log, a_dt_bias, a_norm_g,
                  b_dw_w, b_dw_b, b_ln_g, b_ln_b, c_sinks, band_bias,
                  d_conv_w, d_conv_b, d_w_a, d_b_a, d_w_x, d_b_x, d_lambda,
                  g_mem, w_mem_kv, w_br, w_out):
    B, S, _ = h.shape
    dt = h.dtype
    proj = h @ w_in + b_in
    offsets = [int(o) for o in np.cumsum(SPLIT_SIZES)[:-1]]
    (a_qkv, a_z, a_beta, a_alpha, b_glu, b_z, c_q, c_kv, c_z,
     d_x, d_z, e_q, e_z, gates) = jnp.split(proj, offsets, axis=-1)

    qkv = jax.nn.silu(_causal_dwconv(a_qkv, a_conv_w)).astype(jnp.float32)
    aq, ak, av = jnp.split(qkv, 3, axis=-1)
    aq = _l2_norm(aq.reshape(B, S, GDN_HEADS, GDN_HEAD_DIM)) * (GDN_HEAD_DIM ** -0.5)
    ak = _l2_norm(ak.reshape(B, S, GDN_HEADS, GDN_HEAD_DIM))
    av = av.reshape(B, S, GDN_HEADS, GDN_HEAD_DIM)
    beta = jax.nn.sigmoid(a_beta.astype(jnp.float32))
    g = -jnp.exp(a_log.astype(jnp.float32)) * jax.nn.softplus(a_alpha.astype(jnp.float32) + a_dt_bias)
    ao = _gated_delta_rule(aq, ak, av, g, beta)
    ao = _rms_norm(ao, a_norm_g).reshape(B, S, BRANCH_WIDTH).astype(dt)
    y_a = ao * jax.nn.silu(a_z)

    glu_a, glu_b = jnp.split(b_glu, 2, axis=-1)
    bu = glu_a * jax.nn.sigmoid(glu_b)
    bu = _causal_dwconv(bu, b_dw_w, b_dw_b)
    bu = jax.nn.silu(_layer_norm(bu, b_ln_g, b_ln_b))
    y_b = bu * jax.nn.silu(b_z)

    cq = c_q.reshape(B, S, SWA_Q_HEADS, SWA_HEAD_DIM)
    ck, cv = jnp.split(c_kv, 2, axis=-1)
    ck = ck.reshape(B, S, SWA_KV_HEADS, SWA_HEAD_DIM)
    cv = cv.reshape(B, S, SWA_KV_HEADS, SWA_HEAD_DIM)
    co = _swa_sinks(cq, ck, cv, c_sinks, band_bias).reshape(B, S, BRANCH_WIDTH)
    y_c = co * jax.nn.silu(c_z)

    dxc = _causal_dwconv(d_x, d_conv_w, d_conv_b)
    do = _rglru(dxc, d_w_a, d_b_a, d_w_x, d_b_x, d_lambda)
    y_d = do * jax.nn.silu(d_z)

    mem_kv = _rms_norm(mem, g_mem) @ w_mem_kv
    mk, mv = jnp.split(mem_kv, 2, axis=-1)
    mk = mk.reshape(B, MEM_LEN, XATTN_HEADS, XATTN_HEAD_DIM)
    mv = mv.reshape(B, MEM_LEN, XATTN_HEADS, XATTN_HEAD_DIM)
    eq = e_q.reshape(B, S, XATTN_HEADS, XATTN_HEAD_DIM)
    es = jnp.einsum('bshd,bmhd->bhsm', eq, mk).astype(jnp.float32) * (XATTN_HEAD_DIM ** -0.5)
    ep = jax.nn.softmax(es, axis=-1).astype(dt)
    eo = jnp.einsum('bhsm,bmhd->bshd', ep, mv).reshape(B, S, BRANCH_WIDTH)
    y_e = eo * jax.nn.silu(e_z)

    ys = jnp.stack([y_a, y_b.astype(dt), y_c.astype(dt), y_d.astype(dt), y_e.astype(dt)], axis=2)
    branch_out = jnp.einsum('bsnw,nwd->bsnd', ys, w_br)
    gate = jax.nn.sigmoid(gates.reshape(B, S, N_BRANCHES, D_MODEL))
    merged = jnp.sum(gate * branch_out, axis=2)
    return merged @ w_out

def second_inputs(seed: int = 0) -> dict:
    key = jax.random.key(seed)
    ks = jax.random.split(key, 32)
    f32 = jnp.float32
    L = DEPTH
    W = BRANCH_WIDTH

    def nrm(k, shape, scale):
        return scale * jax.random.normal(k, shape, f32)

    def gain(k, shape):
        return 1.0 + 0.05 * jax.random.normal(k, shape, f32)

    x = nrm(ks[0], (BATCH, SEQ, D_MODEL), 1.0)
    mem = nrm(ks[1], (BATCH, MEM_LEN, D_MODEL), 1.0)
    g_pre = gain(ks[2], (L, D_MODEL))
    g_post = gain(ks[3], (L, D_MODEL))
    w_in = nrm(ks[4], (L, D_MODEL, IN_COLS_2), D_MODEL ** -0.5)
    b_in = nrm(ks[5], (L, IN_COLS_2), 0.02)
    a_conv_w = nrm(ks[6], (L, GDN_CONV, 3 * W), GDN_CONV ** -0.5)
    a_log = jnp.log(jax.random.uniform(ks[7], (L, GDN_HEADS), f32, 1.0, 16.0))
    dt0 = jnp.exp(jax.random.uniform(ks[8], (L, GDN_HEADS), f32, math.log(1e-3), math.log(0.1)))
    a_dt_bias = dt0 + jnp.log(-jnp.expm1(-dt0))
    a_norm_g = gain(ks[9], (L, GDN_HEAD_DIM))
    b_dw_w = nrm(ks[10], (L, CONF_WIDTH, W), CONF_WIDTH ** -0.5)
    b_dw_b = nrm(ks[11], (L, W), 0.02)
    b_ln_g = gain(ks[12], (L, W))
    b_ln_b = nrm(ks[13], (L, W), 0.02)
    c_sinks = nrm(ks[14], (L, SWA_Q_HEADS), 0.5)
    rel_bias = nrm(ks[15], (REL_BUCKETS, SWA_Q_HEADS), 0.5)
    d_conv_w = nrm(ks[16], (L, LRU_CONV, W), LRU_CONV ** -0.5)
    d_conv_b = nrm(ks[17], (L, W), 0.02)
    d_w_a = nrm(ks[18], (L, LRU_BLOCKS, LRU_BLOCK_W, LRU_BLOCK_W), LRU_BLOCK_W ** -0.5)
    d_b_a = nrm(ks[19], (L, W), 0.02)
    d_w_x = nrm(ks[20], (L, LRU_BLOCKS, LRU_BLOCK_W, LRU_BLOCK_W), LRU_BLOCK_W ** -0.5)
    d_b_x = nrm(ks[21], (L, W), 0.02)
    u = jax.random.uniform(ks[22], (L, W), f32, 0.9, 0.999)
    a0 = u ** (1.0 / LRU_C)
    d_lambda = jnp.log(a0) - jnp.log1p(-a0)
    g_mem = gain(ks[23], (L, D_MODEL))
    w_mem_kv = nrm(ks[24], (L, D_MODEL, 2 * W), D_MODEL ** -0.5)
    w_br = nrm(ks[25], (L, N_BRANCHES, W, D_MODEL), W ** -0.5)
    w_out = nrm(ks[26], (L, D_MODEL, D_MODEL), D_MODEL ** -0.5)
    return {"x": x, "mem": mem, "g_pre": g_pre, "g_post": g_post, "w_in": w_in, "b_in": b_in,
            "a_conv_w": a_conv_w, "a_log": a_log, "a_dt_bias": a_dt_bias, "a_norm_g": a_norm_g,
            "b_dw_w": b_dw_w, "b_dw_b": b_dw_b, "b_ln_g": b_ln_g, "b_ln_b": b_ln_b,
            "c_sinks": c_sinks, "rel_bias": rel_bias,
            "d_conv_w": d_conv_w, "d_conv_b": d_conv_b, "d_w_a": d_w_a, "d_b_a": d_b_a,
            "d_w_x": d_w_x, "d_b_x": d_b_x, "d_lambda": d_lambda,
            "g_mem": g_mem, "w_mem_kv": w_mem_kv, "w_br": w_br, "w_out": w_out}

def second_block(x, mem, g_pre, g_post, w_in, b_in, a_conv_w, a_log, a_dt_bias, a_norm_g,
              b_dw_w, b_dw_b, b_ln_g, b_ln_b, c_sinks, rel_bias,
              d_conv_w, d_conv_b, d_w_a, d_b_a, d_w_x, d_b_x, d_lambda,
              g_mem, w_mem_kv, w_br, w_out):
    i = np.arange(WINDOW)[:, None]
    j = np.arange(2 * WINDOW)[None, :]
    bucket = _t5_bucket(i + WINDOW - j)
    band_bias = jnp.transpose(rel_bias[bucket], (2, 0, 1))
    for l in range(DEPTH):
        h = _rms_norm(x, g_pre[l])
        y = _hybrid_mixer(h, mem, w_in[l], b_in[l], a_conv_w[l], a_log[l], a_dt_bias[l], a_norm_g[l],
                          b_dw_w[l], b_dw_b[l], b_ln_g[l], b_ln_b[l], c_sinks[l], band_bias,
                          d_conv_w[l], d_conv_b[l], d_w_a[l], d_b_a[l], d_w_x[l], d_b_x[l], d_lambda[l],
                          g_mem[l], w_mem_kv[l], w_br[l], w_out[l])
        x = x + _rms_norm(y, g_post[l])
    return x


_first_inputs_2 = second_inputs


def second_inputs(seed=0):
    import zlib

    import numpy as np

    out = dict(_first_inputs_2(seed))
    spreads = {}
    factors = {'b_dw_b': 4.361,
     'b_ln_g': 15.089,
     'b_ln_b': 38.39,
     'c_sinks': 64.0,
     'd_b_a': 64.0,
     'd_b_x': 64.0,
     'g_mem': 8.0,
     'a_norm_g': 8.0,
     'rel_bias': 8.0,
     'd_conv_b': 5.537,
     'd_w_a': 2.975}
    for name, (base, spread) in spreads.items():
        noise = np.random.default_rng([zlib.crc32(name.encode()), seed]).standard_normal(out[name].shape)
        drawn = base * np.exp(spread * noise) if base else spread * noise
        out[name] = __import__('jax').numpy.asarray(drawn.astype(out[name].dtype))
    for name, factor in factors.items():
        out[name] = (out[name] * factor).astype(out[name].dtype)
    return out


def setup_inputs(seed=0):
    out = dict(first_inputs(seed))
    for name, value in second_inputs(seed + 1).items():
        if name != "x":
            out[name + "_2"] = value
    return out


def reference(
    x, positions, attn_norm_g, w_in, q_a_norm_g, w_q_b, kv_a_norm_g, w_kv_b, sb_out_norm_g,
    mla_out_norm_g, w_o, mlp_norm_g, w_up, w_down, final_norm_g, mem_2, g_pre_2, g_post_2,
    w_in_2, b_in_2, a_conv_w_2, a_log_2, a_dt_bias_2, a_norm_g_2, b_dw_w_2, b_dw_b_2, b_ln_g_2,
    b_ln_b_2, c_sinks_2, rel_bias_2, d_conv_w_2, d_conv_b_2, d_w_a_2, d_b_a_2, d_w_x_2, d_b_x_2,
    d_lambda_2, g_mem_2, w_mem_kv_2, w_br_2, w_out_2,
):
    x = first_block(
        x, positions, attn_norm_g, w_in, q_a_norm_g, w_q_b, kv_a_norm_g, w_kv_b, sb_out_norm_g,
        mla_out_norm_g, w_o, mlp_norm_g, w_up, w_down, final_norm_g,
    )
    return second_block(
        x, mem_2, g_pre_2, g_post_2, w_in_2, b_in_2, a_conv_w_2, a_log_2, a_dt_bias_2,
        a_norm_g_2, b_dw_w_2, b_dw_b_2, b_ln_g_2, b_ln_b_2, c_sinks_2, rel_bias_2, d_conv_w_2,
        d_conv_b_2, d_w_a_2, d_b_a_2, d_w_x_2, d_b_x_2, d_lambda_2, g_mem_2, w_mem_kv_2, w_br_2,
        w_out_2,
    )


_drawn_inputs = setup_inputs


def setup_inputs(seed=0):
    import zlib

    import numpy as np

    out = dict(_drawn_inputs(seed))
    spreads = {}
    factors = {'g_pre_2': 3.256,
     'g_post_2': 6.338,
     'b_in_2': 7.649,
     'a_log_2': 3.627,
     'a_dt_bias_2': 2.75,
     'a_norm_g_2': 26.596,
     'b_dw_b_2': 2.77,
     'b_ln_g_2': 29.917,
     'b_ln_b_2': 32.864,
     'c_sinks_2': 200.0,
     'rel_bias_2': 200.0,
     'd_conv_b_2': 62.376,
     'd_w_a_2': 64.0,
     'd_b_a_2': 64.0,
     'd_w_x_2': 64.0,
     'd_b_x_2': 42.896,
     'd_lambda_2': 56.408,
     'g_mem_2': 4.809,
     'd_conv_w_2': 8.0}
    for name, (base, spread) in spreads.items():
        noise = np.random.default_rng([zlib.crc32(name.encode()), seed]).standard_normal(out[name].shape)
        drawn = base * np.exp(spread * noise) if base else spread * noise
        out[name] = __import__('jax').numpy.asarray(drawn.astype(out[name].dtype))
    for name, factor in factors.items():
        out[name] = (out[name] * factor).astype(out[name].dtype)
    return out
```

```python
from contextlib import ExitStack, contextmanager
from math import pi

import numpy as np
import concourse.bass as bass
from concourse import mybir

F32 = mybir.dt.float32
I32 = mybir.dt.int32
ALU = mybir.AluOpType
ACT = mybir.ActivationFunctionType
AX = mybir.AxisListType

P = 128
S = 1024
NB = S // P
D = 1024
DC = D // P
HALF = 512
F_FF = 4 * D
SB_H, SB_D = 8, 64
MLA_H, NOPE, ROPE = 4, 128, 64
MLA_SCALE = float((NOPE + ROPE) ** -0.5)
Q_LORA, KV_LORA = 256, 128
MEM = 256
BW = 512
BT = BW // P
NBR = 5
CONVK, CONFK = 4, 31
EPS = 1e-6
NEG = -1e30

C_ID = 0
C_ONE = C_ID + P
C_GT = C_ONE + P
C_LE = C_GT + P
C_LT = C_LE + P
C_NGE = C_LT + P
C_NCAUSAL = C_NGE + P
C_LVL = C_NCAUSAL + P
C_FREQ = C_LVL + 7 * P
C_SGN = C_FREQ + 1
C_EPS = C_SGN + 1
C_QS = C_EPS + 1
C_W = C_QS + 8


def constants():
    p = np.arange(P)[:, None]
    f = np.arange(P)[None, :]
    c = np.zeros((P, C_W), np.float32)
    c[:, C_ID:C_ID + P] = p == f
    c[:, C_ONE:C_ONE + P] = 1
    c[:, C_GT:C_GT + P] = p > f
    c[:, C_LE:C_LE + P] = p <= f
    c[:, C_LT:C_LT + P] = p < f
    c[:, C_NGE:C_NGE + P] = np.where(p >= f, NEG, 0)
    c[:, C_NCAUSAL:C_NCAUSAL + P] = np.where(f > p, NEG, 0)
    for lvl in range(7):
        b = 1 << lvl
        same = (p // (2 * b)) == (f // (2 * b))
        c[:, C_LVL + lvl * P:C_LVL + (lvl + 1) * P] = same & (p % (2 * b) < b) & (f % (2 * b) >= b)
    half = ROPE // 2
    c[:, C_FREQ] = (10000.0 ** (-(np.arange(P) % half) / half)).astype(np.float32)
    c[:, C_SGN] = np.where(np.arange(P) % ROPE < half, -1, 1)
    c[:, C_EPS] = EPS
    c[:, C_QS:C_QS + 4] = 128.0 ** -0.5
    c[:, C_QS + 4:C_QS + 8] = 1
    return c


_PAR = [("attn_g", 8), ("q_a_g", 2), ("kv_a_g", 1), ("sb_g", 4), ("mla_g", 4), ("mlp_g", 8), ("final_g", 8),
        ("pre_g", 8), ("post_g", 8), ("mem_g", 8), ("b_in", 55), ("b_gate", 40), ("a_conv", 48), ("a_norm", 1),
        ("b_conv", 124), ("b_conv_b", 4), ("b_ln_g", 4), ("b_ln_b", 4), ("d_conv", 16), ("d_conv_b", 4),
        ("d_ba", 4), ("d_bx", 4), ("d_lam", 4), ("ab_bias", 8), ("a_log", 4), ("a_dt", 4), ("sinks", 8)]
PAR = {}
_at = 0
for _n, _w in _PAR:
    PAR[_n] = (_at, _w)
    _at += _w
PAR_W = _at

T_AQKV, T_GLU, T_CQ, T_CK, T_CV, T_DX, T_EQ = 0, 12, 20, 24, 26, 27, 31
N_PLAIN = 35
T_AZ, T_BZ, T_CZ, T_DZ, T_EZ = 35, 39, 43, 47, 51
N_IN2 = 55

A_CONST = 0
A_PAR = A_CONST + C_W
A_RES = A_PAR + PAR_W
A_ACT = A_RES + DC * S
A_SMALL = A_ACT + DC * S
A_WORK = A_SMALL + 80
A_END = 52800


class Mem:

    def __init__(self, arena, psum):
        self.arena = arena
        self.ps = psum
        self.const = arena[:, A_CONST:A_CONST + C_W]
        self.par = arena[:, A_PAR:A_PAR + PAR_W]
        self.res = arena[:, A_RES:A_RES + DC * S].rearrange("p (k t) -> p k t", t=S)
        self.act = arena[:, A_ACT:A_ACT + DC * S].rearrange("p (k t) -> p k t", t=S)
        small = arena[:, A_SMALL:A_SMALL + 80]
        self.beta = small[:, 0:32].rearrange("p (c h) -> p c h", h=4)
        self.decay = small[:, 32:64].rearrange("p (c h) -> p c h", h=4)
        self.rate = small[:, 64:68]
        self.top = A_WORK

    def c(self, at, w=P):
        return self.const[:, at:at + w]

    def p(self, name, k=0, w=1):
        at = PAR[name][0] + k
        return self.par[:, at:at + w]

    def clear(self):
        self.top = A_WORK

    def take(self, *shape):
        n = int(np.prod(shape))
        v = self.arena[:, self.top:self.top + n]
        self.top += n
        assert self.top <= A_END, self.top
        if len(shape) == 2:
            v = v.rearrange("p (a b) -> p a b", b=shape[1])
        if len(shape) == 3:
            v = v.rearrange("p (a b c) -> p a b c", b=shape[1], c=shape[2])
        return v


@contextmanager
def phase(nc, *names):
    at = nc.next_id()
    sems = [nc.alloc_semaphore(f"{n}_{at}") for n in names]
    with nc.Block() as block:
        yield (block, *sems)
    nc.clear_and_free_semaphores(sems)
    nc.all_engine_barrier()


def loop(eng, n, body):
    body(0)
    with eng.Fori(1, n) as i:
        body(i)


def load_phase(nc, m, d):
    m.clear()
    pos_i = m.take(S)
    pos, ang, turns, red = m.take(S), m.take(S), m.take(S), m.take(2, S)
    tab = m.take(2, S)
    two_pi = (6.28125, 0.0019340515136718750, 2 * pi - 6.28125 - 0.0019340515136718750)
    lim = 3.1415925
    with phase(nc, "params_in", "x_in", "pos_in", "reduced", "sines", "signed", "tables_out") as (
            block, params_in, x_in, pos_in, reduced, sines, signed, tables_out):

        @block.sync
        def _(sp):
            sp.dma_start(m.const, d["consts"]).then_inc(params_in, 16)
            sp.dma_start(m.par, d["params"]).then_inc(params_in, 16)
            sp.dma_start(pos_i.bitcast(I32), d["positions"].partition_broadcast(P)).then_inc(pos_in, 16)
            sp.dma_start(m.res, d["x"].rearrange("(k p) t -> p k t", p=P)).then_inc(x_in, 16)
            sp.wait_ge(signed, 1)
            sp.dma_start(d["rope"].rearrange("a p t -> p a t"), tab).then_inc(tables_out, 16)
            sp.wait_ge(tables_out, 16)
            sp.wait_ge(x_in, 16)
            sp.wait_ge(params_in, 32)

        @block.vector
        def _(dve):
            n = [0]

            def step(ins):
                n[0] += 1
                ins.then_inc(reduced, 1)
                dve.wait_ge(reduced, n[0])

            dve.wait_ge(pos_in, 16)
            dve.wait_ge(params_in, 32)
            step(dve.tensor_copy(pos, pos_i.bitcast(I32)))
            step(dve.tensor_scalar(ang, pos, m.c(C_FREQ, 1), None, ALU.mult))
            magic = float(3 << 22)
            for j, shift in enumerate((0.25, 0.0)):
                step(dve.tensor_scalar(turns, ang, 1 / (2 * pi), shift, ALU.mult, ALU.add))
                step(dve.tensor_scalar(turns, turns, magic, None, ALU.add))
                step(dve.tensor_scalar(turns, turns, magic, None, ALU.subtract))
                step(dve.scalar_tensor_tensor(red[:, j], turns, -two_pi[0], ang, ALU.mult, ALU.add))
                step(dve.scalar_tensor_tensor(red[:, j], turns, -two_pi[1], red[:, j], ALU.mult, ALU.add))
                step(dve.scalar_tensor_tensor(red[:, j], turns, -two_pi[2], red[:, j], ALU.mult, ALU.add))
                if j == 0:
                    step(dve.tensor_scalar(red[:, j], red[:, j], pi / 2, None, ALU.add))
                step(dve.tensor_scalar(red[:, j], red[:, j], lim, -lim, ALU.min, ALU.max))
            dve.wait_ge(sines, 2)
            dve.tensor_scalar(tab[:, 1], tab[:, 1], m.c(C_SGN, 1), None, ALU.mult).then_inc(signed, 1)

        @block.scalar
        def _(act):
            act.wait_ge(reduced, 17)
            for j in range(2):
                act.activation(tab[:, j], red[:, j], ACT.Sin).then_inc(sines, 1)


def norm_phase(nc, m, src, dst, gain, kc, scratch, residual=None):
    sq, root = scratch
    tot = m.ps[:, 0:2, :].rearrange("p a b -> p (a b)")
    with phase(nc, "squared", "summed", "logged", "rooted", "scaled") as (
            block, squared, summed, logged, rooted, scaled):

        @block.scalar
        def _(act):
            for k in range(kc):
                if k >= 2:
                    act.wait_ge(summed, k - 1)
                act.activation(sq[:, k % 2], src[:, k], ACT.Square).then_inc(squared, 1)
            act.wait_ge(summed, kc)
            act.activation(root, tot, ACT.Ln, bias=m.c(C_EPS, 1), scale=1.0 / (kc * P)).then_inc(logged, 1)
            act.wait_ge(logged, 1)
            act.activation(root, root, ACT.Exp, scale=-0.5).then_inc(rooted, 1)

        @block.tensor
        def _(pe):
            for k in range(kc):
                pe.wait_ge(squared, k + 1)
                for h in range(2):
                    mm = pe.matmul(tot[:, h * HALF:(h + 1) * HALF], m.c(C_ONE), sq[:, k % 2, h * HALF:(h + 1) * HALF],
                                   start=(k == 0), stop=(k == kc - 1))
                mm.then_inc(summed, 1)

        @block.vector
        def _(dve):
            dve.wait_ge(rooted, 1)
            for k in range(kc):
                dve.scalar_tensor_tensor(dst[:, k], src[:, k], gain[:, k:k + 1], root, ALU.mult,
                                         ALU.mult).then_inc(scaled, 1)
            if residual is not None:
                for k in range(kc):
                    dve.wait_ge(scaled, k + 1)
                    dve.tensor_tensor(dst[:, k], dst[:, k], residual[:, k], ALU.add)


def gemm_phase(nc, m, w, src, kc, tiles, finish, bias=None, func=None, out=None, dst=None, tile0=0):
    slots = 2
    wt = m.take(slots, kc, P)
    tmp = m.take(slots, S)
    ps = m.ps[:, 0:2 * slots, :].rearrange("p (s h) f -> p s (h f)", s=slots)
    with phase(nc, "weights_a", "weights_b", "product_done", "evacuated", "relu_done", "stored_a", "stored_b") as (
            block, weights_a, weights_b, product_done, evacuated, relu_done, stored_a, stored_b):
        landed = (weights_a, weights_b)
        stored = (stored_a, stored_b)

        def rounds(eng, body, first=0):
            whole = tiles // 2
            for i in range(first):
                body(i, 0)
                body(i, 1)
            if whole > first:
                with eng.Fori(first, whole) as i:
                    body(i, 0)
                    body(i, 1)
            if tiles % 2:
                body(whole, 0)

        @block.sync
        def _(sp):
            def load(i, s):
                if not (isinstance(i, int) and i == 0):
                    sp.wait_ge(product_done, 2 * i + s - 1)
                sp.dma_start(wt[:, s].rearrange("p k f -> p (k f)"), w[2 * i + s]).then_inc(landed[s], 16)
            rounds(sp, load, first=1)

        @block.tensor
        def _(pe):
            def product(i, s):
                pe.wait_ge(landed[s], 16 * i + 16)
                if not (isinstance(i, int) and i == 0):
                    pe.wait_ge(evacuated, 2 * i + s - 1)
                for k in range(kc):
                    for h in range(2):
                        mm = pe.matmul(ps[:, s, h * HALF:(h + 1) * HALF], wt[:, s, k],
                                       src[:, k, h * HALF:(h + 1) * HALF], start=(k == 0), stop=(k == kc - 1))
                mm.then_inc(product_done, 1)
            rounds(pe, product, first=1)

        if finish == "store" or finish == "keep":
            @block.scalar
            def _(act):
                def evacuate(i, s):
                    j = 2 * i + s
                    act.wait_ge(product_done, j + 1)
                    if finish == "store":
                        act.wait_ge(stored[s], 16 * i)
                    to = tmp[:, s] if finish == "store" else dst[:, j]
                    if bias is None:
                        act.activation(to, ps[:, s], func or ACT.Copy).then_inc(evacuated, 1)
                    else:
                        act.activation(to, ps[:, s], func or ACT.Identity,
                                       bias=bias[:, bass.ds(j, 1)]).then_inc(evacuated, 1)
                    if finish == "store":
                        act.wait_ge(evacuated, j + 1)
                        act.dma_start(out[j + tile0], tmp[:, s]).then_inc(stored[s], 16)
                rounds(act, evacuate, first=1)
                if finish == "store":
                    act.wait_ge(stored[0], 16 * ((tiles + 1) // 2))
                    act.wait_ge(stored[1], 16 * (tiles // 2))

        if finish == "add":
            @block.vector
            def _(dve):
                def add(i, s):
                    dve.wait_ge(product_done, 2 * i + s + 1)
                    dve.tensor_tensor(dst[:, 2 * i + s], ps[:, s], dst[:, 2 * i + s], ALU.add).then_inc(evacuated, 1)
                rounds(dve, add, first=1)

        if finish == "relu2":
            @block.scalar
            def _(act):
                def relu(i, s):
                    act.wait_ge(product_done, 2 * i + s + 1)
                    if not (isinstance(i, int) and i == 0):
                        act.wait_ge(relu_done, 2 * i + s - 1)
                    act.activation(tmp[:, s], ps[:, s], ACT.Relu).then_inc(evacuated, 1)
                rounds(act, relu, first=1)

            @block.vector
            def _(dve):
                def square(i, s):
                    dve.wait_ge(evacuated, 2 * i + s + 1)
                    dve.tensor_tensor(dst[:, 2 * i + s], tmp[:, s], tmp[:, s], ALU.mult).then_inc(relu_done, 1)
                rounds(dve, square, first=1)


def rows_phase(nc, m, src, kc, w, width, tiles, out):
    wt = m.take(kc, width)
    res = m.take(tiles, width)
    with phase(nc, "weights_in", "rows_done", "rows_kept", "rows_out") as (
            block, weights_in, rows_done, rows_kept, rows_out):

        @block.sync
        def _(sp):
            sp.dma_start(wt, w).then_inc(weights_in, 16)
            sp.wait_ge(rows_kept, tiles)
            sp.dma_start(out.rearrange("i p f -> p i f"), res).then_inc(rows_out, 16)
            sp.wait_ge(rows_out, 16)

        @block.tensor
        def _(pe):
            pe.wait_ge(weights_in, 16)
            for i in range(tiles):
                if i >= 4:
                    pe.wait_ge(rows_kept, i - 3)
                for k in range(kc):
                    mm = pe.matmul(m.ps[:, i % 4, 0:width], src[:, k, i * P:(i + 1) * P], wt[:, k],
                                   start=(k == 0), stop=(k == kc - 1))
                mm.then_inc(rows_done, 1)

        @block.scalar
        def _(act):
            for i in range(tiles):
                act.wait_ge(rows_done, i + 1)
                act.activation(res[:, i], m.ps[:, i % 4, 0:width], ACT.Copy).then_inc(rows_kept, 1)


def stick_phase(nc, m, d):
    m.clear()
    q, k, v = m.take(S), m.take(S), m.take(NB, P)
    soft, sp_, lsg, aw = m.take(3, HALF), m.take(4, HALF), m.take(3, HALF), m.take(3, HALF)
    steps = []
    for g in range(2):
        for kb in range(4 * g + 3, -1, -1):
            for e in range(2):
                steps.append((e, g, kb, P * max(0, kb - 4 * g)))
    T = len(steps)
    pairs = SB_H // 2
    carried = np.cumsum([kb > 0 for _, _, kb, _ in steps]).tolist()
    ended = np.cumsum([kb == 0 for _, _, kb, _ in steps]).tolist()
    masked = np.cumsum([kb >= 4 * g for _, g, kb, _ in steps]).tolist()
    fixes = masked[-1]

    def diag(t):
        return steps[t][2] >= 4 * steps[t][1]

    with phase(nc, "staged", "q_scaled", "z_done", "abs_done", "exp_done", "ln_done", "raw_done", "sp_ready",
               "lsg_ready", "later_done", "arg_ready", "carry_done", "a_ready", "av_done", "o_kept") as (
            block, staged, q_scaled, z_done, abs_done, exp_done, ln_done, raw_done, sp_ready,
            lsg_ready, later_done, arg_ready, carry_done, a_ready, av_done, o_kept):

        @block.sync
        def _(sp):
            def body(i):
                sp.wait_ge(z_done, i * T)
                sp.wait_ge(av_done, i * T)
                sp.dma_start(q, d["in1"][i]).then_inc(staged, 16)
                sp.dma_start(k, d["in1"][i + pairs]).then_inc(staged, 16)
                sp.dma_start(v, d["v_sb"][:, :, bass.ds(i * P, P)].rearrange("b p f -> p b f")).then_inc(staged, 16)
            loop(sp, pairs, body)

        @block.tensor
        def _(pe):
            def body(i):
                b = i * T
                pe.wait_ge(staged, 48 * i + 48)
                pe.wait_ge(q_scaled, i + 1)
                for t in range(T + 4):
                    if t < T:
                        e, g, kb, c0 = steps[t]
                        pe.wait_ge(lsg_ready, b + max(t - 2, 0))
                        pe.matmul(m.ps[:, t % 3, c0:HALF], k[64 * e:64 * e + 64, kb * P:(kb + 1) * P],
                                  q[64 * e:64 * e + 64, g * HALF + c0:(g + 1) * HALF],
                                  start=True, stop=True).then_inc(z_done, 1)
                    if 0 <= t - 2 < T:
                        e, g, kb, c0 = steps[t - 2]
                        pe.wait_ge(sp_ready, b + t - 1)
                        pe.wait_ge(arg_ready, b + max(t - 3, 0))
                        pe.matmul(m.ps[:, 3 + e, c0:HALF], m.c(C_GT), sp_[:, (t - 2) % 4, c0:HALF],
                                  start=(kb == 4 * g + 3), stop=False, skip_group_check=True).then_inc(later_done, 1)
                    if 0 <= t - 3 < T and steps[t - 3][2] > 0:
                        e, g, kb, c0 = steps[t - 3]
                        pe.wait_ge(arg_ready, b + t - 2)
                        pe.matmul(m.ps[:, 3 + e, c0:HALF], m.c(C_LE), sp_[:, (t - 3) % 4, c0:HALF],
                                  start=False, stop=False, skip_group_check=True).then_inc(carry_done, 1)
                    if 0 <= t - 4 < T:
                        e, g, kb, c0 = steps[t - 4]
                        pe.wait_ge(a_ready, b + t - 3)
                        if kb == 4 * g + 3:
                            pe.wait_ge(o_kept, i * 4 + (2 * g - 2 + e + 1 if g else 0))
                        mm = pe.matmul(m.ps[64 * e:64 * e + 64, 5 + e, c0:HALF], v[:, kb, 64 * e:64 * e + 64],
                                       aw[:, (t - 4) % 3, c0:HALF], start=(kb == 4 * g + 3), stop=(kb == 0),
                                       skip_group_check=True)
                        mm.then_inc(av_done, 1)
            loop(pe, pairs, body)

        @block.scalar
        def _(act):
            def body(i):
                b = i * T
                act.wait_ge(staged, 48 * i + 48)
                act.activation(q, q, ACT.Copy, scale=float(SB_D ** -0.5)).then_inc(q_scaled, 1)
                for t in range(T + 2):
                    if t < T:
                        c0 = steps[t][3]
                        x = soft[:, t % 3, c0:HALF]
                        act.wait_ge(z_done, b + t + 1)
                        act.activation(x, m.ps[:, t % 3, c0:HALF], ACT.Abs).then_inc(abs_done, 1)
                        act.wait_ge(abs_done, b + t + 1)
                        act.activation(x, x, ACT.Exp, scale=-1.0).then_inc(exp_done, 1)
                        act.wait_ge(exp_done, b + t + 1)
                        act.activation(x, x, ACT.Ln, bias=1.0).then_inc(ln_done, 1)
                    if 0 <= t - 2 < T:
                        c0 = steps[t - 2][3]
                        act.wait_ge(arg_ready, b + t - 1)
                        act.wait_ge(av_done, b + max(t - 4, 0))
                        act.activation(aw[:, (t - 2) % 3, c0:HALF], lsg[:, (t - 2) % 3, c0:HALF],
                                       ACT.Exp).then_inc(a_ready, 1)
            loop(act, pairs, body)

        @block.vector
        def _(dve):
            def body(i):
                b = i * T
                for t in range(T + 6):
                    if 0 <= t - 1 < T:
                        u = t - 1
                        c0 = steps[u][3]
                        z = m.ps[:, u % 3, c0:HALF]
                        ln = soft[:, u % 3, c0:HALF]
                        dve.wait_ge(ln_done, b + u + 1)
                        dve.wait_ge(later_done, b + max(u - 3, 0))
                        dve.wait_ge(carry_done, i * carried[-1] + (carried[u - 4] if u >= 4 else 0))
                        dve.wait_ge(a_ready, b + max(u - 2, 0))
                        one = dve.scalar_tensor_tensor(sp_[:, u % 4, c0:HALF], z, 0.0, ln, ALU.max, ALU.add)
                        one.then_inc(raw_done if diag(u) else sp_ready, 1)
                        two = dve.scalar_tensor_tensor(lsg[:, u % 3, c0:HALF], z, 0.0, ln, ALU.min, ALU.subtract)
                        two.then_inc(raw_done if diag(u) else lsg_ready, 1)
                        if diag(u):
                            own = slice(c0, c0 + P)
                            dve.wait_ge(raw_done, i * 2 * fixes + 2 * masked[u])
                            dve.tensor_tensor(sp_[:, u % 4, own], sp_[:, u % 4, own], m.c(C_LT),
                                              ALU.mult).then_inc(sp_ready, 1)
                            dve.tensor_tensor(lsg[:, u % 3, own], lsg[:, u % 3, own], m.c(C_NGE),
                                              ALU.add).then_inc(lsg_ready, 1)
                    if 0 <= t - 2 < T:
                        u = t - 2
                        e, g, kb, c0 = steps[u]
                        dve.wait_ge(later_done, b + u + 1)
                        dve.wait_ge(lsg_ready, b + u + 1)
                        x = lsg[:, u % 3, c0:HALF]
                        dve.tensor_tensor(x, x, m.ps[:, 3 + e, c0:HALF], ALU.subtract).then_inc(arg_ready, 1)
                    if 0 <= t - 5 < T and steps[t - 5][2] == 0:
                        e, g, kb, c0 = steps[t - 5]
                        dve.wait_ge(av_done, b + t - 4)
                        rows = slice(64 * e, 64 * e + 64)
                        dve.tensor_copy(m.act[rows, i, g * HALF:(g + 1) * HALF], m.ps[rows, 5 + e, :]).then_inc(o_kept, 1)
            loop(dve, pairs, body)


def rope_phase(nc, m, plain, swapped, tab, tiles, out, rows):
    res = m.take(tiles, S)
    t1 = m.take(tiles, S)
    with phase(nc, "cos_done", "sin_done", "turned", "rope_out") as (block, cos_done, sin_done, turned, rope_out):

        @block.vector
        def _(dve):
            for j in range(tiles):
                dve.tensor_tensor(res[:, j], plain[:, j], tab[:, 0], ALU.mult).then_inc(cos_done, 1)
                dve.tensor_tensor(t1[:, j], swapped[:, j], tab[:, 1], ALU.mult).then_inc(sin_done, 1)
                dve.wait_ge(cos_done, j + 1)
                dve.wait_ge(sin_done, j + 1)
                dve.tensor_tensor(res[:, j], res[:, j], t1[:, j], ALU.add).then_inc(turned, 1)

        @block.sync
        def _(sp):
            for j in range(tiles):
                sp.wait_ge(turned, j + 1)
                sp.dma_start(out[j * P:j * P + rows], res[0:rows, j]).then_inc(rope_out, 16)
            sp.wait_ge(rope_out, 16 * tiles)


def latent_phases(nc, m, d):
    m.clear()
    low = m.take(5, S)
    normed = m.take(3, S)
    tab = m.take(2, S)
    scratch = (m.take(2, S), m.take(S))
    with phase(nc, "low_in") as (block, low_in):
        @block.sync
        def _(sp):
            sp.dma_start(low, d["in1"][8:13].rearrange("a p t -> p a t")).then_inc(low_in, 16)
            sp.dma_start(tab, d["rope"].rearrange("a p t -> p a t")).then_inc(low_in, 16)
            sp.wait_ge(low_in, 32)
    norm_phase(nc, m, low[:, 0:2], normed[:, 0:2], m.p("q_a_g", 0, 2), 2, scratch)
    norm_phase(nc, m, low[:, 2:3], normed[:, 2:3], m.p("kv_a_g", 0, 1), 1, scratch)
    base = m.top
    rope_phase(nc, m, low[:, 3:4], low[:, 4:5], tab, 1, d["k_rope"], ROPE)
    m.top = base
    gemm_phase(nc, m, d["w_qn"], normed[:, 0:2], 2, 4, "store", out=d["mla_q"])
    m.top = base
    qr = m.take(4, S)
    gemm_phase(nc, m, d["w_qr"], normed[:, 0:2], 2, 4, "keep", dst=qr)
    rope_phase(nc, m, qr[:, 0:2], qr[:, 2:4], tab, 2, d["q_rope"], P)
    m.top = base
    gemm_phase(nc, m, d["w_kn"], normed[:, 2:3], 1, 4, "store", out=d["mla_k"])
    m.top = base
    rows_phase(nc, m, normed[:, 2:3], 1, d["w_vm"], BW, NB, d["mla_v"])


def latent_attention_phase(nc, m, d):
    m.clear()
    qn, kn, v = m.take(S), m.take(S), m.take(NB, P)
    qr, kr = m.take(S), m.take(S)
    pr = m.take(2, S)
    pt = m.take(2, S)
    mx, nm, rs, ri = m.take(NB), m.take(NB), m.take(NB), m.take(NB)
    T = NB

    def scores(t):
        return m.ps[:, 2 * (t % 2):2 * (t % 2) + 2, :].rearrange("p a f -> p (a f)")
    turned = m.ps[:, 4:6, :].rearrange("p a f -> p (a f)")

    with phase(nc, "staged", "s_done", "diag_masked", "max_done", "negated", "p_ready", "inverted", "p_scaled",
               "t_done", "t_kept", "o_done", "o_kept") as (
            block, staged, s_done, diag_masked, max_done, negated, p_ready, inverted, p_scaled,
            t_done, t_kept, o_done, o_kept):

        @block.sync
        def _(sp):
            sp.dma_start(kr[0:ROPE], d["k_rope"]).then_inc(staged, 16)
            def body(i):
                sp.wait_ge(o_done, i * T)
                sp.dma_start(qn, d["mla_q"][i]).then_inc(staged, 16)
                sp.dma_start(kn, d["mla_k"][i]).then_inc(staged, 16)
                sp.dma_start(qr[0:ROPE], d["q_rope"][bass.ds(i * ROPE, ROPE)]).then_inc(staged, 16)
                sp.dma_start(v, d["mla_v"][:, :, bass.ds(i * P, P)].rearrange("b p f -> p b f")).then_inc(staged, 16)
            loop(sp, MLA_H, body)

        @block.tensor
        def _(pe):
            def body(i):
                b = i * T
                pe.wait_ge(staged, 64 * i + 80)
                for t in range(T + 2):
                    if t < T:
                        pe.wait_ge(p_ready, b + max(t - 1, 0))
                        n = (t + 1) * P
                        for c in range(0, n, HALF):
                            w = min(HALF, n - c)
                            pe.matmul(scores(t)[:, c:c + w], qn[:, t * P:(t + 1) * P], kn[:, c:c + w],
                                      start=True, stop=False)
                            mm = pe.matmul(scores(t)[:, c:c + w], qr[0:ROPE, t * P:(t + 1) * P], kr[0:ROPE, c:c + w],
                                           start=False, stop=True)
                        mm.then_inc(s_done, 1)
                    if 0 <= t - 1 < T:
                        u = t - 1
                        pe.wait_ge(p_scaled, b + u + 1)
                        pe.wait_ge(t_kept, b + u)
                        for kb in range(u + 1):
                            mm = pe.transpose(turned[:, kb * P:(kb + 1) * P], pr[:, u % 2, kb * P:(kb + 1) * P],
                                              m.c(C_ID))
                        mm.then_inc(t_done, 1)
                    if 0 <= t - 2 < T:
                        u = t - 2
                        pe.wait_ge(t_kept, b + u + 1)
                        pe.wait_ge(o_kept, b + max(u - 1, 0))
                        for kb in range(u + 1):
                            mm = pe.matmul(m.ps[:, 6 + u % 2, 0:P], v[:, kb], pt[:, u % 2, kb * P:(kb + 1) * P],
                                           start=(kb == 0), stop=(kb == u))
                        mm.then_inc(o_done, 1)
            loop(pe, MLA_H, body)

        @block.vector
        def _(dve):
            def body(i):
                b = i * T
                for t in range(T + 3):
                    if t < T:
                        dve.wait_ge(s_done, b + t + 1)
                        own = scores(t)[:, t * P:(t + 1) * P]
                        dve.tensor_tensor(own, own, m.c(C_NCAUSAL), ALU.add).then_inc(diag_masked, 1)
                        dve.wait_ge(diag_masked, b + t + 1)
                        dve.wait_ge(negated, b + t)
                        dve.tensor_reduce(mx[:, t:t + 1], scores(t)[:, 0:(t + 1) * P], AX.X, ALU.max).then_inc(max_done, 1)
                        dve.wait_ge(max_done, b + t + 1)
                        dve.wait_ge(p_ready, b + t)
                        dve.tensor_scalar(nm[:, t:t + 1], mx[:, t:t + 1], -MLA_SCALE, None, ALU.mult).then_inc(negated, 1)
                    if 0 <= t - 1 < T:
                        u = t - 1
                        dve.wait_ge(p_ready, b + u + 1)
                        dve.wait_ge(p_scaled, b + u)
                        dve.reciprocal(ri[:, u:u + 1], rs[:, u:u + 1]).then_inc(inverted, 1)
                        dve.wait_ge(inverted, b + u + 1)
                        x = pr[:, u % 2, 0:(u + 1) * P]
                        dve.tensor_scalar(x, x, ri[:, u:u + 1], None, ALU.mult).then_inc(p_scaled, 1)
                    if 0 <= t - 3 < T:
                        u = t - 3
                        dve.wait_ge(o_done, b + u + 1)
                        dve.tensor_copy(m.act[:, 4 + i, u * P:(u + 1) * P], m.ps[:, 6 + u % 2, 0:P]).then_inc(o_kept, 1)
            loop(dve, MLA_H, body)

        @block.scalar
        def _(act):
            def body(i):
                b = i * T
                for t in range(T + 1):
                    if t < T:
                        act.wait_ge(negated, b + t + 1)
                        act.wait_ge(t_done, b + max(t - 1, 0))
                        n = (t + 1) * P
                        act.wait_ge(inverted, b + max(t - 1, 0))
                        act.activation(pr[:, t % 2, 0:n], scores(t)[:, 0:n], ACT.Exp, bias=nm[:, t:t + 1],
                                       scale=MLA_SCALE, accum_out=rs[:, t:t + 1]).then_inc(p_ready, 1)
                    if 0 <= t - 1 < T:
                        u = t - 1
                        act.wait_ge(t_done, b + u + 1)
                        act.wait_ge(o_done, b + max(u - 1, 0))
                        act.activation(pt[:, u % 2, 0:(u + 1) * P], turned[:, 0:(u + 1) * P], ACT.Copy).then_inc(t_kept, 1)
            loop(act, MLA_H, body)


def small_phase(nc, m, d):
    m.clear()
    n = NB * 4
    ab = m.take(NB, 8)
    x, e, w, w2, acc, ea = (m.take(n + 4) for _ in range(6))
    ones8 = (1, NB, 4)
    with phase(nc, "ab_in", "biased", "sig_done", "abs_done", "exp_done", "alog_done", "chain") as (
            block, ab_in, biased, sig_done, abs_done, exp_done, alog_done, chain):

        @block.sync
        def _(sp):
            sp.dma_start(ab, d["ab"].rearrange("c p f -> p c f")).then_inc(ab_in, 16)
            sp.wait_ge(ab_in, 16)

        @block.scalar
        def _(act):
            act.wait_ge(biased, 1)
            act.activation(m.beta, ab[:, :, 0:4], ACT.Sigmoid).then_inc(sig_done, 1)
            act.activation(ea[:, 0:4], m.p("a_log", 0, 4), ACT.Exp).then_inc(alog_done, 1)
            act.wait_ge(biased, 3)
            act.activation(e, x, ACT.Abs).then_inc(abs_done, 1)
            act.wait_ge(abs_done, 1)
            act.activation(e, e, ACT.Exp, scale=-1.0).then_inc(exp_done, 1)

        @block.vector
        def _(dve):
            count = [0]

            def step(ins):
                count[0] += 1
                ins.then_inc(chain, 1)
                dve.wait_ge(chain, count[0])

            dve.wait_ge(ab_in, 16)
            dve.tensor_tensor(ab, ab, m.p("ab_bias", 0, 8).unsqueeze(1).to_broadcast([P, NB, 8]),
                              ALU.add).then_inc(biased, 1)
            dve.wait_ge(biased, 1)
            dve.tensor_tensor(x[:, 0:n].rearrange("p (c h) -> p c h", h=4), ab[:, :, 4:8],
                              m.p("a_dt", 0, 4).unsqueeze(1).to_broadcast([P, NB, 4]), ALU.add).then_inc(biased, 1)
            dve.tensor_scalar(x[:, n:n + 4], m.p("d_lam", 0, 4), -1.0, None, ALU.mult).then_inc(biased, 1)
            dve.wait_ge(exp_done, 1)
            step(dve.tensor_scalar(w, e, 2.0, None, ALU.add))
            step(dve.reciprocal(w, w))
            step(dve.tensor_tensor(w, w, e, ALU.mult))
            step(dve.tensor_tensor(w2, w, w, ALU.mult))
            step(dve.tensor_scalar(acc, w2, 1 / 17, 1 / 15, ALU.mult, ALU.add))
            for k in range(13, 0, -2):
                step(dve.tensor_tensor(acc, acc, w2, ALU.mult))
                step(dve.tensor_scalar(acc, acc, 1 / k, None, ALU.add))
            step(dve.scalar_tensor_tensor(acc, acc, 2.0, w, ALU.mult, ALU.mult))
            step(dve.scalar_tensor_tensor(acc, x, 0.0, acc, ALU.max, ALU.add))
            step(dve.tensor_scalar(m.rate, acc[:, n:n + 4], 8.0, None, ALU.mult))
            dve.wait_ge(alog_done, 1)
            step(dve.scalar_tensor_tensor(m.decay, acc[:, 0:n].rearrange("p (c h) -> p c h", h=4), -1.0,
                                          ea[:, 0:4].unsqueeze(1).to_broadcast([P, NB, 4]), ALU.mult, ALU.mult))


def conv(dve, x, acc, taps, n_taps, bias, chain, count):
    for k in range(n_taps):
        if k == 0 and bias is None:
            ins = dve.tensor_scalar(acc, x[:, 0:S], taps[:, 0:1], None, ALU.mult)
        elif k == 0:
            ins = dve.tensor_scalar(acc, x[:, 0:S], taps[:, 0:1], bias, ALU.mult, ALU.add)
        else:
            dve.wait_ge(chain, count + k)
            ins = dve.scalar_tensor_tensor(acc, x[:, k:k + S], taps[:, k:k + 1], acc, ALU.mult, ALU.add)
        ins.then_inc(chain, 1)


def delta_conv_phase(nc, m, d):
    m.clear()
    pad = CONVK - 1
    tiles = 3 * BT
    x = m.take(2, S + 4)
    y = m.take(tiles, S)
    sq, root = m.take(2, S), m.take(2, S)
    ps = m.ps[:, 0:4, :].rearrange("p (s h) f -> p s (h f)", s=2)
    with phase(nc, "zeroed", "x_a", "x_b", "conv_chain", "silu_done", "squared", "summed", "logged", "rooted",
               "normed", "all_out") as (
            block, zeroed, x_a, x_b, conv_chain, silu_done, squared, summed, logged, rooted, normed, all_out):
        x_in = (x_a, x_b)

        @block.sync
        def _(sp):
            sp.wait_ge(zeroed, 2)
            for j in range(tiles):
                if j >= 2:
                    sp.wait_ge(conv_chain, (j - 1) * CONVK)
                sp.dma_start(x[:, j % 2, pad:pad + S], d["in2"][T_AQKV + j]).then_inc(x_in[j % 2], 16)
            sp.wait_ge(silu_done, tiles)
            sp.dma_start(d["delta"][2 * BT:tiles].rearrange("c p t -> p c t"), y[:, 2 * BT:tiles]).then_inc(all_out, 16)
            sp.wait_ge(normed, 2 * BT)
            sp.dma_start(d["delta"][0:2 * BT].rearrange("c p t -> p c t"), y[:, 0:2 * BT]).then_inc(all_out, 16)
            sp.wait_ge(all_out, 32)

        @block.vector
        def _(dve):
            for s in range(2):
                dve.memset(x[:, s, 0:pad], 0.0).then_inc(zeroed, 1)

            def norm(j):
                dve.wait_ge(rooted, j + 1)
                dve.scalar_tensor_tensor(y[:, j], y[:, j], m.c(C_QS + j, 1), root[:, j % 2], ALU.mult,
                                         ALU.mult).then_inc(normed, 1)
            for j in range(tiles):
                dve.wait_ge(x_in[j % 2], 16 * (j // 2) + 16)
                conv(dve, x[:, j % 2], y[:, j], m.p("a_conv", j * CONVK, CONVK), CONVK, None, conv_chain, j * CONVK)
                if 3 <= j < 3 + 2 * BT:
                    norm(j - 3)

        @block.scalar
        def _(act):
            def root_of(j):
                act.wait_ge(summed, j + 1)
                if j >= 2:
                    act.wait_ge(normed, j - 1)
                act.activation(root[:, j % 2], ps[:, j % 2], ACT.Ln, bias=m.c(C_EPS, 1)).then_inc(logged, 1)
                act.wait_ge(logged, j + 1)
                act.activation(root[:, j % 2], root[:, j % 2], ACT.Exp, scale=-0.5).then_inc(rooted, 1)
            for j in range(tiles):
                act.wait_ge(conv_chain, (j + 1) * CONVK)
                act.activation(y[:, j], y[:, j], ACT.Silu).then_inc(silu_done, 1)
                if j < 2 * BT:
                    act.wait_ge(silu_done, j + 1)
                    if j >= 2:
                        act.wait_ge(summed, j - 1)
                    act.activation(sq[:, j % 2], y[:, j], ACT.Square).then_inc(squared, 1)
                if 1 <= j < 1 + 2 * BT:
                    root_of(j - 1)

        @block.tensor
        def _(pe):
            for j in range(2 * BT):
                pe.wait_ge(squared, j + 1)
                if j >= 2:
                    pe.wait_ge(logged, j - 1)
                for h in range(2):
                    mm = pe.matmul(ps[:, j % 2, h * HALF:(h + 1) * HALF], m.c(C_ONE),
                                   sq[:, j % 2, h * HALF:(h + 1) * HALF], start=True, stop=True)
                mm.then_inc(summed, 1)


def heads(v):
    return v.rearrange("p (h f) -> p h f", h=4)


def wide(column):
    return column.unsqueeze(2).to_broadcast([P, 4, P])


def over_heads(square):
    return square.unsqueeze(1).to_broadcast([P, 4, P])


def delta_prepare_phase(nc, m, d, at, attn, qd, last):
    base = m.top
    st = m.take(3 * BT, P)
    gw, bw, gd, lt, eg = (m.take(BW) for _ in range(5))
    rows = m.take(3, BW)
    gc, egc, kx, bg = (m.take(4) for _ in range(4))
    bank = [m.ps[:, n, :] for n in range(8)]
    with phase(nc, "staged", "spread_g", "spread_b", "sums_done", "rows_done", "products_done", "picked", "g_col",
               "diff_done", "clamped", "l_exp", "l_masked", "eg_done", "egc_done", "kx_diff", "kx_done", "bg_done",
               "a_half", "a_done", "attn_done", "qd_done", "last_done", "k1", "k2", "v1", "rows_out") as (
            block, staged, spread_g, spread_b, sums_done, rows_done, products_done, picked, g_col,
            diff_done, clamped, l_exp, l_masked, eg_done, egc_done, kx_diff, kx_done, bg_done,
            a_half, a_done, attn_done, qd_done, last_done, k1, k2, v1, rows_out):

        @block.sync
        def _(sp):
            def body(c):
                sp.wait_ge(products_done, c)
                sp.wait_ge(rows_done, c)
                sp.wait_ge(qd_done, c)
                sp.dma_start(st, d["delta"][:, :, bass.ds(c * P, P)].rearrange("a p t -> p a t")).then_inc(staged, 16)
                sp.wait_ge(k1, c + 1)
                sp.wait_ge(k2, c + 1)
                sp.wait_ge(v1, c + 1)
                sp.dma_start(d["kv_rows"][c], rows.rearrange("p a f -> p (a f)")).then_inc(rows_out, 16)
            loop(sp, NB, body)
            sp.wait_ge(rows_out, 16 * NB)

        @block.tensor
        def _(pe):
            def body(c):
                pe.wait_ge(spread_g, c + 1)
                pe.wait_ge(eg_done, c)
                pe.wait_ge(diff_done, c)
                pe.wait_ge(last_done, c)
                pe.wait_ge(kx_diff, c)
                for h in range(4):
                    pe.matmul(bank[2][:, h * P:(h + 1) * P], heads(gw)[:, h], m.c(C_LE), start=True, stop=True)
                pe.wait_ge(spread_b, c + 1)
                pe.wait_ge(a_done, c)
                for h in range(4):
                    mm = pe.matmul(bank[3][:, h * P:(h + 1) * P], heads(bw)[:, h], m.c(C_ID), start=True, stop=True)
                mm.then_inc(sums_done, 1)
                pe.wait_ge(staged, 16 * c + 16)
                pe.wait_ge(k1, c)
                pe.wait_ge(k2, c)
                pe.wait_ge(v1, c)
                for h in range(4):
                    pe.transpose(bank[0][:, h * P:(h + 1) * P], st[:, BT + h], m.c(C_ID))
                for h in range(4):
                    mm = pe.transpose(bank[1][:, h * P:(h + 1) * P], st[:, 2 * BT + h], m.c(C_ID))
                mm.then_inc(rows_done, 1)
                pe.wait_ge(attn_done, c)
                for h in range(4):
                    pe.matmul(bank[4][:, h * P:(h + 1) * P], st[:, BT + h], st[:, BT + h], start=True, stop=True)
                for h in range(4):
                    mm = pe.matmul(bank[5][:, h * P:(h + 1) * P], st[:, BT + h], st[:, h], start=True, stop=True)
                mm.then_inc(products_done, 1)
            loop(pe, NB, body)

        @block.vector
        def _(dve):
            def body(c):
                dve.wait_ge(sums_done, c)
                dve.tensor_tensor(heads(gw), over_heads(m.c(C_ONE)), wide(m.decay[:, c]), ALU.mult).then_inc(spread_g, 1)
                dve.tensor_tensor(heads(bw), over_heads(m.c(C_ONE)), wide(m.beta[:, c]), ALU.mult).then_inc(spread_b, 1)
                dve.wait_ge(sums_done, c + 1)
                dve.tensor_tensor(heads(gd), heads(bank[2]), over_heads(m.c(C_ID)), ALU.mult).then_inc(picked, 1)
                dve.wait_ge(picked, c + 1)
                dve.wait_ge(egc_done, c)
                dve.tensor_reduce(gc, heads(gd), AX.X, ALU.add).then_inc(g_col, 1)
                dve.wait_ge(g_col, c + 1)
                dve.tensor_tensor(heads(lt), heads(bank[2]), wide(gc), ALU.subtract).then_inc(diff_done, 1)
                g_last = heads(bank[2])[:, :, P - 1]
                dve.wait_ge(kx_done, c)
                dve.tensor_tensor(kx, g_last, gc, ALU.subtract).then_inc(kx_diff, 1)
                dve.wait_ge(diff_done, c + 1)
                dve.tensor_scalar(lt, lt, 0.0, None, ALU.min).then_inc(clamped, 1)
                dve.wait_ge(eg_done, c + 1)
                dve.tensor_copy(last[:, c], heads(eg)[:, :, P - 1]).then_inc(last_done, 1)
                dve.wait_ge(egc_done, c + 1)
                dve.wait_ge(k1, c)
                dve.tensor_tensor(bg, egc, m.beta[:, c], ALU.mult).then_inc(bg_done, 1)
                dve.wait_ge(l_exp, c + 1)
                dve.tensor_tensor(heads(lt), heads(lt), over_heads(m.c(C_LE)), ALU.mult).then_inc(l_masked, 1)
                dve.wait_ge(l_masked, c + 1)
                dve.wait_ge(products_done, c + 1)
                dve.tensor_tensor(at[:, c], bank[4], lt, ALU.mult).then_inc(a_half, 1)
                dve.tensor_tensor(attn[:, c], bank[5], lt, ALU.mult).then_inc(attn_done, 1)
                dve.wait_ge(a_half, c + 1)
                dve.tensor_tensor(at[:, c], at[:, c], bank[3], ALU.mult).then_inc(a_done, 1)
                dve.tensor_tensor(heads(qd[:, c]), st[:, 0:BT], heads(eg), ALU.mult).then_inc(qd_done, 1)
                dve.wait_ge(rows_out, 16 * c)
                dve.wait_ge(bg_done, c + 1)
                dve.wait_ge(rows_done, c + 1)
                dve.tensor_tensor(heads(rows[:, 0]), heads(bank[0]), wide(bg), ALU.mult).then_inc(k1, 1)
                dve.wait_ge(kx_done, c + 1)
                dve.tensor_tensor(heads(rows[:, 1]), heads(bank[0]), wide(kx), ALU.mult).then_inc(k2, 1)
                dve.tensor_tensor(heads(rows[:, 2]), heads(bank[1]), wide(m.beta[:, c]), ALU.mult).then_inc(v1, 1)
            loop(dve, NB, body)

        @block.scalar
        def _(act):
            def body(c):
                act.wait_ge(g_col, c + 1)
                act.wait_ge(bg_done, c)
                act.activation(egc, gc, ACT.Exp).then_inc(egc_done, 1)
                act.wait_ge(kx_diff, c + 1)
                act.activation(kx, kx, ACT.Exp).then_inc(kx_done, 1)
                act.wait_ge(diff_done, c + 1)
                act.wait_ge(qd_done, c)
                act.wait_ge(last_done, c)
                act.activation(eg, bank[2], ACT.Exp).then_inc(eg_done, 1)
                act.wait_ge(clamped, c + 1)
                act.activation(lt, lt, ACT.Exp).then_inc(l_exp, 1)
            loop(act, NB, body)
    m.top = base


def delta_inverse_phase(nc, m, at, inv, inv_t):
    base = m.top
    masked = m.take(4, 2 * BW)
    mid = m.take(4, 2 * BW)
    groups = 4

    def pair(v, g):
        return v[:, 2 * g:2 * g + 2].rearrange("p c f -> p (c f)")

    def eight(v):
        return v.rearrange("p (n f) -> p n f", f=P)

    def spread(square):
        return square.unsqueeze(1).to_broadcast([P, 8, P])

    def banks(b):
        return m.ps[:, b:b + 2, :].rearrange("p b f -> p (b f)")

    with phase(nc, "a_masked", "mid_done", "mid_kept", "low_done", "up_done", "low_kept", "up_kept") as (
            block, a_masked, mid_done, mid_kept, low_done, up_done, low_kept, up_kept):

        @block.vector
        def _(dve):
            for g in range(groups):
                dve.tensor_tensor(eight(masked[:, g]), eight(pair(at, g)), spread(m.c(C_LVL)), ALU.mult).then_inc(a_masked, 1)
            for g in range(groups):
                dve.wait_ge(mid_done, g + 1)
                dve.tensor_tensor(eight(pair(inv, g)), spread(m.c(C_ID)), eight(banks(2 * (g % 2))), ALU.subtract).then_inc(low_kept, 1)
                dve.tensor_tensor(eight(pair(inv_t, g)), spread(m.c(C_ID)), eight(masked[:, g]), ALU.subtract).then_inc(up_kept, 1)
            with dve.Fori(1, 7) as lvl:
                b = lvl * groups
                mask = m.const[:, C_LVL:C_LVL + 7 * P].rearrange("p (l f) -> p l f", f=P)[:, lvl]
                for g in range(groups):
                    dve.wait_ge(mid_done, b - groups + g + 1)
                    dve.wait_ge(up_kept, b - groups + g + 1)
                    dve.tensor_tensor(eight(masked[:, g]), eight(pair(at, g)), spread(mask), ALU.mult).then_inc(a_masked, 1)
                for g in range(groups):
                    dve.wait_ge(low_kept, b - groups + g + 1)
                    dve.wait_ge(low_done, b - groups + g + 1)
                    dve.tensor_tensor(pair(inv, g), pair(inv, g), banks(4), ALU.subtract).then_inc(low_kept, 1)
                    dve.wait_ge(up_done, b - groups + g + 1)
                    dve.tensor_tensor(pair(inv_t, g), pair(inv_t, g), banks(6), ALU.subtract).then_inc(up_kept, 1)

        @block.tensor
        def _(pe):
            def first(g, b):
                for n in range(8):
                    right = m.c(C_ID) if b is None else pair(inv, g)[:, n * P:(n + 1) * P]
                    mm = pe.matmul(banks(2 * (g % 2))[:, n * P:(n + 1) * P], masked[:, g, n * P:(n + 1) * P], right,
                                   start=True, stop=True)
                mm.then_inc(mid_done, 1)

            for g in range(groups):
                pe.wait_ge(a_masked, g + 1)
                if g >= 2:
                    pe.wait_ge(low_kept, g - 1)
                first(g, None)
            pe.wait_ge(low_kept, groups)
            with pe.Fori(1, 7) as lvl:
                b = lvl * groups
                for g in range(groups + 1):
                    if g < groups:
                        pe.wait_ge(a_masked, b + g + 1)
                        pe.wait_ge(low_kept, b - groups + g + 1)
                        if g >= 2:
                            pe.wait_ge(mid_kept, b - groups + g - 1)
                        first(g, b)
                    if g >= 1:
                        u = g - 1
                        pe.wait_ge(mid_kept, b - groups + u + 1)
                        pe.wait_ge(up_kept, b - groups + u + 1)
                        pe.wait_ge(low_kept, b + u)
                        for n in range(8):
                            cut = slice(n * P, (n + 1) * P)
                            mm = pe.matmul(banks(4)[:, cut], pair(inv_t, u)[:, cut], mid[:, u, cut], start=True, stop=True)
                        mm.then_inc(low_done, 1)
                        pe.wait_ge(up_kept, b + u)
                        for n in range(8):
                            cut = slice(n * P, (n + 1) * P)
                            mm = pe.matmul(banks(6)[:, cut], mid[:, u, cut], pair(inv_t, u)[:, cut], start=True, stop=True)
                        mm.then_inc(up_done, 1)

        @block.scalar
        def _(act):
            with act.Fori(1, 7) as lvl:
                b = lvl * groups
                for g in range(groups):
                    act.wait_ge(mid_done, b + g + 1)
                    act.activation(mid[:, g], banks(2 * (g % 2)), ACT.Copy).then_inc(mid_kept, 1)
    m.top = base


def delta_scan_phase(nc, m, d, attn, qd, inv_t, last, o):
    base = m.top
    rows = m.take(3, BW)
    tt, nw, vn, state = (m.take(BW) for _ in range(4))
    bank = [m.ps[:, n, :] for n in range(8)]

    def h_(v, h):
        return v[:, h * P:(h + 1) * P]

    with phase(nc, "rows_in", "inv_copied", "w_done", "w_kept", "v_done", "v_kept", "o_done", "kv_done", "o_kept",
               "cleared", "state_ready") as (
            block, rows_in, inv_copied, w_done, w_kept, v_done, v_kept, o_done, kv_done, o_kept, cleared, state_ready):

        @block.sync
        def _(sp):
            def body(c):
                sp.wait_ge(kv_done, c)
                sp.dma_start(rows.rearrange("p a f -> p (a f)"), d["kv_rows"][c]).then_inc(rows_in, 16)
            loop(sp, NB, body)

        @block.scalar
        def _(act):
            def body(c):
                act.wait_ge(v_done, c)
                act.activation(tt, inv_t[:, c], ACT.Copy).then_inc(inv_copied, 1)
                act.wait_ge(w_done, c + 1)
                act.activation(nw, bank[0], ACT.Copy, scale=-1.0).then_inc(w_kept, 1)
                act.wait_ge(v_done, c + 1)
                act.wait_ge(kv_done, c)
                act.activation(vn, bank[1], ACT.Copy).then_inc(v_kept, 1)
            loop(act, NB, body)

        @block.tensor
        def _(pe):
            def body(c):
                pe.wait_ge(rows_in, 16 * c + 16)
                pe.wait_ge(inv_copied, c + 1)
                pe.wait_ge(w_kept, c)
                for h in range(4):
                    mm = pe.matmul(h_(bank[0], h), h_(rows[:, 0], h), h_(tt, h), start=True, stop=True)
                mm.then_inc(w_done, 1)
                pe.wait_ge(w_kept, c + 1)
                pe.wait_ge(v_kept, c)
                pe.wait_ge(state_ready, 4 * c + 4)
                for h in range(4):
                    pe.matmul(h_(bank[1], h), h_(tt, h), h_(rows[:, 2], h), start=True, stop=False)
                    mm = pe.matmul(h_(bank[1], h), h_(nw, h), h_(state, h), start=False, stop=True)
                mm.then_inc(v_done, 1)
                pe.wait_ge(v_kept, c + 1)
                for h in range(4):
                    mm = pe.matmul(h_(bank[3], h), h_(rows[:, 1], h), h_(vn, h), start=True, stop=True)
                pe.wait_ge(o_kept, c)
                for h in range(4):
                    pe.matmul(h_(bank[2], h), h_(state, h), qd[:, c, h * P:(h + 1) * P], start=True, stop=False)
                    mm = pe.matmul(h_(bank[2], h), h_(vn, h), attn[:, c, h * P:(h + 1) * P], start=False, stop=True)
                mm.then_inc(kv_done, 1)
            loop(pe, NB, body)

        @block.vector
        def _(dve):
            dve.memset(state, 0.0).then_inc(state_ready, 4)
            def body(c):
                dve.wait_ge(kv_done, c + 1)
                dve.wait_ge(state_ready, 4 * c + 4)
                for h in range(4):
                    dve.scalar_tensor_tensor(h_(state, h), h_(state, h), last[:, c, h:h + 1], h_(bank[3], h),
                                             ALU.mult, ALU.add).then_inc(state_ready, 1)
                dve.tensor_copy(o[:, :, bass.ds(c * P, P)], heads(bank[2])).then_inc(o_kept, 1)
            loop(dve, NB, body)
    m.top = base


def gated_store_phase(nc, m, d, src, scale, root, gate_tile, y_tile):
    z = m.take(BT, S)
    with phase(nc, "z_in", "scaled", "gated", "y_out") as (block, z_in, scaled, gated, y_out):

        @block.sync
        def _(sp):
            sp.dma_start(z, d["in2"][gate_tile:gate_tile + BT].rearrange("c p t -> p c t")).then_inc(z_in, 16)
            for j in range(BT):
                sp.wait_ge(gated, j + 1)
                sp.dma_start(d["y"][y_tile + j], z[:, j]).then_inc(y_out, 16)
            sp.wait_ge(y_out, 16 * BT)

        @block.vector
        def _(dve):
            dve.wait_ge(z_in, 16)
            for j in range(BT):
                if root is None:
                    dve.tensor_tensor(z[:, j], z[:, j], src[:, j], ALU.mult).then_inc(gated, 1)
                else:
                    dve.scalar_tensor_tensor(src[:, j], src[:, j], scale(j), root[:, j], ALU.mult,
                                             ALU.mult).then_inc(scaled, 1)
                    dve.wait_ge(scaled, j + 1)
                    dve.tensor_tensor(z[:, j], z[:, j], src[:, j], ALU.mult).then_inc(gated, 1)


def tile_roots_phase(nc, m, src, root, count):
    sq = m.take(2, S)
    ps = m.ps.rearrange("p (s h) f -> p s (h f)", s=4)
    with phase(nc, "squared", "summed", "logged", "rooted") as (block, squared, summed, logged, rooted):

        @block.scalar
        def _(act):
            for j in range(count):
                if j >= 2:
                    act.wait_ge(summed, j - 1)
                act.activation(sq[:, j % 2], src[:, j], ACT.Square).then_inc(squared, 1)
            for j in range(count):
                act.wait_ge(summed, j + 1)
                act.activation(root[:, j], ps[:, j], ACT.Ln, bias=m.c(C_EPS, 1), scale=1.0 / P).then_inc(logged, 1)
            for j in range(count):
                act.wait_ge(logged, j + 1)
                act.activation(root[:, j], root[:, j], ACT.Exp, scale=-0.5).then_inc(rooted, 1)

        @block.tensor
        def _(pe):
            for j in range(count):
                pe.wait_ge(squared, j + 1)
                for h in range(2):
                    mm = pe.matmul(ps[:, j, h * HALF:(h + 1) * HALF], m.c(C_ONE),
                                   sq[:, j % 2, h * HALF:(h + 1) * HALF], start=True, stop=True)
                mm.then_inc(summed, 1)


def delta_phases(nc, m, d):
    delta_conv_phase(nc, m, d)
    m.clear()
    at, attn, qd = (m.take(NB, BW) for _ in range(3))
    inv, inv_t = m.take(NB, BW), m.take(NB, BW)
    last = m.take(NB, 4)
    delta_prepare_phase(nc, m, d, at, attn, qd, last)
    delta_inverse_phase(nc, m, at, inv, inv_t)
    o = inv.rearrange("p c f -> p (c f)").rearrange("p (h t) -> p h t", h=4)
    delta_scan_phase(nc, m, d, attn, qd, inv_t, last, o)
    root = at.rearrange("p c f -> p (c f)").rearrange("p (h t) -> p h t", h=4)
    base = m.top
    tile_roots_phase(nc, m, o, root, BT)
    m.top = base
    gated_store_phase(nc, m, d, o, lambda j: m.p("a_norm", 0, 1), root, T_AZ, 0)


def conformer_phase(nc, m, d):
    m.clear()
    pad = CONFK - 1
    left, right = m.take(2, S), m.take(2, S)
    x = m.take(2, S + pad + 2)
    y = m.take(BT, S)
    sq, root = m.take(2, S), m.take(S)
    z = m.take(BT, S)
    mean = m.ps[:, 0:2, :].rearrange("p a f -> p (a f)")
    var = m.ps[:, 2:4, :].rearrange("p a f -> p (a f)")
    with phase(nc, "zeroed", "in_a", "in_b", "z_in", "sig_done", "glu_done", "conv_chain", "mean_done", "centred",
               "squared", "var_done", "logged", "rooted", "scaled", "silu_done", "gated", "y_out") as (
            block, zeroed, in_a, in_b, z_in, sig_done, glu_done, conv_chain, mean_done, centred,
            squared, var_done, logged, rooted, scaled, silu_done, gated, y_out):
        x_in = (in_a, in_b)

        @block.sync
        def _(sp):
            for j in range(BT):
                if j >= 2:
                    sp.wait_ge(glu_done, j - 1)
                sp.dma_start(left[:, j % 2], d["in2"][T_GLU + j]).then_inc(x_in[j % 2], 16)
                sp.dma_start(right[:, j % 2], d["in2"][T_GLU + BT + j]).then_inc(x_in[j % 2], 16)
            sp.dma_start(z, d["in2"][T_BZ:T_BZ + BT].rearrange("c p t -> p c t")).then_inc(z_in, 16)
            for j in range(BT):
                sp.wait_ge(gated, j + 1)
                sp.dma_start(d["y"][BT + j], z[:, j]).then_inc(y_out, 16)
            sp.wait_ge(y_out, 16 * BT)

        @block.scalar
        def _(act):
            for j in range(BT):
                act.wait_ge(x_in[j % 2], 32 * (j // 2) + 32)
                act.activation(right[:, j % 2], right[:, j % 2], ACT.Sigmoid).then_inc(sig_done, 1)
            for j in range(BT):
                act.wait_ge(centred, j + 1)
                if j >= 2:
                    act.wait_ge(var_done, j - 1)
                act.activation(sq[:, j % 2], y[:, j], ACT.Square).then_inc(squared, 1)
            act.wait_ge(var_done, BT)
            act.activation(root, var, ACT.Ln, bias=m.c(C_EPS, 1), scale=1.0 / BW).then_inc(logged, 1)
            act.wait_ge(logged, 1)
            act.activation(root, root, ACT.Exp, scale=-0.5).then_inc(rooted, 1)
            for j in range(BT):
                act.wait_ge(scaled, j + 1)
                act.activation(y[:, j], y[:, j], ACT.Silu, bias=m.p("b_ln_b", j)).then_inc(silu_done, 1)

        @block.vector
        def _(dve):
            for s in range(2):
                dve.memset(x[:, s, 0:pad], 0.0).then_inc(zeroed, 1)
            dve.wait_ge(zeroed, 2)
            for j in range(BT):
                dve.wait_ge(sig_done, j + 1)
                dve.tensor_tensor(x[:, j % 2, pad:pad + S], left[:, j % 2], right[:, j % 2], ALU.mult).then_inc(glu_done, 1)
                dve.wait_ge(glu_done, j + 1)
                conv(dve, x[:, j % 2], y[:, j], m.p("b_conv", j * CONFK, CONFK), CONFK, m.p("b_conv_b", j), conv_chain,
                     j * CONFK)
            dve.wait_ge(mean_done, 1)
            for j in range(BT):
                dve.scalar_tensor_tensor(y[:, j], mean, -1.0 / BW, y[:, j], ALU.mult, ALU.add).then_inc(centred, 1)
            dve.wait_ge(rooted, 1)
            for j in range(BT):
                dve.scalar_tensor_tensor(y[:, j], y[:, j], m.p("b_ln_g", j), root, ALU.mult, ALU.mult).then_inc(scaled, 1)
            dve.wait_ge(z_in, 16)
            for j in range(BT):
                dve.wait_ge(silu_done, j + 1)
                dve.tensor_tensor(z[:, j], z[:, j], y[:, j], ALU.mult).then_inc(gated, 1)

        @block.tensor
        def _(pe):
            for j in range(BT):
                pe.wait_ge(conv_chain, (j + 1) * CONFK)
                for h in range(2):
                    mm = pe.matmul(mean[:, h * HALF:(h + 1) * HALF], m.c(C_ONE), y[:, j, h * HALF:(h + 1) * HALF],
                                   start=(j == 0), stop=(j == BT - 1))
            mm.then_inc(mean_done, 1)
            for j in range(BT):
                pe.wait_ge(squared, j + 1)
                for h in range(2):
                    mm = pe.matmul(var[:, h * HALF:(h + 1) * HALF], m.c(C_ONE), sq[:, j % 2, h * HALF:(h + 1) * HALF],
                                   start=(j == 0), stop=(j == BT - 1))
                mm.then_inc(var_done, 1)


def recurrence_phase(nc, m, d):
    m.clear()
    pad = CONVK - 1
    wa, wx = m.take(BT, P), m.take(BT, P)
    x = m.take(2, S + 4)
    xc, r, ig, th, a = (m.take(BT, S) for _ in range(5))
    root = m.take(BT, S)
    neg = m.take(4)
    ps = m.ps.rearrange("p (s h) f -> p s (h f)", s=4)
    with phase(nc, "w_in", "zeroed", "in_a", "in_b", "z_in", "negated", "conv_chain", "r_product", "x_product",
               "r_done", "i_done", "a_done", "t_done", "ln_done", "inv_root", "t_root", "half_b", "gated_b", "b_done",
               "scanned", "gated", "y_out") as (
            block, w_in, zeroed, in_a, in_b, z_in, negated, conv_chain, r_product, x_product,
            r_done, i_done, a_done, t_done, ln_done, inv_root, t_root, half_b, gated_b, b_done, scanned, gated, y_out):
        x_in = (in_a, in_b)

        @block.sync
        def _(sp):
            sp.dma_start(wa, d["w_da"]).then_inc(w_in, 16)
            sp.dma_start(wx, d["w_dx"]).then_inc(w_in, 16)
            sp.wait_ge(zeroed, 2)
            for j in range(BT):
                if j >= 2:
                    sp.wait_ge(conv_chain, (j - 1) * CONVK)
                sp.dma_start(x[:, j % 2, pad:pad + S], d["in2"][T_DX + j]).then_inc(x_in[j % 2], 16)
            sp.wait_ge(b_done, BT)
            sp.dma_start(r, d["in2"][T_DZ:T_DZ + BT].rearrange("c p t -> p c t")).then_inc(z_in, 16)
            for j in range(BT):
                sp.wait_ge(gated, j + 1)
                sp.dma_start(d["y"][3 * BT + j], r[:, j]).then_inc(y_out, 16)
            sp.wait_ge(y_out, 16 * BT)

        @block.tensor
        def _(pe):
            pe.wait_ge(w_in, 32)
            for j in range(BT):
                pe.wait_ge(conv_chain, (j + 1) * CONVK)
                if j >= 2:
                    pe.wait_ge(r_done, j - 1)
                    pe.wait_ge(i_done, j - 1)
                for w, done, s in ((wa, r_product, 2 * (j % 2)), (wx, x_product, 2 * (j % 2) + 1)):
                    for h in range(2):
                        mm = pe.matmul(ps[:, s, h * HALF:(h + 1) * HALF], w[:, j], xc[:, j, h * HALF:(h + 1) * HALF],
                                       start=True, stop=True)
                    mm.then_inc(done, 1)

        @block.scalar
        def _(act):
            for j in range(BT):
                act.wait_ge(r_product, j + 1)
                act.activation(r[:, j], ps[:, 2 * (j % 2)], ACT.Sigmoid, bias=m.p("d_ba", j)).then_inc(r_done, 1)
                act.wait_ge(x_product, j + 1)
                act.activation(ig[:, j], ps[:, 2 * (j % 2) + 1], ACT.Sigmoid, bias=m.p("d_bx", j)).then_inc(i_done, 1)
            act.wait_ge(negated, 1)
            for j in range(BT):
                act.wait_ge(r_done, j + 1)
                act.activation(a[:, j], r[:, j], ACT.Exp, scale=neg[:, j:j + 1]).then_inc(a_done, 1)
                act.activation(th[:, j], r[:, j], ACT.Tanh, scale=m.rate[:, j:j + 1]).then_inc(t_done, 1)
            for j in range(BT):
                act.wait_ge(t_done, j + 1)
                act.activation(root[:, j], th[:, j], ACT.Ln, bias=1.0).then_inc(ln_done, 1)
            for j in range(BT):
                act.wait_ge(ln_done, j + 1)
                act.activation(root[:, j], root[:, j], ACT.Exp, scale=-0.5).then_inc(inv_root, 1)
            for j in range(BT):
                act.activation(th[:, j], th[:, j], ACT.Sqrt, scale=2.0).then_inc(t_root, 1)

        @block.vector
        def _(dve):
            for s in range(2):
                dve.memset(x[:, s, 0:pad], 0.0).then_inc(zeroed, 1)
            dve.tensor_scalar(neg, m.rate, -1.0, None, ALU.mult).then_inc(negated, 1)
            for j in range(BT):
                dve.wait_ge(x_in[j % 2], 16 * (j // 2) + 16)
                conv(dve, x[:, j % 2], xc[:, j], m.p("d_conv", j * CONVK, CONVK), CONVK, m.p("d_conv_b", j), conv_chain,
                     j * CONVK)
            for j in range(BT):
                dve.wait_ge(t_root, j + 1)
                dve.tensor_tensor(th[:, j], th[:, j], root[:, j], ALU.mult).then_inc(half_b, 1)
                dve.wait_ge(half_b, j + 1)
                dve.tensor_tensor(th[:, j], th[:, j], ig[:, j], ALU.mult).then_inc(gated_b, 1)
                dve.wait_ge(gated_b, j + 1)
                dve.tensor_tensor(th[:, j], th[:, j], xc[:, j], ALU.mult).then_inc(b_done, 1)
                dve.wait_ge(b_done, j + 1)
                dve.tensor_tensor_scan(root[:, j], a[:, j], th[:, j], 0.0, ALU.mult, ALU.add).then_inc(scanned, 1)
            dve.wait_ge(z_in, 16)
            for j in range(BT):
                dve.wait_ge(scanned, j + 1)
                dve.tensor_tensor(r[:, j], r[:, j], root[:, j], ALU.mult).then_inc(gated, 1)


def bucket_ranges():
    n = np.arange(P)
    exact, buckets, far = 16, 32, 128
    large = exact + (np.log(np.maximum(n, 1) / exact) / np.log(far / exact) * (buckets - exact)).astype(np.int32)
    b = np.where(n < exact, n, np.minimum(large, buckets - 1))
    return [(int(v), int(np.argmax(b == v)), int(P - np.argmax(b[::-1] == v))) for v in sorted(set(b.tolist()))]


def band_phase(nc, m, d, bias, bias0):
    rel, row = m.take(32), m.take(384)
    ranges = bucket_ranges()
    with phase(nc, "rel_in", "cleared", "placed", "row_out", "band_in", "first_done") as (
            block, rel_in, cleared, placed, row_out, band_in, first_done):

        @block.sync
        def _(sp):
            sp.dma_start(rel[0:8], d["rel_bias"]).then_inc(rel_in, 16)
            sp.wait_ge(placed, len(ranges))
            sp.dma_start(d["band"], row[0:8].unsqueeze(1).to_broadcast([8, P, 384])).then_inc(row_out, 16)
            sp.wait_ge(row_out, 16)
            for h in range(8):
                src = bass.AP(d["band"].tensor, h * P * 384 + P - 1, [[383, P], [1, 2 * P]])
                sp.dma_start(bias[:, h], src).then_inc(band_in, 16)
            sp.wait_ge(band_in, 128)

        @block.vector
        def _(dve):
            dve.memset(row[0:8], NEG).then_inc(cleared, 1)
            dve.wait_ge(cleared, 1)
            dve.wait_ge(rel_in, 16)
            for b, lo, hi in ranges:
                dve.tensor_copy(row[0:8, 256 - hi:256 - lo], rel[0:8, b:b + 1].to_broadcast([8, hi - lo])).then_inc(placed, 1)
            dve.memset(bias0[:, :, 0:P], NEG).then_inc(first_done, 1)
            dve.wait_ge(band_in, 128)
            dve.tensor_copy(bias0[:, :, P:2 * P], bias[:, :, P:2 * P]).then_inc(first_done, 1)


def window_phase(nc, m, d, units, scale, q_tiles, window, biases, sink, k_of, v_of, out_of, q_of, keep_of, y):
    T = units
    qs = m.take(BT, P)
    win = m.take(3, 2 * P)
    vt = m.take(2, P)
    sc, pt = m.take(2, BW), m.take(2, BW)
    mx, nm, rs, ri, dk, es = (m.take(2, 2) for _ in range(6))
    with phase(nc, "cleared", "q_in", "k_in", "v_turned", "v_kept", "s_done", "s_kept", "max_done", "max_sink",
               "negated", "sink_diff", "p_ready", "sink_exp", "sum_done", "inverted", "p_scaled", "t_done", "t_kept",
               "o_done", "o_kept") as (
            block, cleared, q_in, k_in, v_turned, v_kept, s_done, s_kept, max_done, max_sink,
            negated, sink_diff, p_ready, sink_exp, sum_done, inverted, p_scaled, t_done, t_kept, o_done, o_kept):

        def blocks(eng, body):
            body(0)
            with eng.Fori(1, NB) as n:
                body(n)

        @block.sync
        def _(sp):
            def stage(n):
                sp.wait_ge(o_done, n * T)
                sp.dma_start(qs, d["in2"][q_tiles:q_tiles + BT, :, bass.ds(n * P, P)].rearrange("c p t -> p c t")).then_inc(q_in, 16)
                if window is not None:
                    if isinstance(n, int):
                        sp.wait_ge(cleared, 1)
                        sp.dma_start(win[:, :, P:2 * P], d["in2"][window:window + 3, :, 0:P].rearrange("c p t -> p c t")).then_inc(k_in, 16)
                    else:
                        sp.dma_start(win, d["in2"][window:window + 3, :, bass.ds(n * P - P, 2 * P)].rearrange("c p t -> p c t")).then_inc(k_in, 16)
            blocks(sp, stage)

        @block.tensor
        def _(pe):
            def block_(n):
                b = n * T
                pe.wait_ge(q_in, 16 * n + 16)
                if window is not None:
                    pe.wait_ge(k_in, 16 * n + 16)
                    pe.wait_ge(v_kept, n)
                    pe.wait_ge(t_kept, n * T)
                    for s in range(2):
                        mm = pe.transpose(m.ps[:, 4, s * P:(s + 1) * P], win[:, 2, s * P:(s + 1) * P], m.c(C_ID))
                    mm.then_inc(v_turned, 1)
                for t in range(T + 2):
                    if t < T:
                        pe.wait_ge(s_kept, b + max(t - 1, 0))
                        for g in range(2):
                            mm = pe.matmul(m.ps[:, 2 * (t % 2) + g, 0:2 * P], q_of(qs, t, g), k_of(win, t, g),
                                           start=True, stop=True)
                        mm.then_inc(s_done, 1)
                    if 0 <= t - 1 < T:
                        u = t - 1
                        pe.wait_ge(p_scaled, 2 * (b + u) + 2)
                        pe.wait_ge(t_kept, b + max(u - 1, 0))
                        if window is not None:
                            pe.wait_ge(v_kept, n + 1)
                        for c in range(4):
                            mm = pe.transpose(m.ps[:, 4 + u % 2, c * P:(c + 1) * P], sc[:, u % 2, c * P:(c + 1) * P], m.c(C_ID))
                        mm.then_inc(t_done, 1)
                    if 0 <= t - 2 < T:
                        u = t - 2
                        pe.wait_ge(t_kept, b + u + 1)
                        pe.wait_ge(o_kept, b + max(u - 1, 0))
                        for g in range(2):
                            for kb in range(2):
                                c = 2 * g + kb
                                mm = pe.matmul(out_of(m.ps[:, 6 + u % 2], g), v_of(vt, u, g, kb),
                                               pt[:, u % 2, c * P:(c + 1) * P], start=(kb == 0), stop=(kb == 1))
                        mm.then_inc(o_done, 1)
            blocks(pe, block_)

        @block.vector
        def _(dve):
            if window is not None:
                dve.memset(win[:, :, 0:P], 0.0).then_inc(cleared, 1)

            def block_(n):
                b = n * T
                for t in range(T + 3):
                    if t < T:
                        s = t % 2
                        dve.wait_ge(s_done, b + t + 1)
                        dve.wait_ge(t_done, b + max(t - 1, 0))
                        two = m.ps[:, 2 * s:2 * s + 2, 0:2 * P]
                        to = sc[:, s].rearrange("p (g k) -> p g k", g=2)
                        if biases is None:
                            dve.tensor_scalar(to, two, scale, None, ALU.mult).then_inc(s_kept, 1)
                        else:
                            bias = biases[isinstance(n, int)][:, 2 * t:2 * t + 2]
                            dve.scalar_tensor_tensor(to, two, scale, bias, ALU.mult, ALU.add).then_inc(s_kept, 1)
                        dve.wait_ge(s_kept, b + t + 1)
                        dve.wait_ge(sink_diff if sink else negated, b + t)
                        dve.tensor_reduce(mx[:, s], sc[:, s].rearrange("p (g k) -> p g k", g=2), AX.X, ALU.max).then_inc(max_done, 1)
                        dve.wait_ge(max_done, b + t + 1)
                        if sink:
                            dve.tensor_tensor(mx[:, s], mx[:, s], m.p("sinks", 2 * t, 2), ALU.max).then_inc(max_sink, 1)
                            dve.wait_ge(max_sink, b + t + 1)
                            dve.wait_ge(sink_exp, b + max(t - 1, 0))
                            dve.tensor_tensor(dk[:, s], m.p("sinks", 2 * t, 2), mx[:, s], ALU.subtract).then_inc(sink_diff, 1)
                        dve.wait_ge(p_ready, 2 * (b + max(t - 1, 0)))
                        dve.tensor_scalar(nm[:, s], mx[:, s], -1.0, None, ALU.mult).then_inc(negated, 1)
                    if 0 <= t - 1 < T:
                        u = t - 1
                        s = u % 2
                        dve.wait_ge(p_ready, 2 * (b + u) + 2)
                        if sink:
                            dve.wait_ge(sink_exp, b + u + 1)
                            dve.tensor_tensor(rs[:, s], rs[:, s], es[:, s], ALU.add).then_inc(sum_done, 1)
                            dve.wait_ge(sum_done, b + u + 1)
                        dve.wait_ge(p_scaled, 2 * (b + u))
                        dve.reciprocal(ri[:, s], rs[:, s]).then_inc(inverted, 1)
                        dve.wait_ge(inverted, b + u + 1)
                        for g in range(2):
                            w = sc[:, s, g * 2 * P:(g + 1) * 2 * P]
                            dve.tensor_scalar(w, w, ri[:, s, g:g + 1], None, ALU.mult).then_inc(p_scaled, 1)
                    if 0 <= t - 3 < T:
                        u = t - 3
                        dve.wait_ge(o_done, b + u + 1)
                        to, of = keep_of(y, u, n, m.ps[:, 6 + u % 2])
                        dve.tensor_copy(to, of).then_inc(o_kept, 1)
            blocks(dve, block_)

        @block.scalar
        def _(act):
            def block_(n):
                b = n * T
                if window is not None:
                    act.wait_ge(v_turned, n + 1)
                    act.wait_ge(o_done, n * T)
                    act.activation(vt, m.ps[:, 4, 0:2 * P].rearrange("p (s f) -> p s f", s=2), ACT.Copy).then_inc(v_kept, 1)
                for t in range(T + 1):
                    if t < T:
                        s = t % 2
                        act.wait_ge(negated, b + t + 1)
                        act.wait_ge(inverted, b + max(t - 1, 0))
                        for g in range(2):
                            w = sc[:, s, g * 2 * P:(g + 1) * 2 * P]
                            act.activation(w, w, ACT.Exp, bias=nm[:, s, g:g + 1], accum_out=rs[:, s, g:g + 1]).then_inc(p_ready, 1)
                        if sink:
                            act.wait_ge(sink_diff, b + t + 1)
                            act.activation(es[:, s], dk[:, s], ACT.Exp).then_inc(sink_exp, 1)
                    if 0 <= t - 1 < T:
                        u = t - 1
                        act.wait_ge(t_done, b + u + 1)
                        act.wait_ge(o_done, b + max(u - 1, 0))
                        act.activation(pt[:, u % 2], m.ps[:, 4 + u % 2], ACT.Copy).then_inc(t_kept, 1)
            blocks(act, block_)


def sliding_phases(nc, m, d):
    m.clear()
    y = m.take(BT, S)
    bias, bias0 = m.take(8, 2 * P), m.take(8, 2 * P)
    base = m.top
    band_phase(nc, m, d, bias, bias0)
    m.top = base
    window_phase(
        nc, m, d, 4, 64.0 ** -0.5, T_CQ, T_CK, (bias, bias0), True,
        q_of=lambda qs, t, g: qs[64 * g:64 * g + 64, t],
        k_of=lambda win, t, g: win[64 * g:64 * g + 64, t // 2],
        v_of=lambda vt, t, g, kb: vt[:, kb, 64 * (t // 2):64 * (t // 2) + 64],
        out_of=lambda bank, g: bank[64 * g:64 * g + 64, 0:P],
        keep_of=lambda y, t, n, bank: (y[:, t, bass.ds(n * P, P)], bank[:, 0:P]), y=y)
    m.top = base
    gated_store_phase(nc, m, d, y, None, None, T_CZ, 2 * BT)


def memory_phases(nc, m, d):
    m.clear()
    y = m.take(BT, S)
    mem_k = m.take(BT, MEM)
    mem_v = m.take(MEM // P, BW)
    base = m.top
    mem = m.take(DC, MEM)
    sq, root = m.take(2, MEM), m.take(MEM)
    wt = m.take(BT, DC * P)
    wv = m.take(DC, BW)
    with phase(nc, "mem_in", "w_in", "squared", "summed", "logged", "rooted", "scaled", "k_done", "k_kept", "v_done",
               "v_kept") as (
            block, mem_in, w_in, squared, summed, logged, rooted, scaled, k_done, k_kept, v_done, v_kept):

        @block.sync
        def _(sp):
            sp.dma_start(mem, d["mem"].rearrange("(k p) t -> p k t", p=P)).then_inc(mem_in, 16)
            sp.dma_start(wt, d["w_mk"].rearrange("c p f -> p c f")).then_inc(w_in, 16)
            sp.dma_start(wv, d["w_mv"]).then_inc(w_in, 16)

        @block.scalar
        def _(act):
            act.wait_ge(mem_in, 16)
            for k in range(DC):
                if k >= 2:
                    act.wait_ge(summed, k - 1)
                act.activation(sq[:, k % 2], mem[:, k], ACT.Square).then_inc(squared, 1)
            act.wait_ge(summed, DC)
            act.activation(root, m.ps[:, 0, 0:MEM], ACT.Ln, bias=m.c(C_EPS, 1), scale=1.0 / D).then_inc(logged, 1)
            act.wait_ge(logged, 1)
            act.activation(root, root, ACT.Exp, scale=-0.5).then_inc(rooted, 1)
            for j in range(BT):
                act.wait_ge(k_done, j + 1)
                act.activation(mem_k[:, j], m.ps[:, 1 + j % 2, 0:MEM], ACT.Copy).then_inc(k_kept, 1)
            for j in range(MEM // P):
                act.wait_ge(v_done, j + 1)
                act.activation(mem_v[:, j], m.ps[:, 3 + j, :], ACT.Copy).then_inc(v_kept, 1)

        @block.vector
        def _(dve):
            dve.wait_ge(rooted, 1)
            for k in range(DC):
                dve.scalar_tensor_tensor(mem[:, k], mem[:, k], m.p("mem_g", k), root, ALU.mult, ALU.mult).then_inc(scaled, 1)

        @block.tensor
        def _(pe):
            for k in range(DC):
                pe.wait_ge(squared, k + 1)
                pe.matmul(m.ps[:, 0, 0:MEM], m.c(C_ONE), sq[:, k % 2], start=(k == 0), stop=(k == DC - 1)).then_inc(summed, 1)
            pe.wait_ge(scaled, DC)
            pe.wait_ge(w_in, 32)
            for j in range(BT):
                if j >= 2:
                    pe.wait_ge(k_kept, j - 1)
                for k in range(DC):
                    mm = pe.matmul(m.ps[:, 1 + j % 2, 0:MEM], wt[:, j, k * P:(k + 1) * P], mem[:, k],
                                   start=(k == 0), stop=(k == DC - 1))
                mm.then_inc(k_done, 1)
            for j in range(MEM // P):
                for k in range(DC):
                    mm = pe.matmul(m.ps[:, 3 + j, :], mem[:, k, j * P:(j + 1) * P], wv[:, k],
                                   start=(k == 0), stop=(k == DC - 1))
                mm.then_inc(v_done, 1)
    m.top = base
    window_phase(
        nc, m, d, 2, float(P) ** -0.5, T_EQ, None, None, False,
        q_of=lambda qs, t, g: qs[:, 2 * t + g],
        k_of=lambda win, t, g: mem_k[:, 2 * t + g],
        v_of=lambda vt, t, g, kb: mem_v[:, kb, (2 * t + g) * P:(2 * t + g + 1) * P],
        out_of=lambda bank, g: bank[:, g * P:(g + 1) * P],
        keep_of=lambda y, t, n, bank: (y[:, 2 * t:2 * t + 2, bass.ds(n * P, P)],
                                       bank[:, 0:2 * P].rearrange("p (g f) -> p g f", g=2)), y=y)
    m.top = base
    gated_store_phase(nc, m, d, y, None, None, T_EZ, 4 * BT)


def merge_phase(nc, m, d, merged):
    y = m.take(NBR * BT, S)
    wg, wb = m.take(2, DC, P), m.take(2, BT, P)
    sg = m.take(2, S)
    gate_ps = m.ps[:, 0:4, :].rearrange("p (s h) f -> p s (h f)", s=2)
    br_ps = m.ps[:, 4:8, :].rearrange("p (s h) f -> p s (h f)", s=2)
    gate_bias = m.p("b_gate", 0, 40)
    T = 2 * NBR
    with phase(nc, "y_in", "wg_a", "wg_b", "wb_a", "wb_b", "gate_done", "branch_done", "sig_done", "weighted",
               "added") as (
            block, y_in, wg_a, wg_b, wb_a, wb_b, gate_done, branch_done, sig_done, weighted, added):
        g_in, b_in = (wg_a, wg_b), (wb_a, wb_b)

        @block.sync
        def _(sp):
            def load(i, u):
                j, n, s = 2 * i + u // NBR, u % NBR, u % 2
                if not (isinstance(i, int) and u < 2):
                    sp.wait_ge(branch_done, i * T + u - 1)
                sp.dma_start(wg[:, s].rearrange("p k f -> p (k f)"), d["w_gate"][n * DC + j]).then_inc(g_in[s], 16)
                sp.dma_start(wb[:, s].rearrange("p k f -> p (k f)"), d["w_br"][n, j]).then_inc(b_in[s], 16)
            load(0, 0)
            sp.dma_start(y, d["y"].rearrange("c p t -> p c t")).then_inc(y_in, 16)
            for u in range(1, T):
                load(0, u)
            with sp.Fori(1, DC // 2) as i:
                for u in range(T):
                    load(i, u)

        def rounds(eng, body):
            for u in range(T):
                body(0, u)
            with eng.Fori(1, DC // 2) as i:
                for u in range(T):
                    body(i, u)

        @block.tensor
        def _(pe):
            def products(i, u):
                s, n = u % 2, u % NBR
                first = isinstance(i, int) and u < 2
                pe.wait_ge(g_in[s], 16 * (i * NBR + u // 2) + 16)
                if not first:
                    pe.wait_ge(sig_done, i * T + u - 1)
                for k in range(DC):
                    for h in range(2):
                        mm = pe.matmul(gate_ps[:, s, h * HALF:(h + 1) * HALF], wg[:, s, k],
                                       m.act[:, k, h * HALF:(h + 1) * HALF], start=(k == 0), stop=(k == DC - 1))
                mm.then_inc(gate_done, 1)
                pe.wait_ge(b_in[s], 16 * (i * NBR + u // 2) + 16)
                if isinstance(i, int) and u == 0:
                    pe.wait_ge(y_in, 16)
                if not first:
                    pe.wait_ge(weighted, i * T + u - 1)
                for k in range(BT):
                    for h in range(2):
                        mm = pe.matmul(br_ps[:, s, h * HALF:(h + 1) * HALF], wb[:, s, k],
                                       y[:, n * BT + k, h * HALF:(h + 1) * HALF], start=(k == 0), stop=(k == BT - 1))
                mm.then_inc(branch_done, 1)
            rounds(pe, products)

        @block.scalar
        def _(act):
            def sigmoid(i, u):
                j, n, s = 2 * i + u // NBR, u % NBR, u % 2
                act.wait_ge(gate_done, i * T + u + 1)
                if not (isinstance(i, int) and u < 2):
                    act.wait_ge(added, i * T + u - 1)
                act.activation(sg[:, s], gate_ps[:, s], ACT.Sigmoid,
                               bias=gate_bias[:, bass.ds(n * DC + j, 1)]).then_inc(sig_done, 1)
            rounds(act, sigmoid)

        @block.vector
        def _(dve):
            def weigh(i, u):
                j, n, s = 2 * i + u // NBR, u % NBR, u % 2
                dve.wait_ge(sig_done, i * T + u + 1)
                dve.wait_ge(branch_done, i * T + u + 1)
                to = merged[:, j] if n == 0 else sg[:, s]
                ins = dve.tensor_tensor(to, sg[:, s], br_ps[:, s], ALU.mult)
                ins.then_inc(weighted, 1)
                dve.wait_ge(weighted, i * T + u + 1)
                if n == 0:
                    dve.wait_ge(weighted, i * T + u + 1).then_inc(added, 1)
                else:
                    dve.wait_ge(added, i * T + u)
                    dve.tensor_tensor(merged[:, j], merged[:, j], sg[:, s], ALU.add).then_inc(added, 1)
            rounds(dve, weigh)


def second_block(nc, m, d):
    m.clear()
    norm_phase(nc, m, m.res, m.act, m.p("pre_g", 0, 8), DC, (m.take(2, S), m.take(S)))
    m.clear()
    gemm_phase(nc, m, d["w_in2"][0:N_PLAIN], m.act, DC, N_PLAIN, "store", bias=m.p("b_in", 0, N_PLAIN), out=d["in2"])
    m.clear()
    gemm_phase(nc, m, d["w_in2"][N_PLAIN:N_IN2], m.act, DC, N_IN2 - N_PLAIN, "store",
               bias=m.p("b_in", N_PLAIN, N_IN2 - N_PLAIN), func=ACT.Silu, out=d["in2"], tile0=N_PLAIN)
    m.clear()
    rows_phase(nc, m, m.act, DC, d["w_ab"], 8, NB, d["ab"])
    small_phase(nc, m, d)
    delta_phases(nc, m, d)
    conformer_phase(nc, m, d)
    recurrence_phase(nc, m, d)
    sliding_phases(nc, m, d)
    memory_phases(nc, m, d)
    m.clear()
    merged = m.take(DC, S)
    base = m.top
    merge_phase(nc, m, d, merged)
    m.top = base
    gemm_phase(nc, m, d["w_out"], merged, DC, DC, "keep", dst=m.act)
    m.top = base
    norm_phase(nc, m, m.act, m.act, m.p("post_g", 0, 8), DC, (m.take(2, S), m.take(S)), residual=m.res)
    with phase(nc, "all_out") as (block, all_out):
        @block.sync
        def _(sp):
            sp.dma_start(d["out"].rearrange("(k p) t -> p k t", p=P), m.act).then_inc(all_out, 16)
            sp.wait_ge(all_out, 16)


SCRATCH = {
    "rope": (2, P, S), "in1": (13, P, S), "v_sb": (NB, P, BW), "k_rope": (ROPE, S), "q_rope": (2 * P, S),
    "mla_q": (MLA_H, P, S), "mla_k": (MLA_H, P, S), "mla_v": (NB, P, BW),
    "in2": (N_IN2, P, S), "ab": (NB, P, 8), "delta": (3 * BT, P, S), "kv_rows": (NB, P, 3 * BW),
    "band": (8, P, 384), "mem_v": (MEM // P, P, BW), "y": (NBR * BT, P, S),
}


def first_block(nc, m, d):
    load_phase(nc, m, d)
    m.clear()
    norm_phase(nc, m, m.res, m.act, m.p("attn_g", 0, 8), DC, (m.take(2, S), m.take(S)))
    m.clear()
    gemm_phase(nc, m, d["w_in1"], m.act, DC, 13, "store", out=d["in1"])
    m.clear()
    rows_phase(nc, m, m.act, DC, d["w_v1"], BW, NB, d["v_sb"])
    stick_phase(nc, m, d)
    latent_phases(nc, m, d)
    latent_attention_phase(nc, m, d)
    m.clear()
    scratch = (m.take(2, S), m.take(S))
    norm_phase(nc, m, m.act[:, 0:4], m.act[:, 0:4], m.p("sb_g", 0, 4), 4, scratch)
    norm_phase(nc, m, m.act[:, 4:8], m.act[:, 4:8], m.p("mla_g", 0, 4), 4, scratch)
    gemm_phase(nc, m, d["w_o"], m.act, DC, DC, "add", dst=m.res)
    m.clear()
    norm_phase(nc, m, m.res, m.act, m.p("mlp_g", 0, 8), DC, (m.take(2, S), m.take(S)))
    m.clear()
    part = F_FF // P // 2
    hidden = m.take(part, S)
    base = m.top
    for n in range(2):
        m.top = base
        gemm_phase(nc, m, d["w_up"][n * part:(n + 1) * part], m.act, DC, part, "relu2", dst=hidden)
        m.top = base
        gemm_phase(nc, m, d["w_down"][n], hidden, part, DC, "add", dst=m.res)
    m.clear()
    norm_phase(nc, m, m.res, m.res, m.p("final_g", 0, 8), DC, (m.take(2, S), m.take(S)))


def program(nc, d):
    with ExitStack() as ctx:
        arena = ctx.enter_context(nc.sbuf_tensor("arena", [P, A_END], F32))
        psum = ctx.enter_context(nc.psum_tensor("psum", [P, 8, HALF], F32))
        for name, shape in SCRATCH.items():
            d[name] = nc.dram_tensor("scratch_" + name, shape, F32).ap()
        m = Mem(arena, psum)
        first_block(nc, m, d)
        second_block(nc, m, d)


def layout(inp):
    g = {k: np.asarray(v) for k, v in inp.items()}

    def tiles(w):
        k, n = w.shape
        return np.ascontiguousarray(w.reshape(k // P, P, n // P, P).transpose(2, 1, 0, 3).reshape(n // P, P, k))

    def rows(w):
        k, n = w.shape
        return np.ascontiguousarray(w.reshape(k // P, P, n).transpose(1, 0, 2))

    def cols(v):
        return v.reshape(-1, P).T

    def swap(w):
        k, n = w.shape
        return w.reshape(k, n // ROPE, 2, ROPE // 2)[:, :, ::-1].reshape(k, n)

    w_in, w_qb, w_kvb = g["w_in"][0], g["w_q_b"][0], g["w_kv_b"][0]
    kr = w_in[:, 1920:1984]
    qb = w_qb.reshape(Q_LORA, MLA_H, NOPE + ROPE)
    qr = qb[:, :, NOPE:].reshape(Q_LORA, MLA_H * ROPE)
    kvb = w_kvb.reshape(KV_LORA, MLA_H, 2 * P)
    out = {
        "x": np.ascontiguousarray(g["x"][0].T),
        "positions": g["positions"],
        "w_in1": tiles(np.concatenate([w_in[:, 0:1024], w_in[:, 1536:1920], kr, kr, swap(kr), swap(kr)], 1)),
        "w_v1": rows(w_in[:, 1024:1536]),
        "w_qn": tiles(qb[:, :, :NOPE].reshape(Q_LORA, -1)),
        "w_qr": tiles(np.concatenate([qr, swap(qr)], 1)),
        "w_kn": tiles(kvb[:, :, :P].reshape(KV_LORA, -1)),
        "w_vm": rows(np.ascontiguousarray(kvb[:, :, P:]).reshape(KV_LORA, -1)),
        "w_o": tiles(g["w_o"][0]),
        "w_up": tiles(g["w_up"][0]),
        "w_down": np.stack([tiles(part) for part in np.split(g["w_down"][0], 2, axis=0)]),
    }
    w2, b2 = g["w_in_2"][0], g["b_in_2"][0]
    off = np.cumsum([0, 1536, 512, 4, 4, 1024, 512, 512, 256, 512, 512, 512, 512, 512, 5120])
    (qkv, az, be, al, glu, bz, cq, ckv, cz, dx, dz, eq, ez, gate) = [(off[n], off[n + 1]) for n in range(14)]

    def pick(a):
        ck = a[..., ckv[0]:ckv[0] + 128]
        cv = a[..., ckv[0] + 128:ckv[1]]
        k0, k1 = ck[..., :64], ck[..., 64:]
        part = [a[..., lo:hi] for lo, hi in (qkv, glu, cq)]
        part += [k0, k0, k1, k1, cv]
        part += [a[..., lo:hi] for lo, hi in (dx, eq, az, bz, cz, dz, ez)]
        return np.concatenate(part, -1)

    wbr = g["w_br_2"][0]

    def diagonal(w):
        t = np.zeros((BT, P, P), w.dtype)
        for n in range(BT):
            t[n, :64, :64] = w[2 * n]
            t[n, 64:, 64:] = w[2 * n + 1]
        return np.ascontiguousarray(t.transpose(1, 0, 2))

    def taps(w):
        k, c = w.shape
        return w.T.reshape(c // P, P, k).transpose(1, 0, 2).reshape(P, -1)

    def spread(v):
        return np.broadcast_to(v.reshape(1, -1), (P, v.size))

    out.update({
        "mem": np.ascontiguousarray(g["mem_2"][0].T),
        "w_in2": tiles(pick(w2)),
        "w_ab": rows(np.concatenate([w2[:, be[0]:be[1]], w2[:, al[0]:al[1]]], 1)),
        "w_gate": tiles(w2[:, gate[0]:]),
        "w_br": np.stack([tiles(wbr[n]) for n in range(NBR)]),
        "w_out": tiles(g["w_out_2"][0]),
        "w_mk": tiles(g["w_mem_kv_2"][0][:, :BW]),
        "w_mv": rows(g["w_mem_kv_2"][0][:, BW:]),
        "w_da": diagonal(g["d_w_a_2"][0]),
        "w_dx": diagonal(g["d_w_x_2"][0]),
        "rel_bias": np.ascontiguousarray(g["rel_bias_2"].T),
        "consts": constants(),
    })
    vec = {
        "attn_g": cols(g["attn_norm_g"][0]), "q_a_g": cols(g["q_a_norm_g"][0]), "kv_a_g": cols(g["kv_a_norm_g"][0]),
        "sb_g": cols(g["sb_out_norm_g"][0]), "mla_g": cols(g["mla_out_norm_g"][0]), "mlp_g": cols(g["mlp_norm_g"][0]),
        "final_g": cols(g["final_norm_g"]), "pre_g": cols(g["g_pre_2"][0]), "post_g": cols(g["g_post_2"][0]),
        "mem_g": cols(g["g_mem_2"][0]), "b_in": cols(pick(b2)), "b_gate": cols(b2[gate[0]:]),
        "a_conv": taps(g["a_conv_w_2"][0]), "a_norm": cols(g["a_norm_g_2"][0]), "b_conv": taps(g["b_dw_w_2"][0]),
        "b_conv_b": cols(g["b_dw_b_2"][0]), "b_ln_g": cols(g["b_ln_g_2"][0]), "b_ln_b": cols(g["b_ln_b_2"][0]),
        "d_conv": taps(g["d_conv_w_2"][0]), "d_conv_b": cols(g["d_conv_b_2"][0]), "d_ba": cols(g["d_b_a_2"][0]),
        "d_bx": cols(g["d_b_x_2"][0]), "d_lam": cols(g["d_lambda_2"][0]),
        "ab_bias": spread(np.concatenate([b2[be[0]:be[1]], b2[al[0]:al[1]]])),
        "a_log": spread(g["a_log_2"][0]), "a_dt": spread(g["a_dt_bias_2"][0]), "sinks": spread(g["c_sinks_2"][0]),
    }
    for n, w in _PAR:
        assert vec[n].shape == (P, w), (n, vec[n].shape)
    out["params"] = np.ascontiguousarray(np.concatenate([vec[n] for n, _ in _PAR], 1))
    return out


def kernel(**inputs):
    import concourse.bacc as _bacc
    from concourse.bass_utils import run_bass_kernel_spmd as _run

    nc = _bacc.Bacc("TRN2", target_bir_lowering=False, num_devices=1)
    arrays, d = {}, {}
    for name, a in layout(inputs).items():
        arrays["in_" + name] = a
        d[name] = nc.dram_tensor("in_" + name, a.shape, mybir.dt.from_np(a.dtype), kind="ExternalInput").ap()
    d["out"] = nc.dram_tensor("out_x", (D, S), F32, kind="ExternalOutput").ap()
    program(nc, d)
    r = _run(nc, [arrays], core_ids=[0])
    return np.ascontiguousarray(r.results[0]["out_x"].T)[None]
```

```python
from contextlib import ExitStack, contextmanager
from math import pi

import numpy as np
import concourse.bass as bass
from concourse import mybir

F32 = mybir.dt.float32
I32 = mybir.dt.int32
F32R = mybir.dt.float32r
ALU = mybir.AluOpType
ACT = mybir.ActivationFunctionType
AX = mybir.AxisListType

P = 128
S = 1024
NB = S // P
D = 1024
DC = D // P
HALF = 512
F_FF = 4 * D
SB_H, SB_D = 8, 64
MLA_H, NOPE, ROPE = 4, 128, 64
MLA_SCALE = float((NOPE + ROPE) ** -0.5)
Q_LORA, KV_LORA = 256, 128
MEM = 256
BW = 512
BT = BW // P
NBR = 5
CONVK, CONFK = 4, 31
EPS = 1e-6
NEG = -1e30

C_ID = 0
C_ONE = C_ID + P
C_GT = C_ONE + P
C_LE = C_GT + P
C_LT = C_LE + P
C_NGE = C_LT + P
C_NCAUSAL = C_NGE + P
C_LVL = C_NCAUSAL + P
C_FREQ = C_LVL + 7 * P
C_SGN = C_FREQ + 1
C_EPS = C_SGN + 1
C_QS = C_EPS + 1
C_W = C_QS + 8


def constants():
    p = np.arange(P)[:, None]
    f = np.arange(P)[None, :]
    c = np.zeros((P, C_W), np.float32)
    c[:, C_ID:C_ID + P] = p == f
    c[:, C_ONE:C_ONE + P] = 1
    c[:, C_GT:C_GT + P] = p > f
    c[:, C_LE:C_LE + P] = p <= f
    c[:, C_LT:C_LT + P] = p < f
    c[:, C_NGE:C_NGE + P] = np.where(p >= f, NEG, 0)
    c[:, C_NCAUSAL:C_NCAUSAL + P] = np.where(f > p, NEG, 0)
    for lvl in range(7):
        b = 1 << lvl
        same = (p // (2 * b)) == (f // (2 * b))
        c[:, C_LVL + lvl * P:C_LVL + (lvl + 1) * P] = same & (p % (2 * b) < b) & (f % (2 * b) >= b)
    half = ROPE // 2
    c[:, C_FREQ] = (10000.0 ** (-(np.arange(P) % half) / half)).astype(np.float32)
    c[:, C_SGN] = np.where(np.arange(P) % ROPE < half, -1, 1)
    c[:, C_EPS] = EPS
    c[:, C_QS:C_QS + 4] = 128.0 ** -0.5
    c[:, C_QS + 4:C_QS + 8] = 1
    return c


_PAR = [("attn_g", 8), ("q_a_g", 2), ("kv_a_g", 1), ("sb_g", 4), ("mla_g", 4), ("mlp_g", 8), ("final_g", 8),
        ("pre_g", 8), ("post_g", 8), ("mem_g", 8), ("b_in", 55), ("b_gate", 40), ("a_conv", 48), ("a_norm", 1),
        ("b_conv", 124), ("b_conv_b", 4), ("b_ln_g", 4), ("b_ln_b", 4), ("d_conv", 16), ("d_conv_b", 4),
        ("d_ba", 4), ("d_bx", 4), ("d_lam", 4), ("ab_bias", 8), ("a_log", 4), ("a_dt", 4), ("sinks", 8)]
PAR = {}
_at = 0
for _n, _w in _PAR:
    PAR[_n] = (_at, _w)
    _at += _w
PAR_W = _at

T_AQKV, T_GLU, T_CQ, T_CK, T_CV, T_DX, T_EQ = 0, 12, 20, 24, 26, 27, 31
N_PLAIN = 35
T_AZ, T_BZ, T_CZ, T_DZ, T_EZ = 35, 39, 43, 47, 51
N_IN2 = 55

A_CONST = 0
A_PAR = A_CONST + C_W + -C_W % 8
A_SMALL = A_PAR + PAR_W + -PAR_W % 8
A_RES = A_SMALL + 80
A_SPLIT = A_RES + DC * S
A_WORK = A_SPLIT + 2 * DC * S
A_END = 52800
A_ACT = A_END - DC * S


class Split:

    def __init__(self, hi, lo):
        self.hi, self.lo = hi, lo

    def __getitem__(self, key):
        return Split(self.hi[key], self.lo[key])


class Mem:

    def __init__(self, nc):
        self.nc = nc
        self.base = nc.sbuf_base + (-nc.sbuf_base) % 32
        self.ps = nc.alloc_psum_tensor("psum", [P, 8, HALF], F32)[:, :, :]
        self.const = self.at("const", A_CONST, F32, C_W)
        self.par = self.at("par", A_PAR, F32, PAR_W)
        self.res = self.at("res", A_RES, F32, DC, S)
        self.act = self.at("act", A_ACT, F32, DC, S)
        small = self.at("small", A_SMALL, F32, 80)
        self.beta = small[:, 0:32].rearrange("p (c h) -> p c h", h=4)
        self.decay = small[:, 32:64].rearrange("p (c h) -> p c h", h=4)
        self.rate = small[:, 64:68]
        self.top, self.end = A_SPLIT, A_END
        self.split = self.take_split("normed", DC, S)

    def at(self, name, column, dtype, *shape):
        t = self.nc.alloc_sbuf_tensor_at(f"{name}_{self.nc.next_id()}", [P] + list(shape), dtype,
                                         offset=self.base + 4 * column)
        return t[(slice(None),) * (len(shape) + 1)]

    def c(self, at, w=P):
        return self.const[:, at:at + w]

    def p(self, name, k=0, w=1):
        at = PAR[name][0] + k
        return self.par[:, at:at + w]

    def clear(self, top=A_SPLIT, end=A_END):
        self.top, self.end = top, end

    def take(self, *shape):
        self.top += -self.top % 8
        v = self.at("buffer", self.top, F32, *shape)
        self.top += int(np.prod(shape))
        assert self.top <= self.end, self.top
        return v

    def take_split(self, name, *shape):
        n = int(np.prod(shape))
        self.top += -self.top % 8
        parts = [self.at(f"{name}_{part}", self.top + j * n, F32R, *shape) for j, part in enumerate(("hi", "lo"))]
        self.top += 2 * n
        assert self.top <= self.end, self.top
        return Split(*parts)


LN_EXP = "natural_log_exp_and_others"


@contextmanager
def phase(nc, *names):
    at = nc.next_id()
    sems = [nc.alloc_semaphore(f"{n}_{at}") for n in names]
    with nc.Block() as block:
        yield (block, *sems)
    nc.clear_and_free_semaphores(sems)
    nc.all_engine_barrier()


def loop(eng, n, body):
    body(0)
    with eng.Fori(1, n) as i:
        body(i)


def load_phase(nc, m, d):
    m.clear()
    pos_i = m.take(S)
    pos, ang, turns, red = m.take(S), m.take(S), m.take(S), m.take(2, S)
    tab = m.take(2, S)
    two_pi = (6.28125, 0.0019340515136718750, 2 * pi - 6.28125 - 0.0019340515136718750)
    lim = 3.1415925
    with phase(nc, "params_in", "x_in", "pos_in", "reduced", "sines", "signed", "tables_out") as (
            block, params_in, x_in, pos_in, reduced, sines, signed, tables_out):

        @block.sync
        def _(sp):
            sp.dma_start(m.const, d["consts"]).then_inc(params_in, 16)
            sp.dma_start(m.par, d["params"]).then_inc(params_in, 16)
            sp.dma_start(pos_i.bitcast(I32), d["positions"].partition_broadcast(P)).then_inc(pos_in, 16)
            sp.dma_start(m.res, d["x"].rearrange("(k p) t -> p k t", p=P)).then_inc(x_in, 16)
            sp.wait_ge(signed, 1)
            sp.dma_start(d["rope"].rearrange("a p t -> p a t"), tab).then_inc(tables_out, 16)
            sp.wait_ge(tables_out, 16)
            sp.wait_ge(x_in, 16)
            sp.wait_ge(params_in, 32)

        @block.vector
        def _(dve):
            n = [0]

            def step(ins):
                n[0] += 1
                ins.then_inc(reduced, 1)
                dve.wait_ge(reduced, n[0])

            dve.wait_ge(pos_in, 16)
            dve.wait_ge(params_in, 32)
            step(dve.tensor_copy(pos, pos_i.bitcast(I32)))
            step(dve.tensor_scalar(ang, pos, m.c(C_FREQ, 1), None, ALU.mult))
            magic = float(3 << 22)
            for j, shift in enumerate((0.25, 0.0)):
                step(dve.tensor_scalar(turns, ang, 1 / (2 * pi), shift, ALU.mult, ALU.add))
                step(dve.tensor_scalar(turns, turns, magic, None, ALU.add))
                step(dve.tensor_scalar(turns, turns, magic, None, ALU.subtract))
                step(dve.scalar_tensor_tensor(red[:, j], turns, -two_pi[0], ang, ALU.mult, ALU.add))
                step(dve.scalar_tensor_tensor(red[:, j], turns, -two_pi[1], red[:, j], ALU.mult, ALU.add))
                step(dve.scalar_tensor_tensor(red[:, j], turns, -two_pi[2], red[:, j], ALU.mult, ALU.add))
                if j == 0:
                    step(dve.tensor_scalar(red[:, j], red[:, j], pi / 2, None, ALU.add))
                step(dve.tensor_scalar(red[:, j], red[:, j], lim, -lim, ALU.min, ALU.max))
            dve.wait_ge(sines, 2)
            dve.tensor_scalar(tab[:, 1], tab[:, 1], m.c(C_SGN, 1), None, ALU.mult).then_inc(signed, 1)

        @block.scalar
        def _(act):
            act.wait_ge(reduced, 17)
            for j in range(2):
                act.activation(tab[:, j], red[:, j], ACT.Sin).then_inc(sines, 1)


def norm_phase(nc, m, src, dst, gain, kc, scratch, residual=None, spill=None):
    sq, root = scratch
    split = isinstance(dst, Split)
    plain = sq if split else None
    tot = m.ps[:, 0:2, :].rearrange("p a b -> p (a b)")
    with phase(nc, "squared", "summed", "logged", "rooted", "scaled", "hi_done", "lo_done", "spilled") as (
            block, squared, summed, logged, rooted, scaled, hi_done, lo_done, spilled):

        if spill is not None:
            @block.sync
            def _(sp):
                sp.dma_start(spill.rearrange("k p t -> p k t"), src).then_inc(spilled, 16)
                sp.wait_ge(spilled, 16)

        @block.scalar
        def _(act):
            act.preload_act_table_set(LN_EXP)
            for k in range(kc):
                if k >= 2:
                    act.wait_ge(summed, k - 1)
                act.activation(sq[:, k % 2], src[:, k], ACT.Square).then_inc(squared, 1)
            act.wait_ge(summed, kc)
            act.activation(root, tot, ACT.Ln, bias=m.c(C_EPS, 1), scale=1.0 / (kc * P)).then_inc(logged, 1)
            act.wait_ge(logged, 1)
            act.activation(root, root, ACT.Exp, scale=-0.5).then_inc(rooted, 1)
            if split:
                for k in range(kc):
                    act.wait_ge(scaled, k + 1)
                    act.activation(dst.hi[:, k], plain[:, k % 2], ACT.Copy).then_inc(hi_done, 1)

        @block.tensor
        def _(pe):
            for k in range(kc):
                pe.wait_ge(squared, k + 1)
                for h in range(2):
                    mm = pe.matmul(tot[:, h * HALF:(h + 1) * HALF], m.c(C_ONE), sq[:, k % 2, h * HALF:(h + 1) * HALF],
                                   start=(k == 0), stop=(k == kc - 1))
                mm.then_inc(summed, 1)

        @block.vector
        def _(dve):
            def low(k):
                dve.wait_ge(hi_done, k + 1)
                dve.tensor_tensor(dst.lo[:, k], plain[:, k % 2], dst.hi[:, k].bitcast(F32), ALU.subtract).then_inc(lo_done, 1)

            dve.wait_ge(rooted, 1)
            for k in range(kc):
                if split and k >= 2:
                    dve.wait_ge(lo_done, k - 1)
                to = plain[:, k % 2] if split else dst[:, k]
                dve.scalar_tensor_tensor(to, src[:, k], gain[:, k:k + 1], root, ALU.mult, ALU.mult).then_inc(scaled, 1)
                if split and k >= 1:
                    low(k - 1)
            if split:
                low(kc - 1)
            if residual is not None:
                for k in range(kc):
                    dve.wait_ge(scaled, k + 1)
                    dve.tensor_tensor(dst[:, k], dst[:, k], residual[:, k], ALU.add)


def split_phase(nc, src, dst, kc):
    with phase(nc, "hi_done") as (block, hi_done):

        @block.scalar
        def _(act):
            for k in range(kc):
                act.activation(dst.hi[:, k], src[:, k], ACT.Copy).then_inc(hi_done, 1)

        @block.vector
        def _(dve):
            for k in range(kc):
                dve.wait_ge(hi_done, k + 1)
                dve.tensor_tensor(dst.lo[:, k], src[:, k], dst.hi[:, k].bitcast(F32), ALU.subtract)


def three_passes(pe, out, w, x, first, last):
    pe.matmul(out, w.hi, x.hi, start=first, stop=False)
    pe.matmul(out, w.hi, x.lo, start=False, stop=False)
    return pe.matmul(out, w.lo, x.hi, start=False, stop=last)


def halves(v):
    return [v[:, h * HALF:(h + 1) * HALF] for h in range(2)]


def gemm_phase(nc, m, w, src, kc, tiles, finish, bias=None, func=None, out=None, dst=None, tile0=0, reload=None):
    raw = m.take(2, kc, P)
    ws = m.take_split("w", 2, kc, P)
    tmp = m.take(2, S)
    ps = m.ps[:, 0:4, :].rearrange("p (s h) f -> p s (h f)", s=2)
    pairs = tiles // 2
    assert pairs >= 2
    with phase(nc, "weights_a", "weights_b", "w_hi", "w_lo", "product_done", "evacuated", "squared", "x_hi", "x_lo",
               "stored_a", "stored_b", "reloaded") as (
            block, weights_a, weights_b, w_hi, w_lo, product_done, evacuated, squared, x_hi, x_lo, stored_a, stored_b,
            reloaded):
        landed = (weights_a, weights_b)
        stored = (stored_a, stored_b)

        def rounds(eng, body):
            for s in range(2):
                body(0, s)
            if pairs > 2:
                with eng.Fori(1, pairs - 1) as i:
                    for s in range(2):
                        body(i, s)
            for j in range(2 * pairs - 2, tiles):
                body(j // 2, j % 2)

        def start(i):
            return isinstance(i, int) and i == 0

        @block.sync
        def _(sp):
            def load(i, s):
                if not start(i):
                    sp.wait_ge(w_lo, 2 * i + s - 1)
                sp.dma_start(raw[:, s].rearrange("p k f -> p (k f)"), w[2 * i + s]).then_inc(landed[s], 16)
            rounds(sp, load)
            if reload is not None:
                sp.dma_start(reload[0], reload[1].rearrange("k p t -> p k t")).then_inc(reloaded, 16)
                sp.wait_ge(reloaded, 16)

        @block.gpsimd
        def _(pool):
            def low(i, s):
                pool.wait_ge(w_hi, 2 * i + s + 1)
                pool.tensor_tensor(ws.lo[:, s], raw[:, s], ws.hi[:, s].bitcast(F32), ALU.subtract).then_inc(w_lo, 1)
            rounds(pool, low)

        @block.tensor
        def _(pe):
            def product(i, s):
                pe.wait_ge(w_lo, 2 * i + s + 1)
                if not start(i):
                    pe.wait_ge(evacuated, 2 * i + s - 1)
                for k in range(kc):
                    first, last = k == 0, k == kc - 1
                    hi, lo, x = ws.hi[:, s, k], ws.lo[:, s, k], src[:, k]
                    for h, bank in enumerate(halves(ps[:, s])):
                        pe.matmul(bank, hi, halves(x.hi)[h], start=first, stop=False)
                        pe.matmul(bank, hi, halves(x.lo)[h], start=False, stop=False)
                    for h, bank in enumerate(halves(ps[:, s])):
                        mm = pe.matmul(bank, lo, halves(x.hi)[h], start=False, stop=last)
                mm.then_inc(product_done, 1)
            rounds(pe, product)

        @block.scalar
        def _(act):
            def high(i, s):
                act.wait_ge(landed[s], 16 * i + 16)
                if not start(i):
                    act.wait_ge(product_done, 2 * i + s - 1)
                act.activation(ws.hi[:, s], raw[:, s], ACT.Copy).then_inc(w_hi, 1)

            def finish_tile(i, s):
                j = 2 * i + s
                if finish == "store" or finish == "keep":
                    act.wait_ge(product_done, j + 1)
                    if finish == "store" and not start(i):
                        act.wait_ge(stored[s], 16 * i)
                    to = tmp[:, s] if finish == "store" else dst[:, j]
                    if bias is None:
                        act.activation(to, ps[:, s], func or ACT.Copy).then_inc(evacuated, 1)
                    else:
                        act.activation(to, ps[:, s], func or ACT.Identity,
                                       bias=bias[:, bass.ds(j, 1)]).then_inc(evacuated, 1)
                if finish == "relu2":
                    act.wait_ge(product_done, j + 1)
                    if not start(i):
                        act.wait_ge(x_lo, j - 1)
                    act.activation(tmp[:, s], ps[:, s], ACT.Relu).then_inc(evacuated, 1)

            def tile(i, s):
                finish_tile(i, s)
                if not (isinstance(i, int) and 2 * i + s + 2 >= tiles):
                    high(i + 1, s)
                if finish == "store":
                    act.wait_ge(evacuated, 2 * i + s + 1)
                    act.dma_start(out[2 * i + s + tile0], tmp[:, s]).then_inc(stored[s], 16)

            high(0, 0)
            high(0, 1)
            rounds(act, tile)
            if finish == "store":
                act.wait_ge(stored[0], 16 * ((tiles + 1) // 2))
                act.wait_ge(stored[1], 16 * (tiles // 2))

        if finish == "add":
            @block.vector
            def _(dve):
                def add(i, s):
                    dve.wait_ge(product_done, 2 * i + s + 1)
                    dve.tensor_tensor(dst[:, 2 * i + s], ps[:, s], dst[:, 2 * i + s], ALU.add).then_inc(evacuated, 1)
                rounds(dve, add)

        if finish == "relu2":
            @block.vector
            def _(dve):
                def square(i, s):
                    j = 2 * i + s
                    dve.wait_ge(evacuated, j + 1)
                    dve.tensor_tensor(tmp[:, s], tmp[:, s], tmp[:, s], ALU.mult).then_inc(squared, 1)
                    dve.wait_ge(squared, j + 1)
                    dve.tensor_copy(dst.hi[:, j], tmp[:, s]).then_inc(x_hi, 1)
                    dve.wait_ge(x_hi, j + 1)
                    dve.tensor_tensor(dst.lo[:, j], tmp[:, s], dst.hi[:, j].bitcast(F32), ALU.subtract).then_inc(x_lo, 1)
                rounds(dve, square)


def rows_phase(nc, m, src, kc, w, width, tiles, out):
    split = isinstance(src, Split)
    wt = m.take(kc, width)
    ws = m.take_split("w", kc, width) if split else None
    res = m.take(tiles, width)
    with phase(nc, "weights_in", "w_hi", "w_lo", "rows_done", "rows_kept", "rows_out") as (
            block, weights_in, w_hi, w_lo, rows_done, rows_kept, rows_out):

        @block.sync
        def _(sp):
            sp.dma_start(wt, w).then_inc(weights_in, 16)
            sp.wait_ge(rows_kept, tiles)
            sp.dma_start(out.rearrange("i p f -> p i f"), res).then_inc(rows_out, 16)
            sp.wait_ge(rows_out, 16)

        @block.tensor
        def _(pe):
            pe.wait_ge(weights_in, 16)
            if split:
                pe.wait_ge(w_lo, kc)
            for i in range(tiles):
                if i >= 4:
                    pe.wait_ge(rows_kept, i - 3)
                bank = m.ps[:, i % 4, 0:width]
                for k in range(kc):
                    first, last = k == 0, k == kc - 1
                    x = src[:, k, i * P:(i + 1) * P]
                    if split:
                        mm = three_passes(pe, bank, x, ws[:, k], first, last)
                    else:
                        mm = pe.matmul(bank, x, wt[:, k], start=first, stop=last)
                mm.then_inc(rows_done, 1)

        @block.vector
        def _(dve):
            if split:
                for k in range(kc):
                    dve.wait_ge(w_hi, k + 1)
                    dve.tensor_tensor(ws.lo[:, k], wt[:, k], ws.hi[:, k].bitcast(F32), ALU.subtract).then_inc(w_lo, 1)

        @block.scalar
        def _(act):
            if split:
                act.wait_ge(weights_in, 16)
                for k in range(kc):
                    act.activation(ws.hi[:, k], wt[:, k], ACT.Copy).then_inc(w_hi, 1)
            for i in range(tiles):
                act.wait_ge(rows_done, i + 1)
                act.activation(res[:, i], m.ps[:, i % 4, 0:width], ACT.Copy).then_inc(rows_kept, 1)


def stick_phase(nc, m, d):
    m.clear(end=A_ACT)
    q, k, v = m.take(S), m.take(S), m.take(NB, P)
    soft, sp_, lsg, aw = m.take(3, HALF), m.take(4, HALF), m.take(3, HALF), m.take(3, HALF)
    steps = []
    for g in range(2):
        for kb in range(4 * g + 3, -1, -1):
            for e in range(2):
                steps.append((e, g, kb, P * max(0, kb - 4 * g)))
    T = len(steps)
    pairs = SB_H // 2
    carried = np.cumsum([kb > 0 for _, _, kb, _ in steps]).tolist()
    ended = np.cumsum([kb == 0 for _, _, kb, _ in steps]).tolist()
    masked = np.cumsum([kb >= 4 * g for _, g, kb, _ in steps]).tolist()
    fixes = masked[-1]

    def diag(t):
        return steps[t][2] >= 4 * steps[t][1]

    with phase(nc, "staged", "q_scaled", "z_done", "abs_done", "exp_done", "ln_done", "raw_done", "sp_ready",
               "lsg_ready", "later_done", "arg_ready", "carry_done", "a_ready", "av_done", "o_kept") as (
            block, staged, q_scaled, z_done, abs_done, exp_done, ln_done, raw_done, sp_ready,
            lsg_ready, later_done, arg_ready, carry_done, a_ready, av_done, o_kept):

        @block.sync
        def _(sp):
            def body(i):
                sp.wait_ge(z_done, i * T)
                sp.wait_ge(av_done, i * T)
                sp.dma_start(q, d["in1"][i]).then_inc(staged, 16)
                sp.dma_start(k, d["in1"][i + pairs]).then_inc(staged, 16)
                sp.dma_start(v, d["v_sb"][:, :, bass.ds(i * P, P)].rearrange("b p f -> p b f")).then_inc(staged, 16)
            loop(sp, pairs, body)

        @block.tensor
        def _(pe):
            def body(i):
                b = i * T
                pe.wait_ge(staged, 48 * i + 48)
                pe.wait_ge(q_scaled, i + 1)
                for t in range(T + 4):
                    if t < T:
                        e, g, kb, c0 = steps[t]
                        pe.wait_ge(lsg_ready, b + max(t - 2, 0))
                        pe.matmul(m.ps[:, t % 3, c0:HALF], k[64 * e:64 * e + 64, kb * P:(kb + 1) * P],
                                  q[64 * e:64 * e + 64, g * HALF + c0:(g + 1) * HALF],
                                  start=True, stop=True).then_inc(z_done, 1)
                    if 0 <= t - 2 < T:
                        e, g, kb, c0 = steps[t - 2]
                        pe.wait_ge(sp_ready, b + t - 1)
                        pe.wait_ge(arg_ready, b + max(t - 3, 0))
                        pe.matmul(m.ps[:, 3 + e, c0:HALF], m.c(C_GT), sp_[:, (t - 2) % 4, c0:HALF],
                                  start=(kb == 4 * g + 3), stop=False, skip_group_check=True).then_inc(later_done, 1)
                    if 0 <= t - 3 < T and steps[t - 3][2] > 0:
                        e, g, kb, c0 = steps[t - 3]
                        pe.wait_ge(arg_ready, b + t - 2)
                        pe.matmul(m.ps[:, 3 + e, c0:HALF], m.c(C_LE), sp_[:, (t - 3) % 4, c0:HALF],
                                  start=False, stop=False, skip_group_check=True).then_inc(carry_done, 1)
                    if 0 <= t - 4 < T:
                        e, g, kb, c0 = steps[t - 4]
                        pe.wait_ge(a_ready, b + t - 3)
                        if kb == 4 * g + 3:
                            pe.wait_ge(o_kept, i * 4 + (2 * g - 2 + e + 1 if g else 0))
                        mm = pe.matmul(m.ps[64 * e:64 * e + 64, 5 + e, c0:HALF], v[:, kb, 64 * e:64 * e + 64],
                                       aw[:, (t - 4) % 3, c0:HALF], start=(kb == 4 * g + 3), stop=(kb == 0),
                                       skip_group_check=True)
                        mm.then_inc(av_done, 1)
            loop(pe, pairs, body)

        @block.scalar
        def _(act):
            act.preload_act_table_set(LN_EXP)

            def body(i):
                b = i * T
                act.wait_ge(staged, 48 * i + 48)
                act.activation(q, q, ACT.Copy, scale=float(SB_D ** -0.5)).then_inc(q_scaled, 1)
                for t in range(T + 2):
                    if t < T:
                        c0 = steps[t][3]
                        x = soft[:, t % 3, c0:HALF]
                        act.wait_ge(z_done, b + t + 1)
                        act.activation(x, m.ps[:, t % 3, c0:HALF], ACT.Abs).then_inc(abs_done, 1)
                        act.wait_ge(abs_done, b + t + 1)
                        act.activation(x, x, ACT.Exp, scale=-1.0).then_inc(exp_done, 1)
                        act.wait_ge(exp_done, b + t + 1)
                        act.activation(x, x, ACT.Ln, bias=1.0).then_inc(ln_done, 1)
                    if 0 <= t - 2 < T:
                        c0 = steps[t - 2][3]
                        act.wait_ge(arg_ready, b + t - 1)
                        act.wait_ge(av_done, b + max(t - 4, 0))
                        act.activation(aw[:, (t - 2) % 3, c0:HALF], lsg[:, (t - 2) % 3, c0:HALF],
                                       ACT.Exp).then_inc(a_ready, 1)
            loop(act, pairs, body)

        @block.vector
        def _(dve):
            def body(i):
                b = i * T
                for t in range(T + 6):
                    if 0 <= t - 1 < T:
                        u = t - 1
                        c0 = steps[u][3]
                        z = m.ps[:, u % 3, c0:HALF]
                        ln = soft[:, u % 3, c0:HALF]
                        dve.wait_ge(ln_done, b + u + 1)
                        dve.wait_ge(later_done, b + max(u - 3, 0))
                        dve.wait_ge(carry_done, i * carried[-1] + (carried[u - 4] if u >= 4 else 0))
                        dve.wait_ge(a_ready, b + max(u - 2, 0))
                        one = dve.scalar_tensor_tensor(sp_[:, u % 4, c0:HALF], z, 0.0, ln, ALU.max, ALU.add)
                        one.then_inc(raw_done if diag(u) else sp_ready, 1)
                        two = dve.scalar_tensor_tensor(lsg[:, u % 3, c0:HALF], z, 0.0, ln, ALU.min, ALU.subtract)
                        two.then_inc(raw_done if diag(u) else lsg_ready, 1)
                        if diag(u):
                            own = slice(c0, c0 + P)
                            dve.wait_ge(raw_done, i * 2 * fixes + 2 * masked[u])
                            dve.tensor_tensor(sp_[:, u % 4, own], sp_[:, u % 4, own], m.c(C_LT),
                                              ALU.mult).then_inc(sp_ready, 1)
                            dve.tensor_tensor(lsg[:, u % 3, own], lsg[:, u % 3, own], m.c(C_NGE),
                                              ALU.add).then_inc(lsg_ready, 1)
                    if 0 <= t - 2 < T:
                        u = t - 2
                        e, g, kb, c0 = steps[u]
                        dve.wait_ge(later_done, b + u + 1)
                        dve.wait_ge(lsg_ready, b + u + 1)
                        x = lsg[:, u % 3, c0:HALF]
                        dve.tensor_tensor(x, x, m.ps[:, 3 + e, c0:HALF], ALU.subtract).then_inc(arg_ready, 1)
                    if 0 <= t - 5 < T and steps[t - 5][2] == 0:
                        e, g, kb, c0 = steps[t - 5]
                        dve.wait_ge(av_done, b + t - 4)
                        rows = slice(64 * e, 64 * e + 64)
                        dve.tensor_copy(m.act[rows, i, g * HALF:(g + 1) * HALF], m.ps[rows, 5 + e, :]).then_inc(o_kept, 1)
            loop(dve, pairs, body)


def rope_phase(nc, m, plain, swapped, tab, tiles, out, rows):
    res = m.take(tiles, S)
    t1 = m.take(tiles, S)
    with phase(nc, "cos_done", "sin_done", "turned", "rope_out") as (block, cos_done, sin_done, turned, rope_out):

        @block.vector
        def _(dve):
            for j in range(tiles):
                dve.tensor_tensor(res[:, j], plain[:, j], tab[:, 0], ALU.mult).then_inc(cos_done, 1)
                dve.tensor_tensor(t1[:, j], swapped[:, j], tab[:, 1], ALU.mult).then_inc(sin_done, 1)
                dve.wait_ge(cos_done, j + 1)
                dve.wait_ge(sin_done, j + 1)
                dve.tensor_tensor(res[:, j], res[:, j], t1[:, j], ALU.add).then_inc(turned, 1)

        @block.sync
        def _(sp):
            for j in range(tiles):
                sp.wait_ge(turned, j + 1)
                sp.dma_start(out[j * P:j * P + rows], res[0:rows, j]).then_inc(rope_out, 16)
            sp.wait_ge(rope_out, 16 * tiles)


def latent_phases(nc, m, d):
    m.clear(end=A_ACT)
    low = m.take(5, S)
    normed = m.take_split("low", 3, S)
    tab = m.take(2, S)
    scratch = (m.take(2, S), m.take(S))
    with phase(nc, "low_in") as (block, low_in):
        @block.sync
        def _(sp):
            sp.dma_start(low, d["in1"][8:13].rearrange("a p t -> p a t")).then_inc(low_in, 16)
            sp.dma_start(tab, d["rope"].rearrange("a p t -> p a t")).then_inc(low_in, 16)
            sp.wait_ge(low_in, 32)
    norm_phase(nc, m, low[:, 0:2], normed[:, 0:2], m.p("q_a_g", 0, 2), 2, scratch)
    norm_phase(nc, m, low[:, 2:3], normed[:, 2:3], m.p("kv_a_g", 0, 1), 1, scratch)
    base = m.top
    rope_phase(nc, m, low[:, 3:4], low[:, 4:5], tab, 1, d["k_rope"], ROPE)
    m.top = base
    gemm_phase(nc, m, d["w_qn"], normed[:, 0:2], 2, 4, "store", out=d["mla_q"])
    m.top = base
    qr = m.take(4, S)
    gemm_phase(nc, m, d["w_qr"], normed[:, 0:2], 2, 4, "keep", dst=qr)
    rope_phase(nc, m, qr[:, 0:2], qr[:, 2:4], tab, 2, d["q_rope"], P)
    m.top = base
    gemm_phase(nc, m, d["w_kn"], normed[:, 2:3], 1, 4, "store", out=d["mla_k"])
    m.top = base
    rows_phase(nc, m, normed[:, 2:3], 1, d["w_vm"], BW, NB, d["mla_v"])


def latent_attention_phase(nc, m, d):
    m.clear(end=A_ACT)
    qn, kn, v = m.take(S), m.take(S), m.take(NB, P)
    qr, kr = m.take(S), m.take(S)
    pr = m.take(2, S)
    pt = m.take(2, S)
    mx, nm, rs, ri = m.take(NB), m.take(NB), m.take(NB), m.take(NB)
    T = NB

    def scores(t):
        return m.ps[:, 2 * (t % 2):2 * (t % 2) + 2, :].rearrange("p a f -> p (a f)")
    turned = m.ps[:, 4:6, :].rearrange("p a f -> p (a f)")

    with phase(nc, "staged", "s_done", "diag_masked", "max_done", "negated", "p_ready", "inverted", "p_scaled",
               "t_done", "t_kept", "o_done", "o_kept") as (
            block, staged, s_done, diag_masked, max_done, negated, p_ready, inverted, p_scaled,
            t_done, t_kept, o_done, o_kept):

        @block.sync
        def _(sp):
            sp.dma_start(kr[0:ROPE], d["k_rope"]).then_inc(staged, 16)
            def body(i):
                sp.wait_ge(o_done, i * T)
                sp.dma_start(qn, d["mla_q"][i]).then_inc(staged, 16)
                sp.dma_start(kn, d["mla_k"][i]).then_inc(staged, 16)
                sp.dma_start(qr[0:ROPE], d["q_rope"][bass.ds(i * ROPE, ROPE)]).then_inc(staged, 16)
                sp.dma_start(v, d["mla_v"][:, :, bass.ds(i * P, P)].rearrange("b p f -> p b f")).then_inc(staged, 16)
            loop(sp, MLA_H, body)

        @block.tensor
        def _(pe):
            def body(i):
                b = i * T
                pe.wait_ge(staged, 64 * i + 80)
                for t in range(T + 2):
                    if t < T:
                        pe.wait_ge(p_ready, b + max(t - 1, 0))
                        n = (t + 1) * P
                        for c in range(0, n, HALF):
                            w = min(HALF, n - c)
                            pe.matmul(scores(t)[:, c:c + w], qn[:, t * P:(t + 1) * P], kn[:, c:c + w],
                                      start=True, stop=False)
                            mm = pe.matmul(scores(t)[:, c:c + w], qr[0:ROPE, t * P:(t + 1) * P], kr[0:ROPE, c:c + w],
                                           start=False, stop=True)
                        mm.then_inc(s_done, 1)
                    if 0 <= t - 1 < T:
                        u = t - 1
                        pe.wait_ge(p_scaled, b + u + 1)
                        pe.wait_ge(t_kept, b + u)
                        for kb in range(u + 1):
                            mm = pe.transpose(turned[:, kb * P:(kb + 1) * P], pr[:, u % 2, kb * P:(kb + 1) * P],
                                              m.c(C_ID))
                        mm.then_inc(t_done, 1)
                    if 0 <= t - 2 < T:
                        u = t - 2
                        pe.wait_ge(t_kept, b + u + 1)
                        pe.wait_ge(o_kept, b + max(u - 1, 0))
                        for kb in range(u + 1):
                            mm = pe.matmul(m.ps[:, 6 + u % 2, 0:P], v[:, kb], pt[:, u % 2, kb * P:(kb + 1) * P],
                                           start=(kb == 0), stop=(kb == u))
                        mm.then_inc(o_done, 1)
            loop(pe, MLA_H, body)

        @block.vector
        def _(dve):
            def body(i):
                b = i * T
                for t in range(T + 3):
                    if t < T:
                        dve.wait_ge(s_done, b + t + 1)
                        own = scores(t)[:, t * P:(t + 1) * P]
                        dve.tensor_tensor(own, own, m.c(C_NCAUSAL), ALU.add).then_inc(diag_masked, 1)
                        dve.wait_ge(diag_masked, b + t + 1)
                        dve.wait_ge(negated, b + t)
                        dve.tensor_reduce(mx[:, t:t + 1], scores(t)[:, 0:(t + 1) * P], AX.X, ALU.max).then_inc(max_done, 1)
                        dve.wait_ge(max_done, b + t + 1)
                        dve.wait_ge(p_ready, b + t)
                        dve.tensor_scalar(nm[:, t:t + 1], mx[:, t:t + 1], -MLA_SCALE, None, ALU.mult).then_inc(negated, 1)
                    if 0 <= t - 1 < T:
                        u = t - 1
                        dve.wait_ge(p_ready, b + u + 1)
                        dve.wait_ge(p_scaled, b + u)
                        dve.reciprocal(ri[:, u:u + 1], rs[:, u:u + 1]).then_inc(inverted, 1)
                        dve.wait_ge(inverted, b + u + 1)
                        x = pr[:, u % 2, 0:(u + 1) * P]
                        dve.tensor_scalar(x, x, ri[:, u:u + 1], None, ALU.mult).then_inc(p_scaled, 1)
                    if 0 <= t - 3 < T:
                        u = t - 3
                        dve.wait_ge(o_done, b + u + 1)
                        dve.tensor_copy(m.act[:, 4 + i, u * P:(u + 1) * P], m.ps[:, 6 + u % 2, 0:P]).then_inc(o_kept, 1)
            loop(dve, MLA_H, body)

        @block.scalar
        def _(act):
            def body(i):
                b = i * T
                for t in range(T + 1):
                    if t < T:
                        act.wait_ge(negated, b + t + 1)
                        act.wait_ge(t_done, b + max(t - 1, 0))
                        n = (t + 1) * P
                        act.wait_ge(inverted, b + max(t - 1, 0))
                        act.activation(pr[:, t % 2, 0:n], scores(t)[:, 0:n], ACT.Exp, bias=nm[:, t:t + 1],
                                       scale=MLA_SCALE, accum_out=rs[:, t:t + 1]).then_inc(p_ready, 1)
                    if 0 <= t - 1 < T:
                        u = t - 1
                        act.wait_ge(t_done, b + u + 1)
                        act.wait_ge(o_done, b + max(u - 1, 0))
                        act.activation(pt[:, u % 2, 0:(u + 1) * P], turned[:, 0:(u + 1) * P], ACT.Copy).then_inc(t_kept, 1)
            loop(act, MLA_H, body)


def small_phase(nc, m, d):
    m.clear()
    n = NB * 4
    ab = m.take(NB, 8)
    x, e, w, w2, acc, ea = (m.take(n + 4) for _ in range(6))
    ones8 = (1, NB, 4)
    with phase(nc, "ab_in", "biased", "sig_done", "abs_done", "exp_done", "alog_done", "chain") as (
            block, ab_in, biased, sig_done, abs_done, exp_done, alog_done, chain):

        @block.sync
        def _(sp):
            sp.dma_start(ab, d["ab"].rearrange("c p f -> p c f")).then_inc(ab_in, 16)
            sp.wait_ge(ab_in, 16)

        @block.scalar
        def _(act):
            act.wait_ge(biased, 1)
            act.activation(m.beta, ab[:, :, 0:4], ACT.Sigmoid).then_inc(sig_done, 1)
            act.activation(ea[:, 0:4], m.p("a_log", 0, 4), ACT.Exp).then_inc(alog_done, 1)
            act.wait_ge(biased, 3)
            act.activation(e, x, ACT.Abs).then_inc(abs_done, 1)
            act.wait_ge(abs_done, 1)
            act.activation(e, e, ACT.Exp, scale=-1.0).then_inc(exp_done, 1)

        @block.vector
        def _(dve):
            count = [0]

            def step(ins):
                count[0] += 1
                ins.then_inc(chain, 1)
                dve.wait_ge(chain, count[0])

            dve.wait_ge(ab_in, 16)
            dve.tensor_tensor(ab, ab, m.p("ab_bias", 0, 8).unsqueeze(1).to_broadcast([P, NB, 8]),
                              ALU.add).then_inc(biased, 1)
            dve.wait_ge(biased, 1)
            dve.tensor_tensor(x[:, 0:n].rearrange("p (c h) -> p c h", h=4), ab[:, :, 4:8],
                              m.p("a_dt", 0, 4).unsqueeze(1).to_broadcast([P, NB, 4]), ALU.add).then_inc(biased, 1)
            dve.tensor_scalar(x[:, n:n + 4], m.p("d_lam", 0, 4), -1.0, None, ALU.mult).then_inc(biased, 1)
            dve.wait_ge(exp_done, 1)
            step(dve.tensor_scalar(w, e, 2.0, None, ALU.add))
            step(dve.reciprocal(w, w))
            step(dve.tensor_tensor(w, w, e, ALU.mult))
            step(dve.tensor_tensor(w2, w, w, ALU.mult))
            step(dve.tensor_scalar(acc, w2, 1 / 17, 1 / 15, ALU.mult, ALU.add))
            for k in range(13, 0, -2):
                step(dve.tensor_tensor(acc, acc, w2, ALU.mult))
                step(dve.tensor_scalar(acc, acc, 1 / k, None, ALU.add))
            step(dve.scalar_tensor_tensor(acc, acc, 2.0, w, ALU.mult, ALU.mult))
            step(dve.scalar_tensor_tensor(acc, x, 0.0, acc, ALU.max, ALU.add))
            step(dve.tensor_scalar(m.rate, acc[:, n:n + 4], 8.0, None, ALU.mult))
            dve.wait_ge(alog_done, 1)
            step(dve.scalar_tensor_tensor(m.decay, acc[:, 0:n].rearrange("p (c h) -> p c h", h=4), -1.0,
                                          ea[:, 0:4].unsqueeze(1).to_broadcast([P, NB, 4]), ALU.mult, ALU.mult))


def conv(dve, x, acc, taps, n_taps, bias, chain, count):
    for k in range(n_taps):
        if k == 0 and bias is None:
            ins = dve.tensor_scalar(acc, x[:, 0:S], taps[:, 0:1], None, ALU.mult)
        elif k == 0:
            ins = dve.tensor_scalar(acc, x[:, 0:S], taps[:, 0:1], bias, ALU.mult, ALU.add)
        else:
            dve.wait_ge(chain, count + k)
            ins = dve.scalar_tensor_tensor(acc, x[:, k:k + S], taps[:, k:k + 1], acc, ALU.mult, ALU.add)
        ins.then_inc(chain, 1)


def delta_conv_phase(nc, m, d):
    m.clear()
    pad = CONVK - 1
    tiles = 3 * BT
    x = m.take(2, S + 4)
    y = m.take(tiles, S)
    sq, root = m.take(2, S), m.take(2, S)
    ps = m.ps[:, 0:4, :].rearrange("p (s h) f -> p s (h f)", s=2)
    with phase(nc, "zeroed", "x_a", "x_b", "conv_chain", "silu_done", "squared", "summed", "logged", "rooted",
               "normed", "all_out") as (
            block, zeroed, x_a, x_b, conv_chain, silu_done, squared, summed, logged, rooted, normed, all_out):
        x_in = (x_a, x_b)

        @block.sync
        def _(sp):
            sp.wait_ge(zeroed, 2)
            for j in range(tiles):
                if j >= 2:
                    sp.wait_ge(conv_chain, (j - 1) * CONVK)
                sp.dma_start(x[:, j % 2, pad:pad + S], d["in2"][T_AQKV + j]).then_inc(x_in[j % 2], 16)
            sp.wait_ge(silu_done, tiles)
            sp.dma_start(d["delta"][2 * BT:tiles].rearrange("c p t -> p c t"), y[:, 2 * BT:tiles]).then_inc(all_out, 16)
            sp.wait_ge(normed, 2 * BT)
            sp.dma_start(d["delta"][0:2 * BT].rearrange("c p t -> p c t"), y[:, 0:2 * BT]).then_inc(all_out, 16)
            sp.wait_ge(all_out, 32)

        @block.vector
        def _(dve):
            for s in range(2):
                dve.memset(x[:, s, 0:pad], 0.0).then_inc(zeroed, 1)

            def norm(j):
                dve.wait_ge(rooted, j + 1)
                dve.scalar_tensor_tensor(y[:, j], y[:, j], m.c(C_QS + j, 1), root[:, j % 2], ALU.mult,
                                         ALU.mult).then_inc(normed, 1)
            for j in range(tiles):
                dve.wait_ge(x_in[j % 2], 16 * (j // 2) + 16)
                conv(dve, x[:, j % 2], y[:, j], m.p("a_conv", j * CONVK, CONVK), CONVK, None, conv_chain, j * CONVK)
                if 3 <= j < 3 + 2 * BT:
                    norm(j - 3)

        @block.scalar
        def _(act):
            act.preload_act_table_set(LN_EXP)

            def root_of(j):
                act.wait_ge(summed, j + 1)
                if j >= 2:
                    act.wait_ge(normed, j - 1)
                act.activation(root[:, j % 2], ps[:, j % 2], ACT.Ln, bias=m.c(C_EPS, 1)).then_inc(logged, 1)
                act.wait_ge(logged, j + 1)
                act.activation(root[:, j % 2], root[:, j % 2], ACT.Exp, scale=-0.5).then_inc(rooted, 1)
            for j in range(tiles):
                act.wait_ge(conv_chain, (j + 1) * CONVK)
                act.activation(y[:, j], y[:, j], ACT.Silu).then_inc(silu_done, 1)
                if j < 2 * BT:
                    act.wait_ge(silu_done, j + 1)
                    if j >= 2:
                        act.wait_ge(summed, j - 1)
                    act.activation(sq[:, j % 2], y[:, j], ACT.Square).then_inc(squared, 1)
                if 1 <= j < 1 + 2 * BT:
                    root_of(j - 1)

        @block.tensor
        def _(pe):
            for j in range(2 * BT):
                pe.wait_ge(squared, j + 1)
                if j >= 2:
                    pe.wait_ge(logged, j - 1)
                for h in range(2):
                    mm = pe.matmul(ps[:, j % 2, h * HALF:(h + 1) * HALF], m.c(C_ONE),
                                   sq[:, j % 2, h * HALF:(h + 1) * HALF], start=True, stop=True)
                mm.then_inc(summed, 1)


def heads(v):
    return v.rearrange("p (h f) -> p h f", h=4)


def wide(column):
    return column.unsqueeze(2).to_broadcast([P, 4, P])


def over_heads(square):
    return square.unsqueeze(1).to_broadcast([P, 4, P])


def delta_prepare_phase(nc, m, d, at, attn, qd, last):
    base = m.top
    st = m.take(3 * BT, P)
    gw, bw, gd, lt, eg = (m.take(BW) for _ in range(5))
    rows = m.take(3, BW)
    gc, egc, kx, bg = (m.take(4) for _ in range(4))
    bank = [m.ps[:, n, :] for n in range(8)]
    with phase(nc, "staged", "spread_g", "spread_b", "sums_done", "rows_done", "products_done", "picked", "g_col",
               "diff_done", "clamped", "l_exp", "l_masked", "eg_done", "egc_done", "kx_diff", "kx_done", "bg_done",
               "a_half", "a_done", "attn_done", "qd_done", "last_done", "k1", "k2", "v1", "rows_out") as (
            block, staged, spread_g, spread_b, sums_done, rows_done, products_done, picked, g_col,
            diff_done, clamped, l_exp, l_masked, eg_done, egc_done, kx_diff, kx_done, bg_done,
            a_half, a_done, attn_done, qd_done, last_done, k1, k2, v1, rows_out):

        @block.sync
        def _(sp):
            def body(c):
                sp.wait_ge(products_done, c)
                sp.wait_ge(rows_done, c)
                sp.wait_ge(qd_done, c)
                sp.dma_start(st, d["delta"][:, :, bass.ds(c * P, P)].rearrange("a p t -> p a t")).then_inc(staged, 16)
                sp.wait_ge(k1, c + 1)
                sp.wait_ge(k2, c + 1)
                sp.wait_ge(v1, c + 1)
                sp.dma_start(d["kv_rows"][c], rows.rearrange("p a f -> p (a f)")).then_inc(rows_out, 16)
            loop(sp, NB, body)
            sp.wait_ge(rows_out, 16 * NB)

        @block.tensor
        def _(pe):
            def body(c):
                pe.wait_ge(spread_g, c + 1)
                pe.wait_ge(eg_done, c)
                pe.wait_ge(diff_done, c)
                pe.wait_ge(last_done, c)
                pe.wait_ge(kx_diff, c)
                for h in range(4):
                    pe.matmul(bank[2][:, h * P:(h + 1) * P], heads(gw)[:, h], m.c(C_LE), start=True, stop=True)
                pe.wait_ge(spread_b, c + 1)
                pe.wait_ge(a_done, c)
                for h in range(4):
                    mm = pe.matmul(bank[3][:, h * P:(h + 1) * P], heads(bw)[:, h], m.c(C_ID), start=True, stop=True)
                mm.then_inc(sums_done, 1)
                pe.wait_ge(staged, 16 * c + 16)
                pe.wait_ge(k1, c)
                pe.wait_ge(k2, c)
                pe.wait_ge(v1, c)
                for h in range(4):
                    pe.transpose(bank[0][:, h * P:(h + 1) * P], st[:, BT + h], m.c(C_ID))
                for h in range(4):
                    mm = pe.transpose(bank[1][:, h * P:(h + 1) * P], st[:, 2 * BT + h], m.c(C_ID))
                mm.then_inc(rows_done, 1)
                pe.wait_ge(attn_done, c)
                for h in range(4):
                    pe.matmul(bank[4][:, h * P:(h + 1) * P], st[:, BT + h], st[:, BT + h], start=True, stop=True)
                for h in range(4):
                    mm = pe.matmul(bank[5][:, h * P:(h + 1) * P], st[:, BT + h], st[:, h], start=True, stop=True)
                mm.then_inc(products_done, 1)
            loop(pe, NB, body)

        @block.vector
        def _(dve):
            def body(c):
                dve.wait_ge(sums_done, c)
                dve.tensor_tensor(heads(gw), over_heads(m.c(C_ONE)), wide(m.decay[:, c]), ALU.mult).then_inc(spread_g, 1)
                dve.tensor_tensor(heads(bw), over_heads(m.c(C_ONE)), wide(m.beta[:, c]), ALU.mult).then_inc(spread_b, 1)
                dve.wait_ge(sums_done, c + 1)
                dve.tensor_tensor(heads(gd), heads(bank[2]), over_heads(m.c(C_ID)), ALU.mult).then_inc(picked, 1)
                dve.wait_ge(picked, c + 1)
                dve.wait_ge(egc_done, c)
                dve.tensor_reduce(gc, heads(gd), AX.X, ALU.add).then_inc(g_col, 1)
                dve.wait_ge(g_col, c + 1)
                dve.tensor_tensor(heads(lt), heads(bank[2]), wide(gc), ALU.subtract).then_inc(diff_done, 1)
                g_last = heads(bank[2])[:, :, P - 1]
                dve.wait_ge(kx_done, c)
                dve.tensor_tensor(kx, g_last, gc, ALU.subtract).then_inc(kx_diff, 1)
                dve.wait_ge(diff_done, c + 1)
                dve.tensor_scalar(lt, lt, 0.0, None, ALU.min).then_inc(clamped, 1)
                dve.wait_ge(eg_done, c + 1)
                dve.tensor_copy(last[:, c], heads(eg)[:, :, P - 1]).then_inc(last_done, 1)
                dve.wait_ge(egc_done, c + 1)
                dve.wait_ge(k1, c)
                dve.tensor_tensor(bg, egc, m.beta[:, c], ALU.mult).then_inc(bg_done, 1)
                dve.wait_ge(l_exp, c + 1)
                dve.tensor_tensor(heads(lt), heads(lt), over_heads(m.c(C_LE)), ALU.mult).then_inc(l_masked, 1)
                dve.wait_ge(l_masked, c + 1)
                dve.wait_ge(products_done, c + 1)
                dve.tensor_tensor(at[:, c], bank[4], lt, ALU.mult).then_inc(a_half, 1)
                dve.tensor_tensor(attn[:, c], bank[5], lt, ALU.mult).then_inc(attn_done, 1)
                dve.wait_ge(a_half, c + 1)
                dve.tensor_tensor(at[:, c], at[:, c], bank[3], ALU.mult).then_inc(a_done, 1)
                dve.tensor_tensor(heads(qd[:, c]), st[:, 0:BT], heads(eg), ALU.mult).then_inc(qd_done, 1)
                dve.wait_ge(rows_out, 16 * c)
                dve.wait_ge(bg_done, c + 1)
                dve.wait_ge(rows_done, c + 1)
                dve.tensor_tensor(heads(rows[:, 0]), heads(bank[0]), wide(bg), ALU.mult).then_inc(k1, 1)
                dve.wait_ge(kx_done, c + 1)
                dve.tensor_tensor(heads(rows[:, 1]), heads(bank[0]), wide(kx), ALU.mult).then_inc(k2, 1)
                dve.tensor_tensor(heads(rows[:, 2]), heads(bank[1]), wide(m.beta[:, c]), ALU.mult).then_inc(v1, 1)
            loop(dve, NB, body)

        @block.scalar
        def _(act):
            def body(c):
                act.wait_ge(g_col, c + 1)
                act.wait_ge(bg_done, c)
                act.activation(egc, gc, ACT.Exp).then_inc(egc_done, 1)
                act.wait_ge(kx_diff, c + 1)
                act.activation(kx, kx, ACT.Exp).then_inc(kx_done, 1)
                act.wait_ge(diff_done, c + 1)
                act.wait_ge(qd_done, c)
                act.wait_ge(last_done, c)
                act.activation(eg, bank[2], ACT.Exp).then_inc(eg_done, 1)
                act.wait_ge(clamped, c + 1)
                act.activation(lt, lt, ACT.Exp).then_inc(l_exp, 1)
            loop(act, NB, body)
    m.top = base


def delta_inverse_phase(nc, m, at, inv, inv_t):
    base = m.top
    masked = m.take(4, 2 * BW)
    mid = m.take(4, 2 * BW)
    groups = 4

    def pair(v, g):
        return v[:, 2 * g:2 * g + 2].rearrange("p c f -> p (c f)")

    def eight(v):
        return v.rearrange("p (n f) -> p n f", f=P)

    def spread(square):
        return square.unsqueeze(1).to_broadcast([P, 8, P])

    def banks(b):
        return m.ps[:, b:b + 2, :].rearrange("p b f -> p (b f)")

    with phase(nc, "a_masked", "mid_done", "mid_kept", "low_done", "up_done", "low_kept", "up_kept") as (
            block, a_masked, mid_done, mid_kept, low_done, up_done, low_kept, up_kept):

        @block.vector
        def _(dve):
            for g in range(groups):
                dve.tensor_tensor(eight(masked[:, g]), eight(pair(at, g)), spread(m.c(C_LVL)), ALU.mult).then_inc(a_masked, 1)
            for g in range(groups):
                dve.wait_ge(mid_done, g + 1)
                dve.tensor_tensor(eight(pair(inv, g)), spread(m.c(C_ID)), eight(banks(2 * (g % 2))), ALU.subtract).then_inc(low_kept, 1)
                dve.tensor_tensor(eight(pair(inv_t, g)), spread(m.c(C_ID)), eight(masked[:, g]), ALU.subtract).then_inc(up_kept, 1)
            with dve.Fori(1, 7) as lvl:
                b = lvl * groups
                mask = m.const[:, C_LVL:C_LVL + 7 * P].rearrange("p (l f) -> p l f", f=P)[:, lvl]
                for g in range(groups):
                    dve.wait_ge(mid_done, b - groups + g + 1)
                    dve.wait_ge(up_kept, b - groups + g + 1)
                    dve.tensor_tensor(eight(masked[:, g]), eight(pair(at, g)), spread(mask), ALU.mult).then_inc(a_masked, 1)
                for g in range(groups):
                    dve.wait_ge(low_kept, b - groups + g + 1)
                    dve.wait_ge(low_done, b - groups + g + 1)
                    dve.tensor_tensor(pair(inv, g), pair(inv, g), banks(4), ALU.subtract).then_inc(low_kept, 1)
                    dve.wait_ge(up_done, b - groups + g + 1)
                    dve.tensor_tensor(pair(inv_t, g), pair(inv_t, g), banks(6), ALU.subtract).then_inc(up_kept, 1)

        @block.tensor
        def _(pe):
            def first(g, b):
                for n in range(8):
                    right = m.c(C_ID) if b is None else pair(inv, g)[:, n * P:(n + 1) * P]
                    mm = pe.matmul(banks(2 * (g % 2))[:, n * P:(n + 1) * P], masked[:, g, n * P:(n + 1) * P], right,
                                   start=True, stop=True)
                mm.then_inc(mid_done, 1)

            for g in range(groups):
                pe.wait_ge(a_masked, g + 1)
                if g >= 2:
                    pe.wait_ge(low_kept, g - 1)
                first(g, None)
            pe.wait_ge(low_kept, groups)
            with pe.Fori(1, 7) as lvl:
                b = lvl * groups
                for g in range(groups + 1):
                    if g < groups:
                        pe.wait_ge(a_masked, b + g + 1)
                        pe.wait_ge(low_kept, b - groups + g + 1)
                        if g >= 2:
                            pe.wait_ge(mid_kept, b - groups + g - 1)
                        first(g, b)
                    if g >= 1:
                        u = g - 1
                        pe.wait_ge(mid_kept, b - groups + u + 1)
                        pe.wait_ge(up_kept, b - groups + u + 1)
                        pe.wait_ge(low_kept, b + u)
                        for n in range(8):
                            cut = slice(n * P, (n + 1) * P)
                            mm = pe.matmul(banks(4)[:, cut], pair(inv_t, u)[:, cut], mid[:, u, cut], start=True, stop=True)
                        mm.then_inc(low_done, 1)
                        pe.wait_ge(up_kept, b + u)
                        for n in range(8):
                            cut = slice(n * P, (n + 1) * P)
                            mm = pe.matmul(banks(6)[:, cut], mid[:, u, cut], pair(inv_t, u)[:, cut], start=True, stop=True)
                        mm.then_inc(up_done, 1)

        @block.scalar
        def _(act):
            with act.Fori(1, 7) as lvl:
                b = lvl * groups
                for g in range(groups):
                    act.wait_ge(mid_done, b + g + 1)
                    act.activation(mid[:, g], banks(2 * (g % 2)), ACT.Copy).then_inc(mid_kept, 1)
    m.top = base


def delta_scan_phase(nc, m, d, attn, qd, inv_t, last, o):
    base = m.top
    rows = m.take(3, BW)
    tt, nw, vn, state = (m.take(BW) for _ in range(4))
    bank = [m.ps[:, n, :] for n in range(8)]

    def h_(v, h):
        return v[:, h * P:(h + 1) * P]

    with phase(nc, "rows_in", "inv_copied", "w_done", "w_kept", "v_done", "v_kept", "o_done", "kv_done", "o_kept",
               "cleared", "state_ready") as (
            block, rows_in, inv_copied, w_done, w_kept, v_done, v_kept, o_done, kv_done, o_kept, cleared, state_ready):

        @block.sync
        def _(sp):
            def body(c):
                sp.wait_ge(kv_done, c)
                sp.dma_start(rows.rearrange("p a f -> p (a f)"), d["kv_rows"][c]).then_inc(rows_in, 16)
            loop(sp, NB, body)

        @block.scalar
        def _(act):
            def body(c):
                act.wait_ge(v_done, c)
                act.activation(tt, inv_t[:, c], ACT.Copy).then_inc(inv_copied, 1)
                act.wait_ge(w_done, c + 1)
                act.activation(nw, bank[0], ACT.Copy, scale=-1.0).then_inc(w_kept, 1)
                act.wait_ge(v_done, c + 1)
                act.wait_ge(kv_done, c)
                act.activation(vn, bank[1], ACT.Copy).then_inc(v_kept, 1)
            loop(act, NB, body)

        @block.tensor
        def _(pe):
            def body(c):
                pe.wait_ge(rows_in, 16 * c + 16)
                pe.wait_ge(inv_copied, c + 1)
                pe.wait_ge(w_kept, c)
                for h in range(4):
                    mm = pe.matmul(h_(bank[0], h), h_(rows[:, 0], h), h_(tt, h), start=True, stop=True)
                mm.then_inc(w_done, 1)
                pe.wait_ge(w_kept, c + 1)
                pe.wait_ge(v_kept, c)
                pe.wait_ge(state_ready, 4 * c + 4)
                for h in range(4):
                    pe.matmul(h_(bank[1], h), h_(tt, h), h_(rows[:, 2], h), start=True, stop=False)
                    mm = pe.matmul(h_(bank[1], h), h_(nw, h), h_(state, h), start=False, stop=True)
                mm.then_inc(v_done, 1)
                pe.wait_ge(v_kept, c + 1)
                for h in range(4):
                    mm = pe.matmul(h_(bank[3], h), h_(rows[:, 1], h), h_(vn, h), start=True, stop=True)
                pe.wait_ge(o_kept, c)
                for h in range(4):
                    pe.matmul(h_(bank[2], h), h_(state, h), qd[:, c, h * P:(h + 1) * P], start=True, stop=False)
                    mm = pe.matmul(h_(bank[2], h), h_(vn, h), attn[:, c, h * P:(h + 1) * P], start=False, stop=True)
                mm.then_inc(kv_done, 1)
            loop(pe, NB, body)

        @block.vector
        def _(dve):
            dve.memset(state, 0.0).then_inc(state_ready, 4)
            def body(c):
                dve.wait_ge(kv_done, c + 1)
                dve.wait_ge(state_ready, 4 * c + 4)
                for h in range(4):
                    dve.scalar_tensor_tensor(h_(state, h), h_(state, h), last[:, c, h:h + 1], h_(bank[3], h),
                                             ALU.mult, ALU.add).then_inc(state_ready, 1)
                dve.tensor_copy(o[:, :, bass.ds(c * P, P)], heads(bank[2])).then_inc(o_kept, 1)
            loop(dve, NB, body)
    m.top = base


def gated_store_phase(nc, m, d, src, scale, root, gate_tile, y_tile):
    z = m.take(BT, S)
    with phase(nc, "z_in", "scaled", "gated", "y_out") as (block, z_in, scaled, gated, y_out):

        @block.sync
        def _(sp):
            sp.dma_start(z, d["in2"][gate_tile:gate_tile + BT].rearrange("c p t -> p c t")).then_inc(z_in, 16)
            for j in range(BT):
                sp.wait_ge(gated, j + 1)
                sp.dma_start(d["y"][y_tile + j], z[:, j]).then_inc(y_out, 16)
            sp.wait_ge(y_out, 16 * BT)

        @block.vector
        def _(dve):
            dve.wait_ge(z_in, 16)
            for j in range(BT):
                if root is None:
                    dve.tensor_tensor(z[:, j], z[:, j], src[:, j], ALU.mult).then_inc(gated, 1)
                else:
                    dve.scalar_tensor_tensor(src[:, j], src[:, j], scale(j), root[:, j], ALU.mult,
                                             ALU.mult).then_inc(scaled, 1)
                    dve.wait_ge(scaled, j + 1)
                    dve.tensor_tensor(z[:, j], z[:, j], src[:, j], ALU.mult).then_inc(gated, 1)


def tile_roots_phase(nc, m, src, root, count):
    sq = m.take(2, S)
    ps = m.ps.rearrange("p (s h) f -> p s (h f)", s=4)
    with phase(nc, "squared", "summed", "logged", "rooted") as (block, squared, summed, logged, rooted):

        @block.scalar
        def _(act):
            act.preload_act_table_set(LN_EXP)
            for j in range(count):
                if j >= 2:
                    act.wait_ge(summed, j - 1)
                act.activation(sq[:, j % 2], src[:, j], ACT.Square).then_inc(squared, 1)
            for j in range(count):
                act.wait_ge(summed, j + 1)
                act.activation(root[:, j], ps[:, j], ACT.Ln, bias=m.c(C_EPS, 1), scale=1.0 / P).then_inc(logged, 1)
            for j in range(count):
                act.wait_ge(logged, j + 1)
                act.activation(root[:, j], root[:, j], ACT.Exp, scale=-0.5).then_inc(rooted, 1)

        @block.tensor
        def _(pe):
            for j in range(count):
                pe.wait_ge(squared, j + 1)
                for h in range(2):
                    mm = pe.matmul(ps[:, j, h * HALF:(h + 1) * HALF], m.c(C_ONE),
                                   sq[:, j % 2, h * HALF:(h + 1) * HALF], start=True, stop=True)
                mm.then_inc(summed, 1)


def delta_phases(nc, m, d):
    delta_conv_phase(nc, m, d)
    m.clear()
    at, attn, qd = (m.take(NB, BW) for _ in range(3))
    inv, inv_t = m.take(NB, BW), m.take(NB, BW)
    last = m.take(NB, 4)
    delta_prepare_phase(nc, m, d, at, attn, qd, last)
    delta_inverse_phase(nc, m, at, inv, inv_t)
    o = inv.rearrange("p c f -> p (c f)").rearrange("p (h t) -> p h t", h=4)
    delta_scan_phase(nc, m, d, attn, qd, inv_t, last, o)
    root = at.rearrange("p c f -> p (c f)").rearrange("p (h t) -> p h t", h=4)
    base = m.top
    tile_roots_phase(nc, m, o, root, BT)
    m.top = base
    gated_store_phase(nc, m, d, o, lambda j: m.p("a_norm", 0, 1), root, T_AZ, 0)


def conformer_phase(nc, m, d):
    m.clear()
    pad = CONFK - 1
    left, right = m.take(2, S), m.take(2, S)
    x = m.take(2, S + pad + 2)
    y = m.take(BT, S)
    sq, root = m.take(2, S), m.take(S)
    z = m.take(BT, S)
    mean = m.ps[:, 0:2, :].rearrange("p a f -> p (a f)")
    var = m.ps[:, 2:4, :].rearrange("p a f -> p (a f)")
    with phase(nc, "zeroed", "in_a", "in_b", "z_in", "sig_done", "glu_done", "conv_chain", "mean_done", "centred",
               "squared", "var_done", "logged", "rooted", "scaled", "silu_done", "gated", "y_out") as (
            block, zeroed, in_a, in_b, z_in, sig_done, glu_done, conv_chain, mean_done, centred,
            squared, var_done, logged, rooted, scaled, silu_done, gated, y_out):
        x_in = (in_a, in_b)

        @block.sync
        def _(sp):
            for j in range(BT):
                if j >= 2:
                    sp.wait_ge(glu_done, j - 1)
                sp.dma_start(left[:, j % 2], d["in2"][T_GLU + j]).then_inc(x_in[j % 2], 16)
                sp.dma_start(right[:, j % 2], d["in2"][T_GLU + BT + j]).then_inc(x_in[j % 2], 16)
            sp.dma_start(z, d["in2"][T_BZ:T_BZ + BT].rearrange("c p t -> p c t")).then_inc(z_in, 16)
            for j in range(BT):
                sp.wait_ge(gated, j + 1)
                sp.dma_start(d["y"][BT + j], z[:, j]).then_inc(y_out, 16)
            sp.wait_ge(y_out, 16 * BT)

        @block.scalar
        def _(act):
            for j in range(BT):
                act.wait_ge(x_in[j % 2], 32 * (j // 2) + 32)
                act.activation(right[:, j % 2], right[:, j % 2], ACT.Sigmoid).then_inc(sig_done, 1)
            for j in range(BT):
                act.wait_ge(centred, j + 1)
                if j >= 2:
                    act.wait_ge(var_done, j - 1)
                act.activation(sq[:, j % 2], y[:, j], ACT.Square).then_inc(squared, 1)
            act.wait_ge(var_done, BT)
            act.activation(root, var, ACT.Ln, bias=m.c(C_EPS, 1), scale=1.0 / BW).then_inc(logged, 1)
            act.wait_ge(logged, 1)
            act.activation(root, root, ACT.Exp, scale=-0.5).then_inc(rooted, 1)
            for j in range(BT):
                act.wait_ge(scaled, j + 1)
                act.activation(y[:, j], y[:, j], ACT.Silu, bias=m.p("b_ln_b", j)).then_inc(silu_done, 1)

        @block.vector
        def _(dve):
            for s in range(2):
                dve.memset(x[:, s, 0:pad], 0.0).then_inc(zeroed, 1)
            dve.wait_ge(zeroed, 2)
            for j in range(BT):
                dve.wait_ge(sig_done, j + 1)
                dve.tensor_tensor(x[:, j % 2, pad:pad + S], left[:, j % 2], right[:, j % 2], ALU.mult).then_inc(glu_done, 1)
                dve.wait_ge(glu_done, j + 1)
                conv(dve, x[:, j % 2], y[:, j], m.p("b_conv", j * CONFK, CONFK), CONFK, m.p("b_conv_b", j), conv_chain,
                     j * CONFK)
            dve.wait_ge(mean_done, 1)
            for j in range(BT):
                dve.scalar_tensor_tensor(y[:, j], mean, -1.0 / BW, y[:, j], ALU.mult, ALU.add).then_inc(centred, 1)
            dve.wait_ge(rooted, 1)
            for j in range(BT):
                dve.scalar_tensor_tensor(y[:, j], y[:, j], m.p("b_ln_g", j), root, ALU.mult, ALU.mult).then_inc(scaled, 1)
            dve.wait_ge(z_in, 16)
            for j in range(BT):
                dve.wait_ge(silu_done, j + 1)
                dve.tensor_tensor(z[:, j], z[:, j], y[:, j], ALU.mult).then_inc(gated, 1)

        @block.tensor
        def _(pe):
            for j in range(BT):
                pe.wait_ge(conv_chain, (j + 1) * CONFK)
                for h in range(2):
                    mm = pe.matmul(mean[:, h * HALF:(h + 1) * HALF], m.c(C_ONE), y[:, j, h * HALF:(h + 1) * HALF],
                                   start=(j == 0), stop=(j == BT - 1))
            mm.then_inc(mean_done, 1)
            for j in range(BT):
                pe.wait_ge(squared, j + 1)
                for h in range(2):
                    mm = pe.matmul(var[:, h * HALF:(h + 1) * HALF], m.c(C_ONE), sq[:, j % 2, h * HALF:(h + 1) * HALF],
                                   start=(j == 0), stop=(j == BT - 1))
                mm.then_inc(var_done, 1)


def recurrence_phase(nc, m, d):
    m.clear()
    pad = CONVK - 1
    wa, wx = m.take(BT, P), m.take(BT, P)
    x = m.take(2, S + 4)
    xc, r, ig, th, a = (m.take(BT, S) for _ in range(5))
    root = m.take(BT, S)
    neg = m.take(4)
    ps = m.ps.rearrange("p (s h) f -> p s (h f)", s=4)
    with phase(nc, "w_in", "zeroed", "in_a", "in_b", "z_in", "negated", "conv_chain", "r_product", "x_product",
               "r_done", "i_done", "a_done", "t_done", "ln_done", "inv_root", "t_root", "half_b", "gated_b", "b_done",
               "scanned", "gated", "y_out") as (
            block, w_in, zeroed, in_a, in_b, z_in, negated, conv_chain, r_product, x_product,
            r_done, i_done, a_done, t_done, ln_done, inv_root, t_root, half_b, gated_b, b_done, scanned, gated, y_out):
        x_in = (in_a, in_b)

        @block.sync
        def _(sp):
            sp.dma_start(wa, d["w_da"]).then_inc(w_in, 16)
            sp.dma_start(wx, d["w_dx"]).then_inc(w_in, 16)
            sp.wait_ge(zeroed, 2)
            for j in range(BT):
                if j >= 2:
                    sp.wait_ge(conv_chain, (j - 1) * CONVK)
                sp.dma_start(x[:, j % 2, pad:pad + S], d["in2"][T_DX + j]).then_inc(x_in[j % 2], 16)
            sp.wait_ge(b_done, BT)
            sp.dma_start(r, d["in2"][T_DZ:T_DZ + BT].rearrange("c p t -> p c t")).then_inc(z_in, 16)
            for j in range(BT):
                sp.wait_ge(gated, j + 1)
                sp.dma_start(d["y"][3 * BT + j], r[:, j]).then_inc(y_out, 16)
            sp.wait_ge(y_out, 16 * BT)

        @block.tensor
        def _(pe):
            pe.wait_ge(w_in, 32)
            for j in range(BT):
                pe.wait_ge(conv_chain, (j + 1) * CONVK)
                if j >= 2:
                    pe.wait_ge(r_done, j - 1)
                    pe.wait_ge(i_done, j - 1)
                for w, done, s in ((wa, r_product, 2 * (j % 2)), (wx, x_product, 2 * (j % 2) + 1)):
                    for h in range(2):
                        mm = pe.matmul(ps[:, s, h * HALF:(h + 1) * HALF], w[:, j], xc[:, j, h * HALF:(h + 1) * HALF],
                                       start=True, stop=True)
                    mm.then_inc(done, 1)

        @block.scalar
        def _(act):
            for j in range(BT):
                act.wait_ge(r_product, j + 1)
                act.activation(r[:, j], ps[:, 2 * (j % 2)], ACT.Sigmoid, bias=m.p("d_ba", j)).then_inc(r_done, 1)
                act.wait_ge(x_product, j + 1)
                act.activation(ig[:, j], ps[:, 2 * (j % 2) + 1], ACT.Sigmoid, bias=m.p("d_bx", j)).then_inc(i_done, 1)
            act.wait_ge(negated, 1)
            for j in range(BT):
                act.wait_ge(r_done, j + 1)
                act.activation(a[:, j], r[:, j], ACT.Exp, scale=neg[:, j:j + 1]).then_inc(a_done, 1)
                act.activation(th[:, j], r[:, j], ACT.Tanh, scale=m.rate[:, j:j + 1]).then_inc(t_done, 1)
            for j in range(BT):
                act.wait_ge(t_done, j + 1)
                act.activation(root[:, j], th[:, j], ACT.Ln, bias=1.0).then_inc(ln_done, 1)
            for j in range(BT):
                act.wait_ge(ln_done, j + 1)
                act.activation(root[:, j], root[:, j], ACT.Exp, scale=-0.5).then_inc(inv_root, 1)
            for j in range(BT):
                act.activation(th[:, j], th[:, j], ACT.Sqrt, scale=2.0).then_inc(t_root, 1)

        @block.vector
        def _(dve):
            for s in range(2):
                dve.memset(x[:, s, 0:pad], 0.0).then_inc(zeroed, 1)
            dve.tensor_scalar(neg, m.rate, -1.0, None, ALU.mult).then_inc(negated, 1)
            for j in range(BT):
                dve.wait_ge(x_in[j % 2], 16 * (j // 2) + 16)
                conv(dve, x[:, j % 2], xc[:, j], m.p("d_conv", j * CONVK, CONVK), CONVK, m.p("d_conv_b", j), conv_chain,
                     j * CONVK)
            for j in range(BT):
                dve.wait_ge(t_root, j + 1)
                dve.tensor_tensor(th[:, j], th[:, j], root[:, j], ALU.mult).then_inc(half_b, 1)
                dve.wait_ge(half_b, j + 1)
                dve.tensor_tensor(th[:, j], th[:, j], ig[:, j], ALU.mult).then_inc(gated_b, 1)
                dve.wait_ge(gated_b, j + 1)
                dve.tensor_tensor(th[:, j], th[:, j], xc[:, j], ALU.mult).then_inc(b_done, 1)
                dve.wait_ge(b_done, j + 1)
                dve.tensor_tensor_scan(root[:, j], a[:, j], th[:, j], 0.0, ALU.mult, ALU.add).then_inc(scanned, 1)
            dve.wait_ge(z_in, 16)
            for j in range(BT):
                dve.wait_ge(scanned, j + 1)
                dve.tensor_tensor(r[:, j], r[:, j], root[:, j], ALU.mult).then_inc(gated, 1)


def bucket_ranges():
    n = np.arange(P)
    exact, buckets, far = 16, 32, 128
    large = exact + (np.log(np.maximum(n, 1) / exact) / np.log(far / exact) * (buckets - exact)).astype(np.int32)
    b = np.where(n < exact, n, np.minimum(large, buckets - 1))
    return [(int(v), int(np.argmax(b == v)), int(P - np.argmax(b[::-1] == v))) for v in sorted(set(b.tolist()))]


def band_phase(nc, m, d, bias, bias0):
    rel, row = m.take(32), m.take(384)
    ranges = bucket_ranges()
    with phase(nc, "rel_in", "cleared", "placed", "row_out", "band_in", "first_done") as (
            block, rel_in, cleared, placed, row_out, band_in, first_done):

        @block.sync
        def _(sp):
            sp.dma_start(rel[0:8], d["rel_bias"]).then_inc(rel_in, 16)
            sp.wait_ge(placed, len(ranges))
            sp.dma_start(d["band"], row[0:8].unsqueeze(1).to_broadcast([8, P, 384])).then_inc(row_out, 16)
            sp.wait_ge(row_out, 16)
            for h in range(8):
                src = bass.AP(d["band"].tensor, h * P * 384 + P - 1, [[383, P], [1, 2 * P]])
                sp.dma_start(bias[:, h], src).then_inc(band_in, 16)
            sp.wait_ge(band_in, 128)

        @block.vector
        def _(dve):
            dve.memset(row[0:8], NEG).then_inc(cleared, 1)
            dve.wait_ge(cleared, 1)
            dve.wait_ge(rel_in, 16)
            for b, lo, hi in ranges:
                dve.tensor_copy(row[0:8, 256 - hi:256 - lo], rel[0:8, b:b + 1].to_broadcast([8, hi - lo])).then_inc(placed, 1)
            dve.memset(bias0[:, :, 0:P], NEG).then_inc(first_done, 1)
            dve.wait_ge(band_in, 128)
            dve.tensor_copy(bias0[:, :, P:2 * P], bias[:, :, P:2 * P]).then_inc(first_done, 1)


def window_phase(nc, m, d, units, scale, q_tiles, window, biases, sink, k_of, v_of, out_of, q_of, keep_of, y):
    T = units
    qs = m.take(BT, P)
    win = m.take(3, 2 * P)
    vt = m.take(2, P)
    sc, pt = m.take(2, BW), m.take(2, BW)
    mx, nm, rs, ri, dk, es = (m.take(2, 2) for _ in range(6))
    with phase(nc, "cleared", "q_in", "k_in", "v_turned", "v_kept", "s_done", "s_kept", "max_done", "max_sink",
               "negated", "sink_diff", "p_ready", "sink_exp", "sum_done", "inverted", "p_scaled", "t_done", "t_kept",
               "o_done", "o_kept") as (
            block, cleared, q_in, k_in, v_turned, v_kept, s_done, s_kept, max_done, max_sink,
            negated, sink_diff, p_ready, sink_exp, sum_done, inverted, p_scaled, t_done, t_kept, o_done, o_kept):

        def blocks(eng, body):
            body(0)
            with eng.Fori(1, NB) as n:
                body(n)

        @block.sync
        def _(sp):
            def stage(n):
                sp.wait_ge(o_done, n * T)
                sp.dma_start(qs, d["in2"][q_tiles:q_tiles + BT, :, bass.ds(n * P, P)].rearrange("c p t -> p c t")).then_inc(q_in, 16)
                if window is not None:
                    if isinstance(n, int):
                        sp.wait_ge(cleared, 1)
                        sp.dma_start(win[:, :, P:2 * P], d["in2"][window:window + 3, :, 0:P].rearrange("c p t -> p c t")).then_inc(k_in, 16)
                    else:
                        sp.dma_start(win, d["in2"][window:window + 3, :, bass.ds(n * P - P, 2 * P)].rearrange("c p t -> p c t")).then_inc(k_in, 16)
            blocks(sp, stage)

        @block.tensor
        def _(pe):
            def block_(n):
                b = n * T
                pe.wait_ge(q_in, 16 * n + 16)
                if window is not None:
                    pe.wait_ge(k_in, 16 * n + 16)
                    pe.wait_ge(v_kept, n)
                    pe.wait_ge(t_kept, n * T)
                    for s in range(2):
                        mm = pe.transpose(m.ps[:, 4, s * P:(s + 1) * P], win[:, 2, s * P:(s + 1) * P], m.c(C_ID))
                    mm.then_inc(v_turned, 1)
                for t in range(T + 2):
                    if t < T:
                        pe.wait_ge(s_kept, b + max(t - 1, 0))
                        for g in range(2):
                            mm = pe.matmul(m.ps[:, 2 * (t % 2) + g, 0:2 * P], q_of(qs, t, g), k_of(win, t, g),
                                           start=True, stop=True)
                        mm.then_inc(s_done, 1)
                    if 0 <= t - 1 < T:
                        u = t - 1
                        pe.wait_ge(p_scaled, 2 * (b + u) + 2)
                        pe.wait_ge(t_kept, b + max(u - 1, 0))
                        if window is not None:
                            pe.wait_ge(v_kept, n + 1)
                        for c in range(4):
                            mm = pe.transpose(m.ps[:, 4 + u % 2, c * P:(c + 1) * P], sc[:, u % 2, c * P:(c + 1) * P], m.c(C_ID))
                        mm.then_inc(t_done, 1)
                    if 0 <= t - 2 < T:
                        u = t - 2
                        pe.wait_ge(t_kept, b + u + 1)
                        pe.wait_ge(o_kept, b + max(u - 1, 0))
                        for g in range(2):
                            for kb in range(2):
                                c = 2 * g + kb
                                mm = pe.matmul(out_of(m.ps[:, 6 + u % 2], g), v_of(vt, u, g, kb),
                                               pt[:, u % 2, c * P:(c + 1) * P], start=(kb == 0), stop=(kb == 1))
                        mm.then_inc(o_done, 1)
            blocks(pe, block_)

        @block.vector
        def _(dve):
            if window is not None:
                dve.memset(win[:, :, 0:P], 0.0).then_inc(cleared, 1)

            def block_(n):
                b = n * T
                for t in range(T + 3):
                    if t < T:
                        s = t % 2
                        dve.wait_ge(s_done, b + t + 1)
                        dve.wait_ge(t_done, b + max(t - 1, 0))
                        two = m.ps[:, 2 * s:2 * s + 2, 0:2 * P]
                        to = sc[:, s].rearrange("p (g k) -> p g k", g=2)
                        if biases is None:
                            dve.tensor_scalar(to, two, scale, None, ALU.mult).then_inc(s_kept, 1)
                        else:
                            bias = biases[isinstance(n, int)][:, 2 * t:2 * t + 2]
                            dve.scalar_tensor_tensor(to, two, scale, bias, ALU.mult, ALU.add).then_inc(s_kept, 1)
                        dve.wait_ge(s_kept, b + t + 1)
                        dve.wait_ge(sink_diff if sink else negated, b + t)
                        dve.tensor_reduce(mx[:, s], sc[:, s].rearrange("p (g k) -> p g k", g=2), AX.X, ALU.max).then_inc(max_done, 1)
                        dve.wait_ge(max_done, b + t + 1)
                        if sink:
                            dve.tensor_tensor(mx[:, s], mx[:, s], m.p("sinks", 2 * t, 2), ALU.max).then_inc(max_sink, 1)
                            dve.wait_ge(max_sink, b + t + 1)
                            dve.wait_ge(sink_exp, b + max(t - 1, 0))
                            dve.tensor_tensor(dk[:, s], m.p("sinks", 2 * t, 2), mx[:, s], ALU.subtract).then_inc(sink_diff, 1)
                        dve.wait_ge(p_ready, 2 * (b + max(t - 1, 0)))
                        dve.tensor_scalar(nm[:, s], mx[:, s], -1.0, None, ALU.mult).then_inc(negated, 1)
                    if 0 <= t - 1 < T:
                        u = t - 1
                        s = u % 2
                        dve.wait_ge(p_ready, 2 * (b + u) + 2)
                        if sink:
                            dve.wait_ge(sink_exp, b + u + 1)
                            dve.tensor_tensor(rs[:, s], rs[:, s], es[:, s], ALU.add).then_inc(sum_done, 1)
                            dve.wait_ge(sum_done, b + u + 1)
                        dve.wait_ge(p_scaled, 2 * (b + u))
                        dve.reciprocal(ri[:, s], rs[:, s]).then_inc(inverted, 1)
                        dve.wait_ge(inverted, b + u + 1)
                        for g in range(2):
                            w = sc[:, s, g * 2 * P:(g + 1) * 2 * P]
                            dve.tensor_scalar(w, w, ri[:, s, g:g + 1], None, ALU.mult).then_inc(p_scaled, 1)
                    if 0 <= t - 3 < T:
                        u = t - 3
                        dve.wait_ge(o_done, b + u + 1)
                        to, of = keep_of(y, u, n, m.ps[:, 6 + u % 2])
                        dve.tensor_copy(to, of).then_inc(o_kept, 1)
            blocks(dve, block_)

        @block.scalar
        def _(act):
            def block_(n):
                b = n * T
                if window is not None:
                    act.wait_ge(v_turned, n + 1)
                    act.wait_ge(o_done, n * T)
                    act.activation(vt, m.ps[:, 4, 0:2 * P].rearrange("p (s f) -> p s f", s=2), ACT.Copy).then_inc(v_kept, 1)
                for t in range(T + 1):
                    if t < T:
                        s = t % 2
                        act.wait_ge(negated, b + t + 1)
                        act.wait_ge(inverted, b + max(t - 1, 0))
                        for g in range(2):
                            w = sc[:, s, g * 2 * P:(g + 1) * 2 * P]
                            act.activation(w, w, ACT.Exp, bias=nm[:, s, g:g + 1], accum_out=rs[:, s, g:g + 1]).then_inc(p_ready, 1)
                        if sink:
                            act.wait_ge(sink_diff, b + t + 1)
                            act.activation(es[:, s], dk[:, s], ACT.Exp).then_inc(sink_exp, 1)
                    if 0 <= t - 1 < T:
                        u = t - 1
                        act.wait_ge(t_done, b + u + 1)
                        act.wait_ge(o_done, b + max(u - 1, 0))
                        act.activation(pt[:, u % 2], m.ps[:, 4 + u % 2], ACT.Copy).then_inc(t_kept, 1)
            blocks(act, block_)


def sliding_phases(nc, m, d):
    m.clear()
    y = m.take(BT, S)
    bias, bias0 = m.take(8, 2 * P), m.take(8, 2 * P)
    base = m.top
    band_phase(nc, m, d, bias, bias0)
    m.top = base
    window_phase(
        nc, m, d, 4, 64.0 ** -0.5, T_CQ, T_CK, (bias, bias0), True,
        q_of=lambda qs, t, g: qs[64 * g:64 * g + 64, t],
        k_of=lambda win, t, g: win[64 * g:64 * g + 64, t // 2],
        v_of=lambda vt, t, g, kb: vt[:, kb, 64 * (t // 2):64 * (t // 2) + 64],
        out_of=lambda bank, g: bank[64 * g:64 * g + 64, 0:P],
        keep_of=lambda y, t, n, bank: (y[:, t, bass.ds(n * P, P)], bank[:, 0:P]), y=y)
    m.top = base
    gated_store_phase(nc, m, d, y, None, None, T_CZ, 2 * BT)


def memory_phases(nc, m, d):
    m.clear()
    y = m.take(BT, S)
    mem_k = m.take(BT, MEM)
    mem_v = m.take(MEM // P, BW)
    base = m.top
    mem = m.take(DC, MEM)
    sq, root = m.take(2, MEM), m.take(MEM)
    wt = m.take(BT, DC * P)
    wv = m.take(DC, BW)
    with phase(nc, "mem_in", "w_in", "squared", "summed", "logged", "rooted", "scaled", "k_done", "k_kept", "v_done",
               "v_kept") as (
            block, mem_in, w_in, squared, summed, logged, rooted, scaled, k_done, k_kept, v_done, v_kept):

        @block.sync
        def _(sp):
            sp.dma_start(mem, d["mem"].rearrange("(k p) t -> p k t", p=P)).then_inc(mem_in, 16)
            sp.dma_start(wt, d["w_mk"].rearrange("c p f -> p c f")).then_inc(w_in, 16)
            sp.dma_start(wv, d["w_mv"]).then_inc(w_in, 16)

        @block.scalar
        def _(act):
            act.wait_ge(mem_in, 16)
            for k in range(DC):
                if k >= 2:
                    act.wait_ge(summed, k - 1)
                act.activation(sq[:, k % 2], mem[:, k], ACT.Square).then_inc(squared, 1)
            act.wait_ge(summed, DC)
            act.activation(root, m.ps[:, 0, 0:MEM], ACT.Ln, bias=m.c(C_EPS, 1), scale=1.0 / D).then_inc(logged, 1)
            act.wait_ge(logged, 1)
            act.activation(root, root, ACT.Exp, scale=-0.5).then_inc(rooted, 1)
            for j in range(BT):
                act.wait_ge(k_done, j + 1)
                act.activation(mem_k[:, j], m.ps[:, 1 + j % 2, 0:MEM], ACT.Copy).then_inc(k_kept, 1)
            for j in range(MEM // P):
                act.wait_ge(v_done, j + 1)
                act.activation(mem_v[:, j], m.ps[:, 3 + j, :], ACT.Copy).then_inc(v_kept, 1)

        @block.vector
        def _(dve):
            dve.wait_ge(rooted, 1)
            for k in range(DC):
                dve.scalar_tensor_tensor(mem[:, k], mem[:, k], m.p("mem_g", k), root, ALU.mult, ALU.mult).then_inc(scaled, 1)

        @block.tensor
        def _(pe):
            for k in range(DC):
                pe.wait_ge(squared, k + 1)
                pe.matmul(m.ps[:, 0, 0:MEM], m.c(C_ONE), sq[:, k % 2], start=(k == 0), stop=(k == DC - 1)).then_inc(summed, 1)
            pe.wait_ge(scaled, DC)
            pe.wait_ge(w_in, 32)
            for j in range(BT):
                if j >= 2:
                    pe.wait_ge(k_kept, j - 1)
                for k in range(DC):
                    mm = pe.matmul(m.ps[:, 1 + j % 2, 0:MEM], wt[:, j, k * P:(k + 1) * P], mem[:, k],
                                   start=(k == 0), stop=(k == DC - 1))
                mm.then_inc(k_done, 1)
            for j in range(MEM // P):
                for k in range(DC):
                    mm = pe.matmul(m.ps[:, 3 + j, :], mem[:, k, j * P:(j + 1) * P], wv[:, k],
                                   start=(k == 0), stop=(k == DC - 1))
                mm.then_inc(v_done, 1)
    m.top = base
    window_phase(
        nc, m, d, 2, float(P) ** -0.5, T_EQ, None, None, False,
        q_of=lambda qs, t, g: qs[:, 2 * t + g],
        k_of=lambda win, t, g: mem_k[:, 2 * t + g],
        v_of=lambda vt, t, g, kb: mem_v[:, kb, (2 * t + g) * P:(2 * t + g + 1) * P],
        out_of=lambda bank, g: bank[:, g * P:(g + 1) * P],
        keep_of=lambda y, t, n, bank: (y[:, 2 * t:2 * t + 2, bass.ds(n * P, P)],
                                       bank[:, 0:2 * P].rearrange("p (g f) -> p g f", g=2)), y=y)
    m.top = base
    gated_store_phase(nc, m, d, y, None, None, T_EZ, 4 * BT)


def merge_phase(nc, m, d, merged):
    raw_y = m.take(BT, S)
    y = m.take_split("y", BT, S)
    raw_g, raw_b = m.take(2, DC, P), m.take(2, BT, P)
    wg, wb = m.take_split("wg", 2, DC, P), m.take_split("wb", 2, BT, P)
    sg = m.take(2, S)
    gate_ps = m.ps[:, 0:4, :].rearrange("p (s h) f -> p s (h f)", s=2)
    br_ps = m.ps[:, 4:8, :].rearrange("p (s h) f -> p s (h f)", s=2)
    gate_bias = m.p("b_gate", 0, 40)
    T = DC
    with phase(nc, "y_in", "y_hi", "y_lo", "wg_a", "wg_b", "wb_a", "wb_b", "w_hi", "w_lo", "gate_done", "branch_done",
               "sig_done", "weighted", "added") as (
            block, y_in, y_hi, y_lo, wg_a, wg_b, wb_a, wb_b, w_hi, w_lo, gate_done, branch_done,
            sig_done, weighted, added):
        g_in, b_in = (wg_a, wg_b), (wb_a, wb_b)

        def start(n, u):
            return isinstance(n, int) and n == 0 and u < 2

        @block.sync
        def _(sp):
            def branch(n):
                for u in range(T):
                    s = u % 2
                    if not start(n, u):
                        sp.wait_ge(w_lo, n * T + u - 1)
                    sp.dma_start(raw_g[:, s].rearrange("p k f -> p (k f)"), d["w_gate"][n * DC + u]).then_inc(g_in[s], 16)
                    sp.dma_start(raw_b[:, s].rearrange("p k f -> p (k f)"), d["w_br"][n, u]).then_inc(b_in[s], 16)
                    if u == 1:
                        if not isinstance(n, int):
                            sp.wait_ge(y_lo, n * BT)
                        sp.dma_start(raw_y, d["y"][bass.ds(n * BT, BT)].rearrange("c p t -> p c t")).then_inc(y_in, 16)
            loop(sp, NBR, branch)

        @block.gpsimd
        def _(pool):
            def branch(n):
                for u in range(T):
                    s = u % 2
                    pool.wait_ge(w_hi, n * T + u + 1)
                    if not start(n, u):
                        pool.wait_ge(branch_done, n * T + u - 1)
                    pool.tensor_tensor(wg.lo[:, s], raw_g[:, s], wg.hi[:, s].bitcast(F32), ALU.subtract)
                    pool.tensor_tensor(wb.lo[:, s], raw_b[:, s], wb.hi[:, s].bitcast(F32), ALU.subtract).then_inc(w_lo, 1)
            loop(pool, NBR, branch)

        @block.tensor
        def _(pe):
            def product(banks, w, x, kc):
                for k in range(kc):
                    first, last = k == 0, k == kc - 1
                    for h, bank in enumerate(halves(banks)):
                        pe.matmul(bank, w.hi[:, k], halves(x.hi[:, k])[h], start=first, stop=False)
                        pe.matmul(bank, w.hi[:, k], halves(x.lo[:, k])[h], start=False, stop=False)
                    for h, bank in enumerate(halves(banks)):
                        mm = pe.matmul(bank, w.lo[:, k], halves(x.hi[:, k])[h], start=False, stop=last)
                return mm

            def branch(n):
                for u in range(T):
                    s = u % 2
                    pe.wait_ge(w_lo, n * T + u + 1)
                    if not start(n, u):
                        pe.wait_ge(sig_done, n * T + u - 1)
                    product(gate_ps[:, s], wg[:, s], m.split, DC).then_inc(gate_done, 1)
                    if u == 0:
                        pe.wait_ge(y_lo, n * BT + BT)
                    if not start(n, u):
                        pe.wait_ge(weighted, n * T + u - 1)
                    product(br_ps[:, s], wb[:, s], y, BT).then_inc(branch_done, 1)
            loop(pe, NBR, branch)

        @block.scalar
        def _(act):
            def high(n, u):
                s = u % 2
                act.wait_ge(g_in[s], 16 * (n * (T // 2) + u // 2) + 16)
                act.wait_ge(b_in[s], 16 * (n * (T // 2) + u // 2) + 16)
                if not start(n, u):
                    act.wait_ge(branch_done, n * T + u - 1)
                act.activation(wg.hi[:, s], raw_g[:, s], ACT.Copy)
                act.activation(wb.hi[:, s], raw_b[:, s], ACT.Copy).then_inc(w_hi, 1)

            def branch(n, products_left=True):
                act.wait_ge(y_in, 16 * n + 16)
                if not start(n, 0):
                    act.wait_ge(branch_done, n * T)
                for k in range(BT):
                    act.activation(y.hi[:, k], raw_y[:, k], ACT.Copy).then_inc(y_hi, 1)
                for u in range(T):
                    s = u % 2
                    act.wait_ge(gate_done, n * T + u + 1)
                    if not start(n, u):
                        act.wait_ge(added, n * T + u - 1)
                    act.activation(sg[:, s], gate_ps[:, s], ACT.Sigmoid,
                                   bias=gate_bias[:, bass.ds(n * DC + u, 1)]).then_inc(sig_done, 1)
                    if products_left or u + 2 < T:
                        high(n, u + 2)
            high(0, 0)
            high(0, 1)
            branch(0)
            with act.Fori(1, NBR - 1) as n:
                branch(n)
            branch(NBR - 1, False)

        @block.vector
        def _(dve):
            def branch(n):
                for k in range(BT):
                    dve.wait_ge(y_hi, n * BT + k + 1)
                    dve.tensor_tensor(y.lo[:, k], raw_y[:, k], y.hi[:, k].bitcast(F32), ALU.subtract).then_inc(y_lo, 1)
                for u in range(T):
                    s = u % 2
                    dve.wait_ge(sig_done, n * T + u + 1)
                    dve.wait_ge(branch_done, n * T + u + 1)
                    if isinstance(n, int):
                        dve.tensor_tensor(merged[:, u], sg[:, s], br_ps[:, s], ALU.mult).then_inc(weighted, 1)
                        dve.wait_ge(weighted, n * T + u + 1).then_inc(added, 1)
                    else:
                        dve.tensor_tensor(sg[:, s], sg[:, s], br_ps[:, s], ALU.mult).then_inc(weighted, 1)
                        dve.wait_ge(weighted, n * T + u + 1)
                        dve.wait_ge(added, n * T + u)
                        dve.tensor_tensor(merged[:, u], merged[:, u], sg[:, s], ALU.add).then_inc(added, 1)
            loop(dve, NBR, branch)


def second_block(nc, m, d):
    m.clear(top=A_WORK)
    norm_phase(nc, m, m.res, m.split, m.p("pre_g", 0, 8), DC, (m.take(2, S), m.take(S)), spill=d["res"])
    m.clear(top=A_WORK)
    gemm_phase(nc, m, d["w_in2"][0:N_PLAIN], m.split, DC, N_PLAIN, "store", bias=m.p("b_in", 0, N_PLAIN), out=d["in2"])
    m.clear(top=A_WORK)
    gemm_phase(nc, m, d["w_in2"][N_PLAIN:N_IN2], m.split, DC, N_IN2 - N_PLAIN, "store",
               bias=m.p("b_in", N_PLAIN, N_IN2 - N_PLAIN), func=ACT.Silu, out=d["in2"], tile0=N_PLAIN)
    m.clear(top=A_WORK)
    rows_phase(nc, m, m.split, DC, d["w_ab"], 8, NB, d["ab"])
    small_phase(nc, m, d)
    delta_phases(nc, m, d)
    conformer_phase(nc, m, d)
    recurrence_phase(nc, m, d)
    sliding_phases(nc, m, d)
    memory_phases(nc, m, d)
    m.clear(top=A_WORK)
    norm_phase(nc, m, m.res, m.split, m.p("pre_g", 0, 8), DC, (m.take(2, S), m.take(S)))
    m.clear(top=A_WORK)
    merge_phase(nc, m, d, m.res)
    split_phase(nc, m.res, m.split, DC)
    m.clear(top=A_WORK, end=A_ACT)
    gemm_phase(nc, m, d["w_out"], m.split, DC, DC, "keep", dst=m.act, reload=(m.res, d["res"]))
    m.clear(top=A_WORK, end=A_ACT)
    norm_phase(nc, m, m.act, m.act, m.p("post_g", 0, 8), DC, (m.take(2, S), m.take(S)), residual=m.res)
    with phase(nc, "all_out") as (block, all_out):
        @block.sync
        def _(sp):
            sp.dma_start(d["out"].rearrange("(k p) t -> p k t", p=P), m.act).then_inc(all_out, 16)
            sp.wait_ge(all_out, 16)


FF_PARTS = 4
SCRATCH = {
    "rope": (2, P, S), "in1": (13, P, S), "v_sb": (NB, P, BW), "k_rope": (ROPE, S), "q_rope": (2 * P, S),
    "mla_q": (MLA_H, P, S), "mla_k": (MLA_H, P, S), "mla_v": (NB, P, BW),
    "in2": (N_IN2, P, S), "ab": (NB, P, 8), "delta": (3 * BT, P, S), "kv_rows": (NB, P, 3 * BW),
    "band": (8, P, 384), "res": (DC, P, S), "mem_v": (MEM // P, P, BW), "y": (NBR * BT, P, S),
}


def first_block(nc, m, d):
    load_phase(nc, m, d)
    m.clear(top=A_WORK)
    norm_phase(nc, m, m.res, m.split, m.p("attn_g", 0, 8), DC, (m.take(2, S), m.take(S)))
    m.clear(top=A_WORK)
    gemm_phase(nc, m, d["w_in1"], m.split, DC, 13, "store", out=d["in1"])
    m.clear(top=A_WORK)
    rows_phase(nc, m, m.split, DC, d["w_v1"], BW, NB, d["v_sb"])
    stick_phase(nc, m, d)
    latent_phases(nc, m, d)
    latent_attention_phase(nc, m, d)
    m.clear(top=A_WORK, end=A_ACT)
    scratch = (m.take(2, S), m.take(S))
    norm_phase(nc, m, m.act[:, 0:4], m.split[:, 0:4], m.p("sb_g", 0, 4), 4, scratch)
    norm_phase(nc, m, m.act[:, 4:8], m.split[:, 4:8], m.p("mla_g", 0, 4), 4, scratch)
    m.clear(top=A_WORK)
    gemm_phase(nc, m, d["w_o"], m.split, DC, DC, "add", dst=m.res)
    m.clear(top=A_WORK)
    norm_phase(nc, m, m.res, m.split, m.p("mlp_g", 0, 8), DC, (m.take(2, S), m.take(S)))
    m.clear(top=A_WORK)
    part = F_FF // P // FF_PARTS
    hidden = m.take_split("hidden", part, S)
    base = m.top
    for n in range(FF_PARTS):
        m.top = base
        gemm_phase(nc, m, d["w_up"][n * part:(n + 1) * part], m.split, DC, part, "relu2", dst=hidden)
        m.top = base
        gemm_phase(nc, m, d["w_down"][n], hidden, part, DC, "add", dst=m.res)
    m.clear(top=A_WORK)
    norm_phase(nc, m, m.res, m.res, m.p("final_g", 0, 8), DC, (m.take(2, S), m.take(S)))


def program(nc, d):
    for name, shape in SCRATCH.items():
        d[name] = nc.dram_tensor("scratch_" + name, shape, F32).ap()
    m = Mem(nc)
    first_block(nc, m, d)
    second_block(nc, m, d)


def layout(inp):
    g = {k: np.asarray(v) for k, v in inp.items()}

    def tiles(w):
        k, n = w.shape
        return np.ascontiguousarray(w.reshape(k // P, P, n // P, P).transpose(2, 1, 0, 3).reshape(n // P, P, k))

    def rows(w):
        k, n = w.shape
        return np.ascontiguousarray(w.reshape(k // P, P, n).transpose(1, 0, 2))

    def cols(v):
        return v.reshape(-1, P).T

    def swap(w):
        k, n = w.shape
        return w.reshape(k, n // ROPE, 2, ROPE // 2)[:, :, ::-1].reshape(k, n)

    w_in, w_qb, w_kvb = g["w_in"][0], g["w_q_b"][0], g["w_kv_b"][0]
    kr = w_in[:, 1920:1984]
    qb = w_qb.reshape(Q_LORA, MLA_H, NOPE + ROPE)
    qr = qb[:, :, NOPE:].reshape(Q_LORA, MLA_H * ROPE)
    kvb = w_kvb.reshape(KV_LORA, MLA_H, 2 * P)
    out = {
        "x": np.ascontiguousarray(g["x"][0].T),
        "positions": g["positions"],
        "w_in1": tiles(np.concatenate([w_in[:, 0:1024], w_in[:, 1536:1920], kr, kr, swap(kr), swap(kr)], 1)),
        "w_v1": rows(w_in[:, 1024:1536]),
        "w_qn": tiles(qb[:, :, :NOPE].reshape(Q_LORA, -1)),
        "w_qr": tiles(np.concatenate([qr, swap(qr)], 1)),
        "w_kn": tiles(kvb[:, :, :P].reshape(KV_LORA, -1)),
        "w_vm": rows(np.ascontiguousarray(kvb[:, :, P:]).reshape(KV_LORA, -1)),
        "w_o": tiles(g["w_o"][0]),
        "w_up": tiles(g["w_up"][0]),
        "w_down": np.stack([tiles(part) for part in np.split(g["w_down"][0], FF_PARTS, axis=0)]),
    }
    w2, b2 = g["w_in_2"][0], g["b_in_2"][0]
    off = np.cumsum([0, 1536, 512, 4, 4, 1024, 512, 512, 256, 512, 512, 512, 512, 512, 5120])
    (qkv, az, be, al, glu, bz, cq, ckv, cz, dx, dz, eq, ez, gate) = [(off[n], off[n + 1]) for n in range(14)]

    def pick(a):
        ck = a[..., ckv[0]:ckv[0] + 128]
        cv = a[..., ckv[0] + 128:ckv[1]]
        k0, k1 = ck[..., :64], ck[..., 64:]
        part = [a[..., lo:hi] for lo, hi in (qkv, glu, cq)]
        part += [k0, k0, k1, k1, cv]
        part += [a[..., lo:hi] for lo, hi in (dx, eq, az, bz, cz, dz, ez)]
        return np.concatenate(part, -1)

    wbr = g["w_br_2"][0]

    def diagonal(w):
        t = np.zeros((BT, P, P), w.dtype)
        for n in range(BT):
            t[n, :64, :64] = w[2 * n]
            t[n, 64:, 64:] = w[2 * n + 1]
        return np.ascontiguousarray(t.transpose(1, 0, 2))

    def taps(w):
        k, c = w.shape
        return w.T.reshape(c // P, P, k).transpose(1, 0, 2).reshape(P, -1)

    def spread(v):
        return np.broadcast_to(v.reshape(1, -1), (P, v.size))

    out.update({
        "mem": np.ascontiguousarray(g["mem_2"][0].T),
        "w_in2": tiles(pick(w2)),
        "w_ab": rows(np.concatenate([w2[:, be[0]:be[1]], w2[:, al[0]:al[1]]], 1)),
        "w_gate": tiles(w2[:, gate[0]:]),
        "w_br": np.stack([tiles(wbr[n]) for n in range(NBR)]),
        "w_out": tiles(g["w_out_2"][0]),
        "w_mk": tiles(g["w_mem_kv_2"][0][:, :BW]),
        "w_mv": rows(g["w_mem_kv_2"][0][:, BW:]),
        "w_da": diagonal(g["d_w_a_2"][0]),
        "w_dx": diagonal(g["d_w_x_2"][0]),
        "rel_bias": np.ascontiguousarray(g["rel_bias_2"].T),
        "consts": constants(),
    })
    vec = {
        "attn_g": cols(g["attn_norm_g"][0]), "q_a_g": cols(g["q_a_norm_g"][0]), "kv_a_g": cols(g["kv_a_norm_g"][0]),
        "sb_g": cols(g["sb_out_norm_g"][0]), "mla_g": cols(g["mla_out_norm_g"][0]), "mlp_g": cols(g["mlp_norm_g"][0]),
        "final_g": cols(g["final_norm_g"]), "pre_g": cols(g["g_pre_2"][0]), "post_g": cols(g["g_post_2"][0]),
        "mem_g": cols(g["g_mem_2"][0]), "b_in": cols(pick(b2)), "b_gate": cols(b2[gate[0]:]),
        "a_conv": taps(g["a_conv_w_2"][0]), "a_norm": cols(g["a_norm_g_2"][0]), "b_conv": taps(g["b_dw_w_2"][0]),
        "b_conv_b": cols(g["b_dw_b_2"][0]), "b_ln_g": cols(g["b_ln_g_2"][0]), "b_ln_b": cols(g["b_ln_b_2"][0]),
        "d_conv": taps(g["d_conv_w_2"][0]), "d_conv_b": cols(g["d_conv_b_2"][0]), "d_ba": cols(g["d_b_a_2"][0]),
        "d_bx": cols(g["d_b_x_2"][0]), "d_lam": cols(g["d_lambda_2"][0]),
        "ab_bias": spread(np.concatenate([b2[be[0]:be[1]], b2[al[0]:al[1]]])),
        "a_log": spread(g["a_log_2"][0]), "a_dt": spread(g["a_dt_bias_2"][0]), "sinks": spread(g["c_sinks_2"][0]),
    }
    for n, w in _PAR:
        assert vec[n].shape == (P, w), (n, vec[n].shape)
    out["params"] = np.ascontiguousarray(np.concatenate([vec[n] for n, _ in _PAR], 1))
    return out


def kernel(**inputs):
    import concourse.bacc as _bacc
    from concourse.bass_utils import run_bass_kernel_spmd as _run

    nc = _bacc.Bacc("TRN2", target_bir_lowering=False, num_devices=1)
    arrays, d = {}, {}
    for name, a in layout(inputs).items():
        arrays["in_" + name] = a
        d[name] = nc.dram_tensor("in_" + name, a.shape, mybir.dt.from_np(a.dtype), kind="ExternalInput").ap()
    d["out"] = nc.dram_tensor("out_x", (D, S), F32, kind="ExternalOutput").ap()
    program(nc, d)
    r = _run(nc, [arrays], core_ids=[0])
    return np.ascontiguousarray(r.results[0]["out_x"].T)[None]
```

```python
from contextlib import ExitStack, contextmanager
from math import pi

import numpy as np
import concourse.bass as bass
from concourse import mybir

F32 = mybir.dt.float32
I32 = mybir.dt.int32
F32R = mybir.dt.float32r
ALU = mybir.AluOpType
ACT = mybir.ActivationFunctionType
AX = mybir.AxisListType

P = 128
S = 1024
NB = S // P
D = 1024
DC = D // P
HALF = 512
F_FF = 4 * D
SB_H, SB_D = 8, 64
MLA_H, NOPE, ROPE = 4, 128, 64
MLA_SCALE = float((NOPE + ROPE) ** -0.5)
Q_LORA, KV_LORA = 256, 128
MEM = 256
BW = 512
BT = BW // P
NBR = 5
CONVK, CONFK = 4, 31
EPS = 1e-6
NEG = -1e30

C_ID = 0
C_ONE = C_ID + P
C_GT = C_ONE + P
C_LE = C_GT + P
C_LT = C_LE + P
C_NGE = C_LT + P
C_NCAUSAL = C_NGE + P
C_LVL = C_NCAUSAL + P
C_FREQ = C_LVL + 7 * P
C_SGN = C_FREQ + 1
C_EPS = C_SGN + 1
C_QS = C_EPS + 1
C_W = C_QS + 8


def constants():
    p = np.arange(P)[:, None]
    f = np.arange(P)[None, :]
    c = np.zeros((P, C_W), np.float32)
    c[:, C_ID:C_ID + P] = p == f
    c[:, C_ONE:C_ONE + P] = 1
    c[:, C_GT:C_GT + P] = p > f
    c[:, C_LE:C_LE + P] = p <= f
    c[:, C_LT:C_LT + P] = p < f
    c[:, C_NGE:C_NGE + P] = np.where(p >= f, NEG, 0)
    c[:, C_NCAUSAL:C_NCAUSAL + P] = np.where(f > p, NEG, 0)
    for lvl in range(7):
        b = 1 << lvl
        same = (p // (2 * b)) == (f // (2 * b))
        c[:, C_LVL + lvl * P:C_LVL + (lvl + 1) * P] = same & (p % (2 * b) < b) & (f % (2 * b) >= b)
    half = ROPE // 2
    c[:, C_FREQ] = (10000.0 ** (-(np.arange(P) % half) / half)).astype(np.float32)
    c[:, C_SGN] = np.where(np.arange(P) % ROPE < half, -1, 1)
    c[:, C_EPS] = EPS
    c[:, C_QS:C_QS + 4] = 128.0 ** -0.5
    c[:, C_QS + 4:C_QS + 8] = 1
    return c


_PAR = [("attn_g", 8), ("q_a_g", 2), ("kv_a_g", 1), ("sb_g", 4), ("mla_g", 4), ("mlp_g", 8), ("final_g", 8),
        ("pre_g", 8), ("post_g", 8), ("mem_g", 8), ("b_in", 55), ("b_gate", 40), ("a_conv", 48), ("a_norm", 1),
        ("b_conv", 124), ("b_conv_b", 4), ("b_ln_g", 4), ("b_ln_b", 4), ("d_conv", 16), ("d_conv_b", 4),
        ("d_ba", 4), ("d_bx", 4), ("d_lam", 4), ("ab_bias", 8), ("a_log", 4), ("a_dt", 4), ("sinks", 8)]
PAR = {}
_at = 0
for _n, _w in _PAR:
    PAR[_n] = (_at, _w)
    _at += _w
PAR_W = _at

T_AQKV, T_DX, T_GLU = 0, 12, 16
T_AZ, T_BZ, T_CZ, T_DZ, T_EZ = 24, 28, 32, 36, 40
T_CQ, T_CK, T_CV, T_EQ = 44, 48, 50, 51
N_IN2 = 55

A_CONST = 0
A_PAR = A_CONST + C_W + -C_W % 8
A_SMALL = A_PAR + PAR_W + -PAR_W % 8
A_RES = A_SMALL + 80
A_SPLIT = A_RES + DC * S
A_WORK = A_SPLIT + 2 * DC * S
A_END = 52800
A_ACT = A_END - DC * S


class Split:

    def __init__(self, hi, lo):
        self.hi, self.lo = hi, lo

    def __getitem__(self, key):
        return Split(self.hi[key], self.lo[key])


class Mem:

    def __init__(self, nc):
        self.nc = nc
        self.base = nc.sbuf_base + (-nc.sbuf_base) % 32
        self.ps = nc.alloc_psum_tensor("psum", [P, 8, HALF], F32)[:, :, :]
        self.const = self.at("const", A_CONST, F32, C_W)
        self.par = self.at("par", A_PAR, F32, PAR_W)
        self.res = self.at("res", A_RES, F32, DC, S)
        self.act = self.at("act", A_ACT, F32, DC, S)
        small = self.at("small", A_SMALL, F32, 80)
        self.beta = small[:, 0:32].rearrange("p (c h) -> p c h", h=4)
        self.decay = small[:, 32:64].rearrange("p (c h) -> p c h", h=4)
        self.rate = small[:, 64:68]
        self.top, self.end = A_SPLIT, A_END
        self.split = self.take_split("normed", DC, S)

    def at(self, name, column, dtype, *shape):
        t = self.nc.alloc_sbuf_tensor_at(f"{name}_{self.nc.next_id()}", [P] + list(shape), dtype,
                                         offset=self.base + 4 * column)
        return t[(slice(None),) * (len(shape) + 1)]

    def c(self, at, w=P):
        return self.const[:, at:at + w]

    def p(self, name, k=0, w=1):
        at = PAR[name][0] + k
        return self.par[:, at:at + w]

    def clear(self, top=A_SPLIT, end=A_END):
        self.top, self.end = top, end

    def take(self, *shape):
        self.top += -self.top % 8
        v = self.at("buffer", self.top, F32, *shape)
        self.top += int(np.prod(shape))
        assert self.top <= self.end, self.top
        return v

    def take_split(self, name, *shape):
        n = int(np.prod(shape))
        self.top += -self.top % 8
        parts = [self.at(f"{name}_{part}", self.top + j * n, F32R, *shape) for j, part in enumerate(("hi", "lo"))]
        self.top += 2 * n
        assert self.top <= self.end, self.top
        return Split(*parts)


LN_EXP = "natural_log_exp_and_others"


@contextmanager
def phase(nc, *names):
    at = nc.next_id()
    sems = [nc.alloc_semaphore(f"{n}_{at}") for n in names]
    with nc.Block() as block:
        yield (block, *sems)
    nc.clear_and_free_semaphores(sems)
    nc.all_engine_barrier()


def loop(eng, n, body):
    body(0)
    with eng.Fori(1, n) as i:
        body(i)


def rounds_of_two(eng, n, body):
    for i in range(2):
        body(i, i)
    with eng.Fori(1, n // 2 - 1) as i:
        for s in range(2):
            body(2 * i + s, s)
    for i in range(n - 2, n):
        body(i, i % 2)


def is_first(i, below=1):
    return isinstance(i, int) and i < below


def is_last(i, n):
    return isinstance(i, int) and i == n - 1


def load_phase(nc, m, d):
    m.clear()
    pos_i = m.take(S)
    pos, ang, turns, red = m.take(S), m.take(S), m.take(S), m.take(2, S)
    tab = m.take(2, S)
    two_pi = (6.28125, 0.0019340515136718750, 2 * pi - 6.28125 - 0.0019340515136718750)
    lim = 3.1415925
    with phase(nc, "params_in", "x_in", "pos_in", "reduced", "sines", "signed", "tables_out") as (
            block, params_in, x_in, pos_in, reduced, sines, signed, tables_out):

        @block.sync
        def _(sp):
            sp.dma_start(m.const, d["consts"]).then_inc(params_in, 16)
            sp.dma_start(m.par, d["params"]).then_inc(params_in, 16)
            sp.dma_start(pos_i.bitcast(I32), d["positions"].partition_broadcast(P)).then_inc(pos_in, 16)
            sp.dma_start(m.res, d["x"].rearrange("(k p) t -> p k t", p=P)).then_inc(x_in, 16)
            sp.wait_ge(signed, 1)
            sp.dma_start(d["rope"].rearrange("a p t -> p a t"), tab).then_inc(tables_out, 16)
            sp.wait_ge(tables_out, 16)
            sp.wait_ge(x_in, 16)
            sp.wait_ge(params_in, 32)

        @block.vector
        def _(dve):
            n = [0]

            def step(ins):
                n[0] += 1
                ins.then_inc(reduced, 1)
                dve.wait_ge(reduced, n[0])

            dve.wait_ge(pos_in, 16)
            dve.wait_ge(params_in, 32)
            step(dve.tensor_copy(pos, pos_i.bitcast(I32)))
            step(dve.tensor_scalar(ang, pos, m.c(C_FREQ, 1), None, ALU.mult))
            magic = float(3 << 22)
            for j, shift in enumerate((0.25, 0.0)):
                step(dve.tensor_scalar(turns, ang, 1 / (2 * pi), shift, ALU.mult, ALU.add))
                step(dve.tensor_scalar(turns, turns, magic, None, ALU.add))
                step(dve.tensor_scalar(turns, turns, magic, None, ALU.subtract))
                step(dve.scalar_tensor_tensor(red[:, j], turns, -two_pi[0], ang, ALU.mult, ALU.add))
                step(dve.scalar_tensor_tensor(red[:, j], turns, -two_pi[1], red[:, j], ALU.mult, ALU.add))
                step(dve.scalar_tensor_tensor(red[:, j], turns, -two_pi[2], red[:, j], ALU.mult, ALU.add))
                if j == 0:
                    step(dve.tensor_scalar(red[:, j], red[:, j], pi / 2, None, ALU.add))
                step(dve.tensor_scalar(red[:, j], red[:, j], lim, -lim, ALU.min, ALU.max))
            dve.wait_ge(sines, 2)
            dve.tensor_scalar(tab[:, 1], tab[:, 1], m.c(C_SGN, 1), None, ALU.mult).then_inc(signed, 1)

        @block.scalar
        def _(act):
            act.wait_ge(reduced, 17)
            for j in range(2):
                act.activation(tab[:, j], red[:, j], ACT.Sin).then_inc(sines, 1)


def norm_phase(nc, m, src, dst, gain, kc, scratch, residual=None, spill=None, out=None):
    sq, root = scratch
    split = isinstance(dst, Split)
    plain = sq if split else None
    tot = m.ps[:, 0:2, :].rearrange("p a b -> p (a b)")
    with phase(nc, "squared", "added", "summed", "logged", "rooted", "scaled", "hi_done", "lo_even", "lo_odd",
               "spilled", "finished", "all_out") as (
            block, squared, added, summed, logged, rooted, scaled, hi_done, lo_even, lo_odd, spilled, finished, all_out):

        if spill is not None:
            @block.sync
            def _(sp):
                sp.dma_start(spill.rearrange("k p t -> p k t"), src).then_inc(spilled, 16)
                sp.wait_ge(spilled, 16)

        if out is not None:
            @block.sync
            def _(sp):
                for k in range(kc):
                    sp.wait_ge(finished, k + 1)
                    sp.dma_start(out[k * P:(k + 1) * P], dst[:, k]).then_inc(all_out, 16)
                sp.wait_ge(all_out, 16 * kc)

        @block.scalar
        def _(act):
            act.preload_act_table_set(LN_EXP)
            for k in range(kc):
                if k >= 2:
                    act.wait_ge(added, max(k - 2, 1))
                act.activation(sq[:, k % 2], src[:, k], ACT.Square).then_inc(squared, 1)
            act.wait_ge(summed, 1)
            act.activation(root, tot, ACT.Ln, bias=m.c(C_EPS, 1), scale=1.0 / (kc * P)).then_inc(logged, 1)
            act.wait_ge(logged, 1)
            act.activation(root, root, ACT.Exp, scale=-0.5).then_inc(rooted, 1)
            if split:
                for k in range(kc):
                    act.wait_ge(scaled, k + 1)
                    act.activation(dst.hi[:, k], plain[:, k % 2], ACT.Copy).then_inc(hi_done, 1)

        @block.tensor
        def _(pe):
            if kc > 1:
                pe.wait_ge(added, kc - 1)
            else:
                pe.wait_ge(squared, 1)
            total = root if kc > 1 else sq[:, 0]
            for h in range(2):
                mm = pe.matmul(halves(tot)[h], m.c(C_ONE), halves(total)[h], start=True, stop=True)
            mm.then_inc(summed, 1)

        def low(eng, k, done):
            eng.wait_ge(hi_done, k + 1)
            eng.tensor_tensor(dst.lo[:, k], plain[:, k % 2], dst.hi[:, k].bitcast(F32), ALU.subtract).then_inc(done, 1)

        if split and kc > 1:
            @block.gpsimd
            def _(pool):
                for k in range(1, kc, 2):
                    low(pool, k, lo_odd)

        @block.vector
        def _(dve):
            for k in range(1, kc):
                dve.wait_ge(squared, k + 1)
                if k >= 2:
                    dve.wait_ge(added, k - 1)
                dve.tensor_tensor(root, sq[:, 0] if k == 1 else root, sq[:, k % 2], ALU.add).then_inc(added, 1)
            dve.wait_ge(rooted, 1)
            for k in range(kc):
                if split and k >= 2:
                    dve.wait_ge(lo_odd if k % 2 else lo_even, k // 2)
                to = plain[:, k % 2] if split else dst[:, k]
                dve.scalar_tensor_tensor(to, src[:, k], gain[:, k:k + 1], root, ALU.mult, ALU.mult).then_inc(scaled, 1)
                if split and k % 2:
                    low(dve, k - 1, lo_even)
                if residual is not None:
                    dve.wait_ge(scaled, k + 1)
                    dve.tensor_tensor(dst[:, k], dst[:, k], residual[:, k], ALU.add).then_inc(finished, 1)
            if split and kc % 2:
                low(dve, kc - 1, lo_even)


def split_phase(nc, src, dst, kc):
    with phase(nc, "hi_done") as (block, hi_done):

        @block.scalar
        def _(act):
            for k in range(kc):
                act.activation(dst.hi[:, k], src[:, k], ACT.Copy).then_inc(hi_done, 1)

        @block.vector
        def _(dve):
            for k in range(kc):
                dve.wait_ge(hi_done, k + 1)
                dve.tensor_tensor(dst.lo[:, k], src[:, k], dst.hi[:, k].bitcast(F32), ALU.subtract)


def three_passes(pe, out, w, x, first, last):
    pe.matmul(out, w.hi, x.hi, start=first, stop=False)
    pe.matmul(out, w.hi, x.lo, start=False, stop=False)
    return pe.matmul(out, w.lo, x.hi, start=False, stop=last)


def halves(v):
    return [v[:, h * HALF:(h + 1) * HALF] for h in range(2)]


def gemm_phase(nc, m, w, src, kc, tiles, finish, bias=None, func=None, out=None, dst=None, tile0=0, reload=None):
    raw = m.take(2, kc, P)
    ws = m.take_split("w", 2, kc, P)
    tmp = m.take(2, S)
    ps = m.ps[:, 0:4, :].rearrange("p (s h) f -> p s (h f)", s=2)
    pairs = tiles // 2
    assert pairs >= 2
    with phase(nc, "weights_a", "weights_b", "w_hi", "w_lo", "product_done", "evacuated", "squared", "x_hi", "x_lo",
               "stored_a", "stored_b", "reloaded") as (
            block, weights_a, weights_b, w_hi, w_lo, product_done, evacuated, squared, x_hi, x_lo, stored_a, stored_b,
            reloaded):
        landed = (weights_a, weights_b)
        stored = (stored_a, stored_b)

        def rounds(eng, body):
            for s in range(2):
                body(0, s)
            if pairs > 2:
                with eng.Fori(1, pairs - 1) as i:
                    for s in range(2):
                        body(i, s)
            for j in range(2 * pairs - 2, tiles):
                body(j // 2, j % 2)

        def start(i):
            return isinstance(i, int) and i == 0

        @block.sync
        def _(sp):
            def load(i, s):
                if not start(i):
                    sp.wait_ge(w_lo, 2 * i + s - 1)
                sp.dma_start(raw[:, s].rearrange("p k f -> p (k f)"), w[2 * i + s]).then_inc(landed[s], 16)
            rounds(sp, load)
            if reload is not None:
                sp.dma_start(reload[0], reload[1].rearrange("k p t -> p k t")).then_inc(reloaded, 16)
                sp.wait_ge(reloaded, 16)

        @block.gpsimd
        def _(pool):
            def low(i, s):
                pool.wait_ge(w_hi, 2 * i + s + 1)
                pool.tensor_tensor(ws.lo[:, s], raw[:, s], ws.hi[:, s].bitcast(F32), ALU.subtract).then_inc(w_lo, 1)
            rounds(pool, low)

        @block.tensor
        def _(pe):
            def product(i, s):
                pe.wait_ge(w_lo, 2 * i + s + 1)
                if not start(i):
                    pe.wait_ge(evacuated, 2 * i + s - 1)
                for k in range(kc):
                    first, last = k == 0, k == kc - 1
                    hi, lo, x = ws.hi[:, s, k], ws.lo[:, s, k], src[:, k]
                    for h, bank in enumerate(halves(ps[:, s])):
                        pe.matmul(bank, hi, halves(x.hi)[h], start=first, stop=False)
                        pe.matmul(bank, hi, halves(x.lo)[h], start=False, stop=False)
                    for h, bank in enumerate(halves(ps[:, s])):
                        mm = pe.matmul(bank, lo, halves(x.hi)[h], start=False, stop=last)
                mm.then_inc(product_done, 1)
            rounds(pe, product)

        @block.scalar
        def _(act):
            def high(i, s):
                act.wait_ge(landed[s], 16 * i + 16)
                if not start(i):
                    act.wait_ge(product_done, 2 * i + s - 1)
                act.activation(ws.hi[:, s], raw[:, s], ACT.Copy).then_inc(w_hi, 1)

            def finish_tile(i, s):
                j = 2 * i + s
                if finish == "store" or finish == "keep":
                    act.wait_ge(product_done, j + 1)
                    if finish == "store" and not start(i):
                        act.wait_ge(stored[s], 16 * i)
                    to = tmp[:, s] if finish == "store" else dst[:, j]
                    if bias is None:
                        act.activation(to, ps[:, s], func or ACT.Copy).then_inc(evacuated, 1)
                    else:
                        act.activation(to, ps[:, s], func or ACT.Identity,
                                       bias=bias[:, bass.ds(j, 1)]).then_inc(evacuated, 1)

            def tile(i, s):
                finish_tile(i, s)
                if not (isinstance(i, int) and 2 * i + s + 2 >= tiles):
                    high(i + 1, s)
                if finish == "store":
                    act.wait_ge(evacuated, 2 * i + s + 1)
                    act.dma_start(out[2 * i + s + tile0], tmp[:, s]).then_inc(stored[s], 16)

            high(0, 0)
            high(0, 1)
            rounds(act, tile)
            if finish == "store":
                act.wait_ge(stored[0], 16 * ((tiles + 1) // 2))
                act.wait_ge(stored[1], 16 * (tiles // 2))

        if finish == "add":
            @block.vector
            def _(dve):
                def add(i, s):
                    dve.wait_ge(product_done, 2 * i + s + 1)
                    dve.tensor_tensor(dst[:, 2 * i + s], ps[:, s], dst[:, 2 * i + s], ALU.add).then_inc(evacuated, 1)
                rounds(dve, add)


def product_of(pe, banks, w, x, kc, before=None):
    for k in range(kc):
        if before is not None:
            before(k)
        first, last = k == 0, k == kc - 1
        for h, bank in enumerate(halves(banks)):
            pe.matmul(bank, w.hi[:, k], halves(x.hi[:, k])[h], start=first, stop=False)
            pe.matmul(bank, w.hi[:, k], halves(x.lo[:, k])[h], start=False, stop=False)
        for h, bank in enumerate(halves(banks)):
            mm = pe.matmul(bank, w.lo[:, k], halves(x.hi[:, k])[h], start=False, stop=last)
    return mm


def mlp_phase(nc, m, w, parts):
    H = DC
    T = 2 * H
    hidden = m.take_split("hidden", H, S)
    raw = m.take(2, DC, P)
    ws = m.take_split("w", 2, DC, P)
    tmp = m.take(2, S)
    ps = m.ps[:, 0:4, :].rearrange("p (s h) f -> p s (h f)", s=2)
    with phase(nc, "weights_a", "weights_b", "w_hi", "w_lo", "product_done", "relu_done", "squared", "h_hi", "h_lo",
               "add_done") as (
            block, weights_a, weights_b, w_hi, w_lo, product_done, relu_done, squared, h_hi, h_lo, add_done):
        landed = (weights_a, weights_b)

        def start(n, u):
            return isinstance(n, int) and n == 0 and u < 2

        @block.sync
        def _(sp):
            def part(n):
                for u in range(T):
                    if not start(n, u):
                        sp.wait_ge(w_lo, n * T + u - 1)
                    sp.dma_start(raw[:, u % 2].rearrange("p k f -> p (k f)"), w[n * T + u]).then_inc(landed[u % 2], 16)
            loop(sp, parts, part)

        @block.gpsimd
        def _(pool):
            def part(n):
                for u in range(T):
                    s = u % 2
                    pool.wait_ge(w_hi, n * T + u + 1)
                    pool.tensor_tensor(ws.lo[:, s], raw[:, s], ws.hi[:, s].bitcast(F32), ALU.subtract).then_inc(w_lo, 1)
            loop(pool, parts, part)

        @block.tensor
        def _(pe):
            def part(n):
                def hidden_ready(k):
                    pe.wait_ge(h_lo, n * H + k + 1)

                for u in range(T):
                    s = u % 2
                    pe.wait_ge(w_lo, n * T + u + 1)
                    if u < 2 and not start(n, u):
                        pe.wait_ge(add_done, n * H + u - 1)
                    elif 2 <= u < H + 2:
                        pe.wait_ge(relu_done, n * H + u - 1)
                    elif u >= H + 2:
                        pe.wait_ge(add_done, n * H + u - H - 1)
                    if u < H:
                        mm = product_of(pe, ps[:, s], ws[:, s], m.split, DC)
                    else:
                        mm = product_of(pe, ps[:, s], ws[:, s], hidden, H, hidden_ready if u == H else None)
                    mm.then_inc(product_done, 1)
            loop(pe, parts, part)

        @block.scalar
        def _(act):
            def high(n, u):
                s = u % 2
                act.wait_ge(landed[s], 16 * (n * H + u // 2) + 16)
                if not start(n, u):
                    act.wait_ge(product_done, n * T + u - 1)
                act.activation(ws.hi[:, s], raw[:, s], ACT.Copy).then_inc(w_hi, 1)

            def part(n, more=True):
                for u in range(T):
                    s = u % 2
                    if u < H:
                        act.wait_ge(product_done, n * T + u + 1)
                        if not start(n, u):
                            act.wait_ge(h_lo, n * H + u - 1)
                        act.activation(tmp[:, s], ps[:, s], ACT.Relu).then_inc(relu_done, 1)
                    if more or u + 2 < T:
                        high(n, u + 2)
            high(0, 0)
            high(0, 1)
            part(0)
            with act.Fori(1, parts - 1) as n:
                part(n)
            part(parts - 1, False)

        @block.vector
        def _(dve):
            def part(n):
                for u in range(H):
                    s, j = u % 2, n * H + u
                    dve.wait_ge(relu_done, j + 1)
                    dve.tensor_tensor(tmp[:, s], tmp[:, s], tmp[:, s], ALU.mult).then_inc(squared, 1)
                    dve.wait_ge(squared, j + 1)
                    dve.tensor_copy(hidden.hi[:, u], tmp[:, s]).then_inc(h_hi, 1)
                    dve.wait_ge(h_hi, j + 1)
                    dve.tensor_tensor(hidden.lo[:, u], tmp[:, s], hidden.hi[:, u].bitcast(F32), ALU.subtract).then_inc(h_lo, 1)
                for u in range(H):
                    dve.wait_ge(product_done, n * T + H + u + 1)
                    if not isinstance(n, int):
                        dve.wait_ge(add_done, n * H + u - H + 1)
                    dve.tensor_tensor(m.res[:, u], ps[:, u % 2], m.res[:, u], ALU.add).then_inc(add_done, 1)
            loop(dve, parts, part)


def rows_phase(nc, m, src, kc, w, width, tiles, out=None, dst=None):
    split = isinstance(src, Split)
    wt = m.take(kc, width)
    ws = m.take_split("w", kc, width) if split else None
    res = dst if out is None else m.take(tiles, width)
    with phase(nc, "weights_in", "w_hi", "w_lo", "rows_done", "rows_kept", "rows_out") as (
            block, weights_in, w_hi, w_lo, rows_done, rows_kept, rows_out):

        @block.sync
        def _(sp):
            sp.dma_start(wt, w).then_inc(weights_in, 16)
            if out is not None:
                sp.wait_ge(rows_kept, tiles)
                sp.dma_start(out.rearrange("i p f -> p i f"), res).then_inc(rows_out, 16)
                sp.wait_ge(rows_out, 16)

        @block.tensor
        def _(pe):
            pe.wait_ge(weights_in, 16)
            if split:
                pe.wait_ge(w_lo, kc)
            for i in range(tiles):
                if i >= 4:
                    pe.wait_ge(rows_kept, i - 3)
                bank = m.ps[:, i % 4, 0:width]
                for k in range(kc):
                    first, last = k == 0, k == kc - 1
                    x = src[:, k, i * P:(i + 1) * P]
                    if split:
                        mm = three_passes(pe, bank, x, ws[:, k], first, last)
                    else:
                        mm = pe.matmul(bank, x, wt[:, k], start=first, stop=last)
                mm.then_inc(rows_done, 1)

        @block.vector
        def _(dve):
            if split:
                for k in range(kc):
                    dve.wait_ge(w_hi, k + 1)
                    dve.tensor_tensor(ws.lo[:, k], wt[:, k], ws.hi[:, k].bitcast(F32), ALU.subtract).then_inc(w_lo, 1)

        @block.scalar
        def _(act):
            if split:
                act.wait_ge(weights_in, 16)
                for k in range(kc):
                    act.activation(ws.hi[:, k], wt[:, k], ACT.Copy).then_inc(w_hi, 1)
            for i in range(tiles):
                act.wait_ge(rows_done, i + 1)
                act.activation(res[:, i], m.ps[:, i % 4, 0:width], ACT.Copy).then_inc(rows_kept, 1)


def stick_phase(nc, m, d):
    m.clear(end=A_ACT)
    q, k, v = m.take(S), m.take(S), m.take(NB, P)
    soft, sp_, lsg, aw = m.take(3, HALF), m.take(4, HALF), m.take(3, HALF), m.take(3, HALF)
    steps = []
    for g in range(2):
        for kb in range(4 * g + 3, -1, -1):
            for e in range(2):
                steps.append((e, g, kb, P * max(0, kb - 4 * g)))
    T = len(steps)
    pairs = SB_H // 2
    carried = np.cumsum([kb > 0 for _, _, kb, _ in steps]).tolist()
    ended = np.cumsum([kb == 0 for _, _, kb, _ in steps]).tolist()
    masked = np.cumsum([kb >= 4 * g for _, g, kb, _ in steps]).tolist()
    fixes = masked[-1]

    def diag(t):
        return steps[t][2] >= 4 * steps[t][1]

    with phase(nc, "staged", "q_scaled", "z_done", "abs_done", "exp_done", "ln_done", "raw_done", "sp_ready",
               "lsg_ready", "later_done", "arg_ready", "carry_done", "a_ready", "av_done", "o_kept") as (
            block, staged, q_scaled, z_done, abs_done, exp_done, ln_done, raw_done, sp_ready,
            lsg_ready, later_done, arg_ready, carry_done, a_ready, av_done, o_kept):

        @block.sync
        def _(sp):
            def body(i):
                sp.wait_ge(z_done, i * T)
                sp.wait_ge(av_done, i * T)
                sp.dma_start(q, d["in1"][i]).then_inc(staged, 16)
                sp.dma_start(k, d["in1"][i + pairs]).then_inc(staged, 16)
                sp.dma_start(v, d["v_sb"][:, :, bass.ds(i * P, P)].rearrange("b p f -> p b f")).then_inc(staged, 16)
            loop(sp, pairs, body)

        @block.tensor
        def _(pe):
            def body(i):
                b = i * T
                pe.wait_ge(staged, 48 * i + 48)
                pe.wait_ge(q_scaled, i + 1)
                for t in range(T + 4):
                    if t < T:
                        e, g, kb, c0 = steps[t]
                        pe.wait_ge(lsg_ready, b + max(t - 2, 0))
                        pe.matmul(m.ps[:, t % 3, c0:HALF], k[64 * e:64 * e + 64, kb * P:(kb + 1) * P],
                                  q[64 * e:64 * e + 64, g * HALF + c0:(g + 1) * HALF],
                                  start=True, stop=True).then_inc(z_done, 1)
                    if 0 <= t - 2 < T:
                        e, g, kb, c0 = steps[t - 2]
                        pe.wait_ge(sp_ready, b + t - 1)
                        pe.wait_ge(arg_ready, b + max(t - 3, 0))
                        pe.matmul(m.ps[:, 3 + e, c0:HALF], m.c(C_GT), sp_[:, (t - 2) % 4, c0:HALF],
                                  start=(kb == 4 * g + 3), stop=False, skip_group_check=True).then_inc(later_done, 1)
                    if 0 <= t - 3 < T and steps[t - 3][2] > 0:
                        e, g, kb, c0 = steps[t - 3]
                        pe.wait_ge(arg_ready, b + t - 2)
                        pe.matmul(m.ps[:, 3 + e, c0:HALF], m.c(C_LE), sp_[:, (t - 3) % 4, c0:HALF],
                                  start=False, stop=False, skip_group_check=True).then_inc(carry_done, 1)
                    if 0 <= t - 4 < T:
                        e, g, kb, c0 = steps[t - 4]
                        pe.wait_ge(a_ready, b + t - 3)
                        if kb == 4 * g + 3:
                            pe.wait_ge(o_kept, i * 4 + (2 * g - 2 + e + 1 if g else 0))
                        mm = pe.matmul(m.ps[64 * e:64 * e + 64, 5 + e, c0:HALF], v[:, kb, 64 * e:64 * e + 64],
                                       aw[:, (t - 4) % 3, c0:HALF], start=(kb == 4 * g + 3), stop=(kb == 0),
                                       skip_group_check=True)
                        mm.then_inc(av_done, 1)
            loop(pe, pairs, body)

        @block.scalar
        def _(act):
            act.preload_act_table_set(LN_EXP)

            def body(i):
                b = i * T
                act.wait_ge(staged, 48 * i + 48)
                act.activation(q, q, ACT.Copy, scale=float(SB_D ** -0.5)).then_inc(q_scaled, 1)
                for t in range(T + 2):
                    if t < T:
                        c0 = steps[t][3]
                        x = soft[:, t % 3, c0:HALF]
                        act.wait_ge(z_done, b + t + 1)
                        act.activation(x, m.ps[:, t % 3, c0:HALF], ACT.Abs).then_inc(abs_done, 1)
                        act.wait_ge(abs_done, b + t + 1)
                        act.activation(x, x, ACT.Exp, scale=-1.0).then_inc(exp_done, 1)
                        act.wait_ge(exp_done, b + t + 1)
                        act.activation(x, x, ACT.Ln, bias=1.0).then_inc(ln_done, 1)
                    if 0 <= t - 2 < T:
                        c0 = steps[t - 2][3]
                        act.wait_ge(arg_ready, b + t - 1)
                        act.wait_ge(av_done, b + max(t - 4, 0))
                        act.activation(aw[:, (t - 2) % 3, c0:HALF], lsg[:, (t - 2) % 3, c0:HALF],
                                       ACT.Exp).then_inc(a_ready, 1)
            loop(act, pairs, body)

        @block.vector
        def _(dve):
            def body(i):
                b = i * T
                for t in range(T + 6):
                    if 0 <= t - 1 < T:
                        u = t - 1
                        c0 = steps[u][3]
                        z = m.ps[:, u % 3, c0:HALF]
                        ln = soft[:, u % 3, c0:HALF]
                        dve.wait_ge(ln_done, b + u + 1)
                        dve.wait_ge(later_done, b + max(u - 3, 0))
                        dve.wait_ge(carry_done, i * carried[-1] + (carried[u - 4] if u >= 4 else 0))
                        dve.wait_ge(a_ready, b + max(u - 2, 0))
                        one = dve.scalar_tensor_tensor(sp_[:, u % 4, c0:HALF], z, 0.0, ln, ALU.max, ALU.add)
                        one.then_inc(raw_done if diag(u) else sp_ready, 1)
                        two = dve.scalar_tensor_tensor(lsg[:, u % 3, c0:HALF], z, 0.0, ln, ALU.min, ALU.subtract)
                        two.then_inc(raw_done if diag(u) else lsg_ready, 1)
                        if diag(u):
                            own = slice(c0, c0 + P)
                            dve.wait_ge(raw_done, i * 2 * fixes + 2 * masked[u])
                            dve.tensor_tensor(sp_[:, u % 4, own], sp_[:, u % 4, own], m.c(C_LT),
                                              ALU.mult).then_inc(sp_ready, 1)
                            dve.tensor_tensor(lsg[:, u % 3, own], lsg[:, u % 3, own], m.c(C_NGE),
                                              ALU.add).then_inc(lsg_ready, 1)
                    if 0 <= t - 2 < T:
                        u = t - 2
                        e, g, kb, c0 = steps[u]
                        dve.wait_ge(later_done, b + u + 1)
                        dve.wait_ge(lsg_ready, b + u + 1)
                        x = lsg[:, u % 3, c0:HALF]
                        dve.tensor_tensor(x, x, m.ps[:, 3 + e, c0:HALF], ALU.subtract).then_inc(arg_ready, 1)
                    if 0 <= t - 5 < T and steps[t - 5][2] == 0:
                        e, g, kb, c0 = steps[t - 5]
                        dve.wait_ge(av_done, b + t - 4)
                        rows = slice(64 * e, 64 * e + 64)
                        dve.tensor_copy(m.act[rows, i, g * HALF:(g + 1) * HALF], m.ps[rows, 5 + e, :]).then_inc(o_kept, 1)
            loop(dve, pairs, body)


def rope_phase(nc, m, plain, swapped, tab, tiles, out, rows):
    res = m.take(tiles, S)
    t1 = m.take(tiles, S)
    with phase(nc, "cos_done", "sin_done", "turned", "rope_out") as (block, cos_done, sin_done, turned, rope_out):

        @block.vector
        def _(dve):
            for j in range(tiles):
                dve.tensor_tensor(res[:, j], plain[:, j], tab[:, 0], ALU.mult).then_inc(cos_done, 1)
                dve.tensor_tensor(t1[:, j], swapped[:, j], tab[:, 1], ALU.mult).then_inc(sin_done, 1)
                dve.wait_ge(cos_done, j + 1)
                dve.wait_ge(sin_done, j + 1)
                dve.tensor_tensor(res[:, j], res[:, j], t1[:, j], ALU.add).then_inc(turned, 1)

        @block.sync
        def _(sp):
            for j in range(tiles):
                sp.wait_ge(turned, j + 1)
                sp.dma_start(out[j * P:j * P + rows], res[0:rows, j]).then_inc(rope_out, 16)
            sp.wait_ge(rope_out, 16 * tiles)


def latent_phases(nc, m, d):
    m.clear(end=A_ACT)
    low = m.take(5, S)
    normed = m.take_split("low", 3, S)
    tab = m.take(2, S)
    scratch = (m.take(2, S), m.take(S))
    with phase(nc, "low_in") as (block, low_in):
        @block.sync
        def _(sp):
            sp.dma_start(low, d["in1"][8:13].rearrange("a p t -> p a t")).then_inc(low_in, 16)
            sp.dma_start(tab, d["rope"].rearrange("a p t -> p a t")).then_inc(low_in, 16)
            sp.wait_ge(low_in, 32)
    norm_phase(nc, m, low[:, 0:2], normed[:, 0:2], m.p("q_a_g", 0, 2), 2, scratch)
    norm_phase(nc, m, low[:, 2:3], normed[:, 2:3], m.p("kv_a_g", 0, 1), 1, scratch)
    base = m.top
    rope_phase(nc, m, low[:, 3:4], low[:, 4:5], tab, 1, d["k_rope"], ROPE)
    m.top = base
    gemm_phase(nc, m, d["w_qn"], normed[:, 0:2], 2, 4, "store", out=d["mla_q"])
    m.top = base
    qr = m.take(4, S)
    gemm_phase(nc, m, d["w_qr"], normed[:, 0:2], 2, 4, "keep", dst=qr)
    rope_phase(nc, m, qr[:, 0:2], qr[:, 2:4], tab, 2, d["q_rope"], P)
    m.top = base
    gemm_phase(nc, m, d["w_kn"], normed[:, 2:3], 1, 4, "store", out=d["mla_k"])
    m.top = base
    rows_phase(nc, m, normed[:, 2:3], 1, d["w_vm"], BW, NB, d["mla_v"])


def latent_attention_phase(nc, m, d):
    m.clear(end=A_ACT)
    qn, kn, v = m.take(2, S), m.take(2, S), m.take(2, NB, P)
    qr, kr = m.take(2, S), m.take(S)
    pr = m.take(2, S)
    pt = m.take(2, S)
    mx, nm, rs, ri = (m.take(2 * NB) for _ in range(4))
    T = 2 * NB

    def scores(t):
        return m.ps[:, 2 * (t % 2):2 * (t % 2) + 2, :].rearrange("p a f -> p (a f)")
    turned = m.ps[:, 4:6, :].rearrange("p a f -> p (a f)")

    with phase(nc, "kr_in", "staged_a", "staged_b", "s_done", "diag_masked", "max_done", "negated", "p_ready", "inverted",
               "p_scaled", "t_done", "t_kept", "o_done", "o_kept") as (
            block, kr_in, staged_a, staged_b, s_done, diag_masked, max_done, negated, p_ready, inverted,
            p_scaled, t_done, t_kept, o_done, o_kept):
        staged = (staged_a, staged_b)

        @block.sync
        def _(sp):
            sp.dma_start(kr[0:ROPE], d["k_rope"]).then_inc(kr_in, 16)

            def body(i):
                for g in range(2):
                    if not (isinstance(i, int) and i == 0):
                        sp.wait_ge(o_done, i * T - T + (g + 1) * NB)
                    h = 2 * i + g
                    sp.dma_start(qn[:, g], d["mla_q"][h]).then_inc(staged[g], 16)
                    sp.dma_start(kn[:, g], d["mla_k"][h]).then_inc(staged[g], 16)
                    sp.dma_start(qr[0:ROPE, g], d["q_rope"][bass.ds(h * ROPE, ROPE)]).then_inc(staged[g], 16)
                    sp.dma_start(v[:, g], d["mla_v"][:, :, bass.ds(h * P, P)].rearrange("b p f -> p b f")).then_inc(staged[g], 16)
            loop(sp, MLA_H // 2, body)

        @block.tensor
        def _(pe):
            pe.wait_ge(kr_in, 16)

            def body(i):
                b = i * T
                for t in range(T + 2):
                    if t < T:
                        g, q = t // NB, t % NB
                        if q == 0:
                            pe.wait_ge(staged[g], 64 * i + 64)
                        pe.wait_ge(p_ready, b + max(t - 1, 0))
                        n = (q + 1) * P
                        for c in range(0, n, HALF):
                            w = min(HALF, n - c)
                            pe.matmul(scores(t)[:, c:c + w], qn[:, g, q * P:(q + 1) * P], kn[:, g, c:c + w],
                                      start=True, stop=False)
                            mm = pe.matmul(scores(t)[:, c:c + w], qr[0:ROPE, g, q * P:(q + 1) * P], kr[0:ROPE, c:c + w],
                                           start=False, stop=True)
                        mm.then_inc(s_done, 1)
                    if 0 <= t - 1 < T:
                        u = t - 1
                        pe.wait_ge(p_scaled, b + u + 1)
                        pe.wait_ge(t_kept, b + u)
                        for kb in range(u % NB + 1):
                            mm = pe.transpose(turned[:, kb * P:(kb + 1) * P], pr[:, u % 2, kb * P:(kb + 1) * P],
                                              m.c(C_ID))
                        mm.then_inc(t_done, 1)
                    if 0 <= t - 2 < T:
                        u = t - 2
                        pe.wait_ge(t_kept, b + u + 1)
                        pe.wait_ge(o_kept, b + max(u - 1, 0))
                        for kb in range(u % NB + 1):
                            mm = pe.matmul(m.ps[:, 6 + u % 2, 0:P], v[:, u // NB, kb], pt[:, u % 2, kb * P:(kb + 1) * P],
                                           start=(kb == 0), stop=(kb == u % NB))
                        mm.then_inc(o_done, 1)
            loop(pe, MLA_H // 2, body)

        @block.vector
        def _(dve):
            def body(i):
                b = i * T
                for t in range(T + 3):
                    if t < T:
                        q = t % NB
                        dve.wait_ge(s_done, b + t + 1)
                        own = scores(t)[:, q * P:(q + 1) * P]
                        dve.tensor_tensor(own, own, m.c(C_NCAUSAL), ALU.add).then_inc(diag_masked, 1)
                        dve.wait_ge(diag_masked, b + t + 1)
                        dve.wait_ge(negated, b + t)
                        dve.tensor_reduce(mx[:, t:t + 1], scores(t)[:, 0:(q + 1) * P], AX.X, ALU.max).then_inc(max_done, 1)
                        dve.wait_ge(max_done, b + t + 1)
                        dve.wait_ge(p_ready, b + t)
                        dve.tensor_scalar(nm[:, t:t + 1], mx[:, t:t + 1], -MLA_SCALE, None, ALU.mult).then_inc(negated, 1)
                        dve.wait_ge(p_ready, b + t + 1)
                        dve.wait_ge(p_scaled, b + t)
                        dve.reciprocal(ri[:, t:t + 1], rs[:, t:t + 1]).then_inc(inverted, 1)
                        dve.wait_ge(inverted, b + t + 1)
                        x = pr[:, t % 2, 0:(q + 1) * P]
                        dve.tensor_scalar(x, x, ri[:, t:t + 1], None, ALU.mult).then_inc(p_scaled, 1)
                    if 0 <= t - 3 < T:
                        u = t - 3
                        dve.wait_ge(o_done, b + u + 1)
                        dve.tensor_copy(m.act[:, 4 + 2 * i + u // NB, u % NB * P:(u % NB + 1) * P],
                                        m.ps[:, 6 + u % 2, 0:P]).then_inc(o_kept, 1)
            loop(dve, MLA_H // 2, body)

        @block.scalar
        def _(act):
            def body(i):
                b = i * T
                for t in range(T + 1):
                    if t < T:
                        act.wait_ge(negated, b + t + 1)
                        act.wait_ge(t_done, b + max(t - 1, 0))
                        n = (t % NB + 1) * P
                        act.wait_ge(inverted, b + max(t - 1, 0))
                        act.activation(pr[:, t % 2, 0:n], scores(t)[:, 0:n], ACT.Exp, bias=nm[:, t:t + 1],
                                       scale=MLA_SCALE, accum_out=rs[:, t:t + 1]).then_inc(p_ready, 1)
                    if 0 <= t - 1 < T:
                        u = t - 1
                        n = (u % NB + 1) * P
                        act.wait_ge(t_done, b + u + 1)
                        act.wait_ge(o_done, b + max(u - 1, 0))
                        act.activation(pt[:, u % 2, 0:n], turned[:, 0:n], ACT.Copy).then_inc(t_kept, 1)
            loop(act, MLA_H // 2, body)


def beta_alpha_phase(nc, m, d, ab):
    n = 8
    wt = m.take(DC, n)
    ws = m.take_split("w", DC, n)
    flat = m.take(S)
    ps = m.ps[0:n, 0:2, :].rearrange("p b f -> p (b f)")
    turned = m.ps[:, 2, 0:NB * n]
    with phase(nc, "weights_in", "w_hi", "w_lo", "product_done", "kept", "turn_done", "rows_kept") as (
            block, weights_in, w_hi, w_lo, product_done, kept, turn_done, rows_kept):

        @block.sync
        def _(sp):
            sp.dma_start(wt, d["w_ab"]).then_inc(weights_in, 16)

        @block.vector
        def _(dve):
            dve.wait_ge(w_hi, 1)
            dve.tensor_tensor(ws.lo, wt, ws.hi.bitcast(F32), ALU.subtract).then_inc(w_lo, 1)

        @block.scalar
        def _(act):
            act.wait_ge(weights_in, 16)
            act.activation(ws.hi, wt, ACT.Copy).then_inc(w_hi, 1)
            act.wait_ge(product_done, 1)
            act.activation(flat[0:n], ps, ACT.Copy).then_inc(kept, 1)
            act.wait_ge(turn_done, 1)
            act.activation(ab, turned.rearrange("p (c f) -> p c f", f=n), ACT.Copy).then_inc(rows_kept, 1)

        @block.tensor
        def _(pe):
            pe.wait_ge(w_lo, 1)
            product_of(pe, ps, ws, m.split, DC).then_inc(product_done, 1)
            pe.wait_ge(kept, 1)
            for c in range(NB):
                mm = pe.transpose(turned[:, c * n:(c + 1) * n], flat[0:n, c * P:(c + 1) * P], m.c(C_ID)[0:n, 0:n])
            mm.then_inc(turn_done, 1)


def small_phase(nc, m, ab):
    n = NB * 4
    x, e, w, w2, acc, ea = (m.take(n + 4) for _ in range(6))
    ones8 = (1, NB, 4)
    with phase(nc, "biased", "sig_done", "abs_done", "exp_done", "alog_done", "chain") as (
            block, biased, sig_done, abs_done, exp_done, alog_done, chain):

        @block.scalar
        def _(act):
            act.wait_ge(biased, 1)
            act.activation(m.beta, ab[:, :, 0:4], ACT.Sigmoid).then_inc(sig_done, 1)
            act.activation(ea[:, 0:4], m.p("a_log", 0, 4), ACT.Exp).then_inc(alog_done, 1)
            act.wait_ge(biased, 3)
            act.activation(e, x, ACT.Abs).then_inc(abs_done, 1)
            act.wait_ge(abs_done, 1)
            act.activation(e, e, ACT.Exp, scale=-1.0).then_inc(exp_done, 1)

        @block.vector
        def _(dve):
            count = [0]

            def step(ins):
                count[0] += 1
                ins.then_inc(chain, 1)
                dve.wait_ge(chain, count[0])

            dve.tensor_tensor(ab, ab, m.p("ab_bias", 0, 8).unsqueeze(1).to_broadcast([P, NB, 8]),
                              ALU.add).then_inc(biased, 1)
            dve.wait_ge(biased, 1)
            dve.tensor_tensor(x[:, 0:n].rearrange("p (c h) -> p c h", h=4), ab[:, :, 4:8],
                              m.p("a_dt", 0, 4).unsqueeze(1).to_broadcast([P, NB, 4]), ALU.add).then_inc(biased, 1)
            dve.tensor_scalar(x[:, n:n + 4], m.p("d_lam", 0, 4), -1.0, None, ALU.mult).then_inc(biased, 1)
            dve.wait_ge(exp_done, 1)
            step(dve.tensor_scalar(w, e, 2.0, None, ALU.add))
            step(dve.reciprocal(w, w))
            step(dve.tensor_tensor(w, w, e, ALU.mult))
            step(dve.tensor_tensor(w2, w, w, ALU.mult))
            step(dve.tensor_scalar(acc, w2, 1 / 17, 1 / 15, ALU.mult, ALU.add))
            for k in range(13, 0, -2):
                step(dve.tensor_tensor(acc, acc, w2, ALU.mult))
                step(dve.tensor_scalar(acc, acc, 1 / k, None, ALU.add))
            step(dve.scalar_tensor_tensor(acc, acc, 2.0, w, ALU.mult, ALU.mult))
            step(dve.scalar_tensor_tensor(acc, x, 0.0, acc, ALU.max, ALU.add))
            step(dve.tensor_scalar(m.rate, acc[:, n:n + 4], 8.0, None, ALU.mult))
            dve.wait_ge(alog_done, 1)
            step(dve.scalar_tensor_tensor(m.decay, acc[:, 0:n].rearrange("p (c h) -> p c h", h=4), -1.0,
                                          ea[:, 0:4].unsqueeze(1).to_broadcast([P, NB, 4]), ALU.mult, ALU.mult))


def conv(dve, x, acc, taps, n_taps, bias, chain, count):
    for k in range(n_taps):
        if k == 0 and bias is None:
            ins = dve.tensor_scalar(acc, x[:, 0:S], taps[:, 0:1], None, ALU.mult)
        elif k == 0:
            ins = dve.tensor_scalar(acc, x[:, 0:S], taps[:, 0:1], bias, ALU.mult, ALU.add)
        else:
            dve.wait_ge(chain, count + k)
            ins = dve.scalar_tensor_tensor(acc, x[:, k:k + S], taps[:, k:k + 1], acc, ALU.mult, ALU.add)
        ins.then_inc(chain, 1)


def in2_phase(nc, m, d, y):
    pad, wide_pad = CONVK - 1, CONFK - 1
    N_CONV, N_KEEP, N_SILU = T_GLU, 2 * BT, T_CQ - T_AZ
    first_silu, first_plain = T_AZ, T_CQ
    assert T_DX % 2 == 0 and N_CONV % 2 == 0 and first_silu == N_CONV + N_KEEP and first_plain % 2 == 0
    raw = m.take(2, DC, P)
    ws = m.take_split("w", 2, DC, P)
    res = m.take(2, S)
    x = m.take(2, S + pad)
    glu = m.take(N_KEEP, S)
    u = m.take(2, S + wide_pad)
    ps = m.ps[:, 0:4, :].rearrange("p (s h) f -> p s (h f)", s=2)
    bias = m.p("b_in", 0, N_IN2)
    with phase(nc, "weights_a", "weights_b", "w_hi", "w_lo", "product_done", "evacuated", "stored_a", "stored_b",
               "zeroed", "short_chain", "silu_done", "glu_done", "long_chain") as (
            block, weights_a, weights_b, w_hi, w_lo, product_done, evacuated, stored_a, stored_b,
            zeroed, short_chain, silu_done, glu_done, long_chain):
        landed, stored = (weights_a, weights_b), (stored_a, stored_b)

        def rounds(eng, body, base, tiles):
            with eng.Fori(base // 2, (base + tiles) // 2) as i:
                for s in range(2):
                    body(2 * i + s, s)
            if tiles % 2:
                body(base + tiles - 1, 0)

        def all_rounds(eng, body):
            body(0, 0)
            body(1, 1)
            rounds(eng, body, 2, N_IN2 - 2)

        def start(j):
            return isinstance(j, int) and j < 2

        def turns(j, s):
            return j // 2 if isinstance(j, int) else (j - s) // 2

        @block.sync
        def _(sp):
            def load(i, s, j):
                if not start(j):
                    sp.wait_ge(w_lo, j - 1)
                sp.dma_start(raw[:, s].rearrange("p k f -> p (k f)"), d["w_in2"][j]).then_inc(landed[s], 16)
            all_rounds(sp, lambda j, s: load(None, s, j))

        @block.gpsimd
        def _(pool):
            def low(j, s):
                pool.wait_ge(w_hi, j + 1)
                pool.tensor_tensor(ws.lo[:, s], raw[:, s], ws.hi[:, s].bitcast(F32), ALU.subtract).then_inc(w_lo, 1)
            all_rounds(pool, low)

        @block.tensor
        def _(pe):
            def product(j, s):
                pe.wait_ge(w_lo, j + 1)
                if not start(j):
                    pe.wait_ge(evacuated, j - 1)
                product_of(pe, ps[:, s], ws[:, s], m.split, DC).then_inc(product_done, 1)
            all_rounds(pe, product)

        @block.scalar
        def _(act):
            def high(i, s):
                act.wait_ge(landed[s], 16 * i + 16)
                if not (isinstance(i, int) and i == 0):
                    act.wait_ge(product_done, 2 * i + s - 1)
                act.activation(ws.hi[:, s], raw[:, s], ACT.Copy).then_inc(w_hi, 1)

            def evacuate(i, s, to, func):
                j = 2 * i + s
                act.wait_ge(product_done, j + 1)
                act.activation(to, ps[:, s], func, bias=bias[:, bass.ds(j, 1)]).then_inc(evacuated, 1)
                if not (isinstance(i, int) and j + 2 >= N_IN2):
                    high(i + 1, s)

            def convolved(i, s):
                j = 2 * i + s
                act.wait_ge(short_chain, CONVK * j + CONVK)
                if not isinstance(j, int) or j < T_DX:
                    act.activation(res[:, s], res[:, s], ACT.Silu).then_inc(silu_done, 1)
                    act.wait_ge(silu_done, j + 1)
                act.dma_start(d["in2"][j], res[:, s]).then_inc(stored[s], 16)

            def short(i, s):
                if not (isinstance(i, int) and i == 0):
                    act.wait_ge(short_chain, CONVK * (2 * i + s) - CONVK)
                evacuate(i, s, x[:, s, pad:pad + S], ACT.Identity)
                if s == 1:
                    convolved(i, 0)
                elif not (isinstance(i, int) and i == 0):
                    convolved(i - 1, 1)

            def straight(func, gone):
                def body(i, s):
                    act.wait_ge(stored[s], 16 * i - 16 * gone)
                    evacuate(i, s, res[:, s], func)
                    act.wait_ge(evacuated, 2 * i + s + 1)
                    act.dma_start(d["in2"][2 * i + s], res[:, s]).then_inc(stored[s], 16)
                return body

            act.wait_ge(zeroed, 2)
            high(0, 0)
            high(0, 1)
            for s in range(2):
                short(0, s)
            with act.Fori(1, T_DX // 2) as i:
                for s in range(2):
                    short(i, s)
            for j in range(T_DX, N_CONV):
                short(j // 2, j % 2)
            convolved(N_CONV // 2 - 1, 1)
            for j in range(N_CONV, first_silu):
                k = j - N_CONV
                evacuate(j // 2, j % 2, glu[:, k], ACT.Identity if k < BT else ACT.Sigmoid)
            silu = straight(ACT.Silu, N_KEEP // 2)
            with act.Fori(first_silu // 2, first_plain // 2) as i:
                for s in range(2):
                    silu(i, s)
            plain = straight(ACT.Identity, N_KEEP // 2)
            with act.Fori(first_plain // 2, N_IN2 // 2 - 1) as i:
                for s in range(2):
                    plain(i, s)
            for j in range(N_IN2 // 2 * 2 - 2, N_IN2):
                plain(j // 2, j % 2)
            for s in range(2):
                act.wait_ge(stored[s], 16 * ((N_IN2 - N_KEEP + 1 - s) // 2))

        @block.vector
        def _(dve):
            for s in range(2):
                dve.memset(x[:, s, 0:pad], 0.0).then_inc(zeroed, 1)
            for j in range(N_CONV):
                s = j % 2
                dve.wait_ge(evacuated, j + 1)
                if j < 2:
                    dve.wait_ge(zeroed, 2)
                else:
                    dve.wait_ge(stored[s], 16 * (j // 2))
                if j < T_DX:
                    taps, tap_bias = m.p("a_conv", j * CONVK, CONVK), None
                else:
                    taps, tap_bias = m.p("d_conv", (j - T_DX) * CONVK, CONVK), m.p("d_conv_b", j - T_DX)
                conv(dve, x[:, s], res[:, s], taps, CONVK, tap_bias, short_chain, j * CONVK)
            for s in range(2):
                dve.memset(u[:, s, 0:wide_pad], 0.0).then_inc(zeroed, 1)
            dve.wait_ge(zeroed, 4)
            for j in range(BT):
                dve.wait_ge(evacuated, N_CONV + BT + j + 1)
                dve.tensor_tensor(u[:, j % 2, wide_pad:wide_pad + S], glu[:, j], glu[:, BT + j], ALU.mult).then_inc(glu_done, 1)
                dve.wait_ge(glu_done, j + 1)
                conv(dve, u[:, j % 2], y[:, j], m.p("b_conv", j * CONFK, CONFK), CONFK, m.p("b_conv_b", j), long_chain,
                     j * CONFK)


def delta_norm_phase(nc, m, d):
    m.clear()
    tiles = 2 * BT
    y = m.take(tiles, S)
    sq, root = m.take(2, S), m.take(2, S)
    ps = m.ps.rearrange("p (s h) f -> p s (h f)", s=4)
    with phase(nc, "y_a", "y_b", "squared", "summed", "logged", "rooted", "normed", "all_out") as (
            block, y_a, y_b, squared, summed, logged, rooted, normed, all_out):

        @block.sync
        def _(sp):
            for h, y_in in enumerate((y_a, y_b)):
                sp.dma_start(y[:, h * BT:(h + 1) * BT],
                             d["in2"][T_AQKV + h * BT:T_AQKV + (h + 1) * BT].rearrange("c p t -> p c t")).then_inc(y_in, 16)
            for j in range(tiles):
                sp.wait_ge(normed, j + 1)
                sp.dma_start(d["delta"][j], y[:, j]).then_inc(all_out, 16)
            sp.wait_ge(all_out, 16 * tiles)

        @block.vector
        def _(dve):
            for j in range(tiles):
                dve.wait_ge(rooted, j + 1)
                dve.scalar_tensor_tensor(y[:, j], y[:, j], m.c(C_QS + j, 1), root[:, j % 2], ALU.mult,
                                         ALU.mult).then_inc(normed, 1)

        @block.scalar
        def _(act):
            act.preload_act_table_set(LN_EXP)

            def root_of(j):
                act.wait_ge(summed, j + 1)
                if j >= 2:
                    act.wait_ge(normed, j - 1)
                act.activation(root[:, j % 2], ps[:, j % 4], ACT.Ln, bias=m.c(C_EPS, 1)).then_inc(logged, 1)
                act.wait_ge(logged, j + 1)
                act.activation(root[:, j % 2], root[:, j % 2], ACT.Exp, scale=-0.5).then_inc(rooted, 1)
            for j in range(tiles):
                if j == 0:
                    act.wait_ge(y_a, 16)
                if j == BT:
                    act.wait_ge(y_b, 16)
                if j >= 2:
                    act.wait_ge(summed, j - 1)
                act.activation(sq[:, j % 2], y[:, j], ACT.Square).then_inc(squared, 1)
                if j >= 1:
                    root_of(j - 1)
            root_of(tiles - 1)

        @block.tensor
        def _(pe):
            for j in range(tiles):
                pe.wait_ge(squared, j + 1)
                if j >= 4:
                    pe.wait_ge(logged, j - 3)
                for h in range(2):
                    mm = pe.matmul(ps[:, j % 4, h * HALF:(h + 1) * HALF], m.c(C_ONE),
                                   sq[:, j % 2, h * HALF:(h + 1) * HALF], start=True, stop=True)
                mm.then_inc(summed, 1)


def heads(v):
    return v.rearrange("p (h f) -> p h f", h=4)


def wide(column):
    return column.unsqueeze(2).to_broadcast([P, 4, P])


def over_heads(square):
    return square.unsqueeze(1).to_broadcast([P, 4, P])


def delta_prepare_phase(nc, m, d, at, attn, qd, last):
    base = m.top
    staging = m.take(2, 3 * BT, P)
    gw, bw, gd, lt, eg = (m.take(BW) for _ in range(5))
    rows = m.take(3, BW)
    gc, egc, kx, bg = (m.take(4) for _ in range(4))
    bank = [m.ps[:, n, :] for n in range(8)]
    with phase(nc, "staged_a", "staged_b", "spread_g", "spread_b", "sums_done", "rows_done", "products_done", "picked", "g_col",
               "diff_done", "clamped", "l_exp", "l_masked", "eg_done", "egc_done", "kx_diff", "kx_done", "bg_done",
               "a_half", "a_done", "attn_done", "qd_done", "last_done", "k1", "k2", "v1", "rows_out") as (
            block, staged_a, staged_b, spread_g, spread_b, sums_done, rows_done, products_done, picked, g_col,
            diff_done, clamped, l_exp, l_masked, eg_done, egc_done, kx_diff, kx_done, bg_done,
            a_half, a_done, attn_done, qd_done, last_done, k1, k2, v1, rows_out):

        staged = (staged_a, staged_b)

        @block.sync
        def _(sp):
            def stage(c, s):
                if not is_first(c, 2):
                    sp.wait_ge(products_done, c - 1)
                    sp.wait_ge(rows_done, c - 1)
                    sp.wait_ge(qd_done, c - 1)
                sp.dma_start(staging[:, s, 0:2 * BT], d["delta"][:, :, bass.ds(c * P, P)].rearrange("a p t -> p a t")).then_inc(staged[s], 16)
                sp.dma_start(staging[:, s, 2 * BT:3 * BT], d["in2"][T_AQKV + 2 * BT:T_AQKV + 3 * BT, :, bass.ds(c * P, P)].rearrange(
                    "a p t -> p a t")).then_inc(staged[s], 16)

            def body(c, s):
                if not is_last(c, NB):
                    stage(c + 1, 1 - s)
                sp.wait_ge(k1, c + 1)
                sp.wait_ge(k2, c + 1)
                sp.wait_ge(v1, c + 1)
                sp.dma_start(d["kv_rows"][c], rows.rearrange("p a f -> p (a f)")).then_inc(rows_out, 16)
            stage(0, 0)
            rounds_of_two(sp, NB, body)
            sp.wait_ge(rows_out, 16 * NB)

        @block.tensor
        def _(pe):
            def body(c, s):
                st = staging[:, s]
                pe.wait_ge(spread_g, c + 1)
                if not is_first(c):
                    pe.wait_ge(eg_done, c)
                if not is_first(c):
                    pe.wait_ge(diff_done, c)
                if not is_first(c):
                    pe.wait_ge(last_done, c)
                if not is_first(c):
                    pe.wait_ge(kx_diff, c)
                for h in range(4):
                    pe.matmul(bank[2][:, h * P:(h + 1) * P], heads(gw)[:, h], m.c(C_LE), start=True, stop=True)
                pe.wait_ge(spread_b, c + 1)
                if not is_first(c):
                    pe.wait_ge(a_done, c)
                for h in range(4):
                    mm = pe.matmul(bank[3][:, h * P:(h + 1) * P], heads(bw)[:, h], m.c(C_ID), start=True, stop=True)
                mm.then_inc(sums_done, 1)
                pe.wait_ge(staged[s], 16 * (c - s) + 32)
                if not is_first(c):
                    pe.wait_ge(k1, c)
                if not is_first(c):
                    pe.wait_ge(k2, c)
                if not is_first(c):
                    pe.wait_ge(v1, c)
                for h in range(4):
                    pe.transpose(bank[0][:, h * P:(h + 1) * P], st[:, BT + h], m.c(C_ID))
                for h in range(4):
                    mm = pe.transpose(bank[1][:, h * P:(h + 1) * P], st[:, 2 * BT + h], m.c(C_ID))
                mm.then_inc(rows_done, 1)
                if not is_first(c):
                    pe.wait_ge(attn_done, c)
                for h in range(4):
                    pe.matmul(bank[4][:, h * P:(h + 1) * P], st[:, BT + h], st[:, BT + h], start=True, stop=True)
                for h in range(4):
                    mm = pe.matmul(bank[5][:, h * P:(h + 1) * P], st[:, BT + h], st[:, h], start=True, stop=True)
                mm.then_inc(products_done, 1)
            rounds_of_two(pe, NB, body)

        @block.vector
        def _(dve):
            def body(c, s):
                st = staging[:, s]
                if not is_first(c):
                    dve.wait_ge(sums_done, c)
                dve.tensor_tensor(heads(gw), over_heads(m.c(C_ONE)), wide(m.decay[:, c]), ALU.mult).then_inc(spread_g, 1)
                dve.tensor_tensor(heads(bw), over_heads(m.c(C_ONE)), wide(m.beta[:, c]), ALU.mult).then_inc(spread_b, 1)
                dve.wait_ge(sums_done, c + 1)
                dve.tensor_tensor(heads(gd), heads(bank[2]), over_heads(m.c(C_ID)), ALU.mult).then_inc(picked, 1)
                dve.wait_ge(picked, c + 1)
                if not is_first(c):
                    dve.wait_ge(egc_done, c)
                dve.tensor_reduce(gc, heads(gd), AX.X, ALU.add).then_inc(g_col, 1)
                dve.wait_ge(g_col, c + 1)
                dve.tensor_tensor(heads(lt), heads(bank[2]), wide(gc), ALU.subtract).then_inc(diff_done, 1)
                g_last = heads(bank[2])[:, :, P - 1]
                if not is_first(c):
                    dve.wait_ge(kx_done, c)
                dve.tensor_tensor(kx, g_last, gc, ALU.subtract).then_inc(kx_diff, 1)
                dve.wait_ge(diff_done, c + 1)
                dve.tensor_scalar(lt, lt, 0.0, None, ALU.min).then_inc(clamped, 1)
                dve.wait_ge(eg_done, c + 1)
                dve.tensor_copy(last[:, c], heads(eg)[:, :, P - 1]).then_inc(last_done, 1)
                dve.wait_ge(egc_done, c + 1)
                if not is_first(c):
                    dve.wait_ge(k1, c)
                dve.tensor_tensor(bg, egc, m.beta[:, c], ALU.mult).then_inc(bg_done, 1)
                dve.wait_ge(l_exp, c + 1)
                dve.tensor_tensor(heads(lt), heads(lt), over_heads(m.c(C_LE)), ALU.mult).then_inc(l_masked, 1)
                dve.wait_ge(l_masked, c + 1)
                dve.wait_ge(products_done, c + 1)
                dve.tensor_tensor(at[:, c], bank[4], lt, ALU.mult).then_inc(a_half, 1)
                dve.tensor_tensor(attn[:, c], bank[5], lt, ALU.mult).then_inc(attn_done, 1)
                dve.wait_ge(a_half, c + 1)
                dve.tensor_tensor(at[:, c], at[:, c], bank[3], ALU.mult).then_inc(a_done, 1)
                dve.tensor_tensor(heads(qd[:, c]), st[:, 0:BT], heads(eg), ALU.mult).then_inc(qd_done, 1)
                if not is_first(c):
                    dve.wait_ge(rows_out, 16 * c)
                dve.wait_ge(bg_done, c + 1)
                dve.wait_ge(rows_done, c + 1)
                dve.tensor_tensor(heads(rows[:, 0]), heads(bank[0]), wide(bg), ALU.mult).then_inc(k1, 1)
                dve.wait_ge(kx_done, c + 1)
                dve.tensor_tensor(heads(rows[:, 1]), heads(bank[0]), wide(kx), ALU.mult).then_inc(k2, 1)
                dve.tensor_tensor(heads(rows[:, 2]), heads(bank[1]), wide(m.beta[:, c]), ALU.mult).then_inc(v1, 1)
            rounds_of_two(dve, NB, body)

        @block.scalar
        def _(act):
            def body(c):
                act.wait_ge(g_col, c + 1)
                act.wait_ge(bg_done, c)
                act.activation(egc, gc, ACT.Exp).then_inc(egc_done, 1)
                act.wait_ge(kx_diff, c + 1)
                act.activation(kx, kx, ACT.Exp).then_inc(kx_done, 1)
                act.wait_ge(diff_done, c + 1)
                act.wait_ge(qd_done, c)
                act.wait_ge(last_done, c)
                act.activation(eg, bank[2], ACT.Exp).then_inc(eg_done, 1)
                act.wait_ge(clamped, c + 1)
                act.activation(lt, lt, ACT.Exp).then_inc(l_exp, 1)
            loop(act, NB, body)
    m.top = base


def delta_inverse_phase(nc, m, at, inv, inv_t):
    base = m.top
    masked = m.take(4, 2 * BW)
    mid = m.take(4, 2 * BW)
    groups = 4

    def pair(v, g):
        return v[:, 2 * g:2 * g + 2].rearrange("p c f -> p (c f)")

    def eight(v):
        return v.rearrange("p (n f) -> p n f", f=P)

    def spread(square):
        return square.unsqueeze(1).to_broadcast([P, 8, P])

    def banks(b):
        return m.ps[:, b:b + 2, :].rearrange("p b f -> p (b f)")

    with phase(nc, "a_masked", "mid_done", "mid_kept", "low_done", "up_done", "low_kept", "up_kept") as (
            block, a_masked, mid_done, mid_kept, low_done, up_done, low_kept, up_kept):

        @block.vector
        def _(dve):
            for g in range(groups):
                dve.tensor_tensor(eight(masked[:, g]), eight(pair(at, g)), spread(m.c(C_LVL)), ALU.mult).then_inc(a_masked, 1)
            for g in range(groups):
                dve.wait_ge(mid_done, g + 1)
                dve.tensor_tensor(eight(pair(inv, g)), spread(m.c(C_ID)), eight(banks(2 * (g % 2))), ALU.subtract).then_inc(low_kept, 1)
                dve.tensor_tensor(eight(pair(inv_t, g)), spread(m.c(C_ID)), eight(masked[:, g]), ALU.subtract).then_inc(up_kept, 1)
            with dve.Fori(1, 7) as lvl:
                b = lvl * groups
                mask = m.const[:, C_LVL:C_LVL + 7 * P].rearrange("p (l f) -> p l f", f=P)[:, lvl]
                for g in range(groups):
                    dve.wait_ge(mid_done, b - groups + g + 1)
                    dve.wait_ge(up_kept, b - groups + g + 1)
                    dve.tensor_tensor(eight(masked[:, g]), eight(pair(at, g)), spread(mask), ALU.mult).then_inc(a_masked, 1)
                for g in range(groups):
                    dve.wait_ge(low_kept, b - groups + g + 1)
                    dve.wait_ge(low_done, b - groups + g + 1)
                    dve.tensor_tensor(pair(inv, g), pair(inv, g), banks(4), ALU.subtract).then_inc(low_kept, 1)
                    dve.wait_ge(up_done, b - groups + g + 1)
                    dve.tensor_tensor(pair(inv_t, g), pair(inv_t, g), banks(6), ALU.subtract).then_inc(up_kept, 1)

        @block.tensor
        def _(pe):
            def first(g, b):
                for n in range(8):
                    right = m.c(C_ID) if b is None else pair(inv, g)[:, n * P:(n + 1) * P]
                    mm = pe.matmul(banks(2 * (g % 2))[:, n * P:(n + 1) * P], masked[:, g, n * P:(n + 1) * P], right,
                                   start=True, stop=True)
                mm.then_inc(mid_done, 1)

            for g in range(groups):
                pe.wait_ge(a_masked, g + 1)
                if g >= 2:
                    pe.wait_ge(low_kept, g - 1)
                first(g, None)
            pe.wait_ge(low_kept, groups)
            with pe.Fori(1, 7) as lvl:
                b = lvl * groups
                for g in range(groups + 1):
                    if g < groups:
                        pe.wait_ge(a_masked, b + g + 1)
                        pe.wait_ge(low_kept, b - groups + g + 1)
                        if g >= 2:
                            pe.wait_ge(mid_kept, b - groups + g - 1)
                        first(g, b)
                    if g >= 1:
                        u = g - 1
                        pe.wait_ge(mid_kept, b - groups + u + 1)
                        pe.wait_ge(up_kept, b - groups + u + 1)
                        pe.wait_ge(low_kept, b + u)
                        for n in range(8):
                            cut = slice(n * P, (n + 1) * P)
                            mm = pe.matmul(banks(4)[:, cut], pair(inv_t, u)[:, cut], mid[:, u, cut], start=True, stop=True)
                        mm.then_inc(low_done, 1)
                        pe.wait_ge(up_kept, b + u)
                        for n in range(8):
                            cut = slice(n * P, (n + 1) * P)
                            mm = pe.matmul(banks(6)[:, cut], mid[:, u, cut], pair(inv_t, u)[:, cut], start=True, stop=True)
                        mm.then_inc(up_done, 1)

        @block.scalar
        def _(act):
            with act.Fori(1, 7) as lvl:
                b = lvl * groups
                for g in range(groups):
                    act.wait_ge(mid_done, b + g + 1)
                    act.activation(mid[:, g], banks(2 * (g % 2)), ACT.Copy).then_inc(mid_kept, 1)
    m.top = base


def delta_scan_phase(nc, m, d, attn, qd, inv_t, last, o):
    base = m.top
    N = NB
    rows = m.take(2, 3, BW)
    tt, nw, state = m.take(2, BW), m.take(2, BW), m.take(2, BW)
    vn = m.take(BW)
    w_ps, v_ps, o_ps, kv_ps = (m.ps[:, n, :] for n in range(4))

    def h_(v, h):
        return v[:, h * P:(h + 1) * P]

    with phase(nc, "rows_a", "rows_b", "inv_copied", "w_done", "w_kept", "v_done", "v_kept", "kv_done", "o_done",
               "o_kept", "state_ready") as (
            block, rows_a, rows_b, inv_copied, w_done, w_kept, v_done, v_kept, kv_done, o_done, o_kept, state_ready):
        rows_in = (rows_a, rows_b)

        @block.sync
        def _(sp):
            def body(c, s):
                if not is_first(c, 2):
                    sp.wait_ge(o_done, c - 1)
                sp.dma_start(rows[:, s].rearrange("p a f -> p (a f)"), d["kv_rows"][c]).then_inc(rows_in[s], 16)
            rounds_of_two(sp, N, body)

        @block.scalar
        def _(act):
            def inverse(c, s):
                if not is_first(c, 2):
                    act.wait_ge(v_done, c - 1)
                act.activation(tt[:, s], inv_t[:, c], ACT.Copy).then_inc(inv_copied, 1)

            def negative(c, s):
                act.wait_ge(w_done, c + 1)
                act.activation(nw[:, s], w_ps, ACT.Copy, scale=-1.0).then_inc(w_kept, 1)

            def body(c, s):
                if not is_last(c, N):
                    inverse(c + 1, 1 - s)
                act.wait_ge(v_done, c + 1)
                if not is_first(c):
                    act.wait_ge(o_done, c)
                act.activation(vn, v_ps, ACT.Copy).then_inc(v_kept, 1)
                if not is_last(c, N):
                    negative(c + 1, 1 - s)
            inverse(0, 0)
            negative(0, 0)
            rounds_of_two(act, N, body)

        @block.tensor
        def _(pe):
            def w(c, s):
                pe.wait_ge(rows_in[s], 8 * (c - s) + 16)
                pe.wait_ge(inv_copied, c + 1)
                if not is_first(c):
                    pe.wait_ge(w_kept, c)
                for h in range(4):
                    mm = pe.matmul(h_(w_ps, h), h_(rows[:, s, 0], h), h_(tt[:, s], h), start=True, stop=True)
                mm.then_inc(w_done, 1)

            def body(c, s):
                pe.wait_ge(w_kept, c + 1)
                if not is_first(c):
                    pe.wait_ge(v_kept, c)
                pe.wait_ge(state_ready, 4 * c + 4)
                for h in range(4):
                    pe.matmul(h_(v_ps, h), h_(tt[:, s], h), h_(rows[:, s, 2], h), start=True, stop=False)
                    mm = pe.matmul(h_(v_ps, h), h_(nw[:, s], h), h_(state[:, s], h), start=False, stop=True)
                mm.then_inc(v_done, 1)
                if not is_last(c, N):
                    w(c + 1, 1 - s)
                pe.wait_ge(v_kept, c + 1)
                for h in range(4):
                    mm = pe.matmul(h_(kv_ps, h), h_(rows[:, s, 1], h), h_(vn, h), start=True, stop=True)
                mm.then_inc(kv_done, 1)
                if not is_first(c):
                    pe.wait_ge(o_kept, c)
                for h in range(4):
                    pe.matmul(h_(o_ps, h), h_(state[:, s], h), qd[:, c, h * P:(h + 1) * P], start=True, stop=False)
                    mm = pe.matmul(h_(o_ps, h), h_(vn, h), attn[:, c, h * P:(h + 1) * P], start=False, stop=True)
                mm.then_inc(o_done, 1)
            w(0, 0)
            rounds_of_two(pe, N, body)

        @block.vector
        def _(dve):
            dve.memset(state[:, 0], 0.0).then_inc(state_ready, 4)

            def body(c, s):
                dve.wait_ge(kv_done, c + 1)
                dve.wait_ge(state_ready, 4 * c + 4)
                if not is_first(c):
                    dve.wait_ge(o_done, c)
                for h in range(4):
                    dve.scalar_tensor_tensor(h_(state[:, 1 - s], h), h_(state[:, s], h), last[:, c, h:h + 1], h_(kv_ps, h),
                                             ALU.mult, ALU.add).then_inc(state_ready, 1)
                dve.wait_ge(o_done, c + 1)
                dve.tensor_copy(o[:, :, bass.ds(c * P, P)], heads(o_ps)).then_inc(o_kept, 1)
            rounds_of_two(dve, N, body)
    m.top = base


def gated_store_phase(nc, m, d, src, scale, root, gate_tile, y_tile):
    z = m.take(BT, S)
    with phase(nc, "z_in", "scaled", "gated", "y_out") as (block, z_in, scaled, gated, y_out):

        @block.sync
        def _(sp):
            sp.dma_start(z, d["in2"][gate_tile:gate_tile + BT].rearrange("c p t -> p c t")).then_inc(z_in, 16)
            for j in range(BT):
                sp.wait_ge(gated, j + 1)
                sp.dma_start(d["y"][y_tile + j], z[:, j]).then_inc(y_out, 16)
            sp.wait_ge(y_out, 16 * BT)

        @block.vector
        def _(dve):
            dve.wait_ge(z_in, 16)
            for j in range(BT):
                if root is None:
                    dve.tensor_tensor(z[:, j], z[:, j], src[:, j], ALU.mult).then_inc(gated, 1)
                else:
                    dve.scalar_tensor_tensor(src[:, j], src[:, j], scale(j), root[:, j], ALU.mult,
                                             ALU.mult).then_inc(scaled, 1)
                    dve.wait_ge(scaled, j + 1)
                    dve.tensor_tensor(z[:, j], z[:, j], src[:, j], ALU.mult).then_inc(gated, 1)


def tile_roots_phase(nc, m, src, root, count):
    sq = m.take(2, S)
    ps = m.ps.rearrange("p (s h) f -> p s (h f)", s=4)
    with phase(nc, "squared", "summed", "logged", "rooted") as (block, squared, summed, logged, rooted):

        @block.scalar
        def _(act):
            act.preload_act_table_set(LN_EXP)
            for j in range(count):
                if j >= 2:
                    act.wait_ge(summed, j - 1)
                act.activation(sq[:, j % 2], src[:, j], ACT.Square).then_inc(squared, 1)
            for j in range(count):
                act.wait_ge(summed, j + 1)
                act.activation(root[:, j], ps[:, j], ACT.Ln, bias=m.c(C_EPS, 1), scale=1.0 / P).then_inc(logged, 1)
            for j in range(count):
                act.wait_ge(logged, j + 1)
                act.activation(root[:, j], root[:, j], ACT.Exp, scale=-0.5).then_inc(rooted, 1)

        @block.tensor
        def _(pe):
            for j in range(count):
                pe.wait_ge(squared, j + 1)
                for h in range(2):
                    mm = pe.matmul(ps[:, j, h * HALF:(h + 1) * HALF], m.c(C_ONE),
                                   sq[:, j % 2, h * HALF:(h + 1) * HALF], start=True, stop=True)
                mm.then_inc(summed, 1)


def delta_phases(nc, m, d):
    delta_norm_phase(nc, m, d)
    m.clear()
    at, attn, qd = (m.take(NB, BW) for _ in range(3))
    inv, inv_t = m.take(NB, BW), m.take(NB, BW)
    last = m.take(NB, 4)
    delta_prepare_phase(nc, m, d, at, attn, qd, last)
    delta_inverse_phase(nc, m, at, inv, inv_t)
    o = inv.rearrange("p c f -> p (c f)").rearrange("p (h t) -> p h t", h=4)
    delta_scan_phase(nc, m, d, attn, qd, inv_t, last, o)
    root = at.rearrange("p c f -> p (c f)").rearrange("p (h t) -> p h t", h=4)
    base = m.top
    tile_roots_phase(nc, m, o, root, BT)
    m.top = base
    gated_store_phase(nc, m, d, o, lambda j: m.p("a_norm", 0, 1), root, T_AZ, 0)


def conformer_phase(nc, m, d, y):
    sq, root = m.take(2, S), m.take(S)
    z = m.take(BT, S)
    mean = m.ps[:, 0:2, :].rearrange("p a f -> p (a f)")
    var = m.ps[:, 2:4, :].rearrange("p a f -> p (a f)")
    with phase(nc, "z_in", "mean_done", "centred", "squared", "var_done", "logged", "rooted", "scaled", "silu_done",
               "gated", "y_out") as (
            block, z_in, mean_done, centred, squared, var_done, logged, rooted, scaled, silu_done, gated, y_out):

        @block.sync
        def _(sp):
            sp.dma_start(z, d["in2"][T_BZ:T_BZ + BT].rearrange("c p t -> p c t")).then_inc(z_in, 16)
            for j in range(BT):
                sp.wait_ge(gated, j + 1)
                sp.dma_start(d["y"][BT + j], z[:, j]).then_inc(y_out, 16)
            sp.wait_ge(y_out, 16 * BT)

        @block.scalar
        def _(act):
            act.preload_act_table_set(LN_EXP)
            for j in range(BT):
                act.wait_ge(centred, j + 1)
                if j >= 2:
                    act.wait_ge(var_done, j - 1)
                act.activation(sq[:, j % 2], y[:, j], ACT.Square).then_inc(squared, 1)
            act.wait_ge(var_done, BT)
            act.activation(root, var, ACT.Ln, bias=m.c(C_EPS, 1), scale=1.0 / BW).then_inc(logged, 1)
            act.wait_ge(logged, 1)
            act.activation(root, root, ACT.Exp, scale=-0.5).then_inc(rooted, 1)
            for j in range(BT):
                act.wait_ge(scaled, j + 1)
                act.activation(y[:, j], y[:, j], ACT.Silu, bias=m.p("b_ln_b", j)).then_inc(silu_done, 1)

        @block.vector
        def _(dve):
            dve.wait_ge(mean_done, 1)
            for j in range(BT):
                dve.scalar_tensor_tensor(y[:, j], mean, -1.0 / BW, y[:, j], ALU.mult, ALU.add).then_inc(centred, 1)
            dve.wait_ge(rooted, 1)
            for j in range(BT):
                dve.scalar_tensor_tensor(y[:, j], y[:, j], m.p("b_ln_g", j), root, ALU.mult, ALU.mult).then_inc(scaled, 1)
            dve.wait_ge(z_in, 16)
            for j in range(BT):
                dve.wait_ge(silu_done, j + 1)
                dve.tensor_tensor(z[:, j], z[:, j], y[:, j], ALU.mult).then_inc(gated, 1)

        @block.tensor
        def _(pe):
            for j in range(BT):
                for h in range(2):
                    mm = pe.matmul(mean[:, h * HALF:(h + 1) * HALF], m.c(C_ONE), y[:, j, h * HALF:(h + 1) * HALF],
                                   start=(j == 0), stop=(j == BT - 1))
            mm.then_inc(mean_done, 1)
            for j in range(BT):
                pe.wait_ge(squared, j + 1)
                for h in range(2):
                    mm = pe.matmul(var[:, h * HALF:(h + 1) * HALF], m.c(C_ONE), sq[:, j % 2, h * HALF:(h + 1) * HALF],
                                   start=(j == 0), stop=(j == BT - 1))
                mm.then_inc(var_done, 1)


def bucket_ranges():
    n = np.arange(P)
    exact, buckets, far = 16, 32, 128
    large = exact + (np.log(np.maximum(n, 1) / exact) / np.log(far / exact) * (buckets - exact)).astype(np.int32)
    b = np.where(n < exact, n, np.minimum(large, buckets - 1))
    return [(int(v), int(np.argmax(b == v)), int(P - np.argmax(b[::-1] == v))) for v in sorted(set(b.tolist()))]


def recurrence_keys_phase(nc, m, d, bias, bias0, mem_k, mem_v):
    wa, wx = m.take(BT, P), m.take(BT, P)
    xc, r, ig, th, a = (m.take(BT, S) for _ in range(5))
    root = xc
    z = r
    neg = m.take(4)
    ps = m.ps.rearrange("p (s h) f -> p s (h f)", s=4)
    rel, row = m.take(32), m.take(384)
    ranges = bucket_ranges()
    mem = m.take(DC, MEM)
    mem_sq, mem_root = m.take(2, MEM), m.take(MEM)
    wt = m.take(BT, DC * P)
    wv = m.take(DC, BW)
    with phase(nc, "w_in", "x_in", "z_in", "negated", "r_product", "x_product", "r_done", "i_done", "a_done", "t_done",
               "weighed", "ln_done", "inv_root", "t_root", "half_b", "b_done", "scanned", "gated", "y_out",
               "rel_in", "cleared", "placed", "row_out", "band_in", "first_done",
               "mem_in", "mem_w_in", "squared", "summed", "logged", "rooted", "scaled", "k_done", "v_done", "kv_kept") as (
            block, w_in, x_in, z_in, negated, r_product, x_product, r_done, i_done, a_done, t_done,
            weighed, ln_done, inv_root, t_root, half_b, b_done, scanned, gated, y_out,
            rel_in, cleared, placed, row_out, band_in, first_done,
            mem_in, mem_w_in, squared, summed, logged, rooted, scaled, k_done, v_done, kv_kept):

        @block.sync
        def _(sp):
            sp.dma_start(rel[0:8], d["rel_bias"]).then_inc(rel_in, 16)
            sp.dma_start(mem, d["mem"].rearrange("(k p) t -> p k t", p=P)).then_inc(mem_in, 16)
            sp.dma_start(wa, d["w_da"]).then_inc(w_in, 16)
            sp.dma_start(wx, d["w_dx"]).then_inc(w_in, 16)
            for j in range(BT):
                sp.dma_start(xc[:, j], d["in2"][T_DX + j]).then_inc(x_in, 16)
            sp.wait_ge(placed, len(ranges))
            sp.dma_start(d["band"], row[0:8].unsqueeze(1).to_broadcast([8, P, 384])).then_inc(row_out, 16)
            sp.dma_start(wt, d["w_mk"].rearrange("c p f -> p c f")).then_inc(mem_w_in, 16)
            sp.dma_start(wv, d["w_mv"]).then_inc(mem_w_in, 16)
            sp.wait_ge(row_out, 16)
            for h in range(8):
                src = bass.AP(d["band"].tensor, h * P * 384 + P - 1, [[383, P], [1, 2 * P]])
                sp.dma_start(bias[:, h], src).then_inc(band_in, 16)
            sp.wait_ge(a_done, BT)
            sp.wait_ge(t_done, BT)
            sp.dma_start(z, d["in2"][T_DZ:T_DZ + BT].rearrange("c p t -> p c t")).then_inc(z_in, 16)
            for j in range(BT):
                sp.wait_ge(gated, j + 1)
                sp.dma_start(d["y"][3 * BT + j], z[:, j]).then_inc(y_out, 16)
            sp.wait_ge(y_out, 16 * BT)
            sp.wait_ge(band_in, 128)

        @block.tensor
        def _(pe):
            for k in range(DC):
                pe.wait_ge(squared, k + 1)
                pe.matmul(m.ps[:, 0, 0:MEM], m.c(C_ONE), mem_sq[:, k % 2], start=(k == 0), stop=(k == DC - 1)).then_inc(summed, 1)
            pe.wait_ge(logged, 1)
            pe.wait_ge(w_in, 32)
            pe.wait_ge(x_in, 16 * BT)
            for j in range(BT):
                if j >= 2:
                    pe.wait_ge(r_done, j - 1)
                    pe.wait_ge(i_done, j - 1)
                for w, done, s in ((wa, r_product, 2 * (j % 2)), (wx, x_product, 2 * (j % 2) + 1)):
                    for h in range(2):
                        mm = pe.matmul(ps[:, s, h * HALF:(h + 1) * HALF], w[:, j], xc[:, j, h * HALF:(h + 1) * HALF],
                                       start=True, stop=True)
                    mm.then_inc(done, 1)
            pe.wait_ge(r_done, BT)
            pe.wait_ge(i_done, BT)
            pe.wait_ge(scaled, DC)
            pe.wait_ge(mem_w_in, 32)
            for j in range(BT):
                for k in range(DC):
                    mm = pe.matmul(m.ps[:, j, 0:MEM], wt[:, j, k * P:(k + 1) * P], mem[:, k],
                                   start=(k == 0), stop=(k == DC - 1))
                mm.then_inc(k_done, 1)
            for j in range(MEM // P):
                for k in range(DC):
                    mm = pe.matmul(m.ps[:, BT + j, :], mem[:, k, j * P:(j + 1) * P], wv[:, k],
                                   start=(k == 0), stop=(k == DC - 1))
                mm.then_inc(v_done, 1)

        @block.scalar
        def _(act):
            act.preload_act_table_set(LN_EXP)
            act.wait_ge(mem_in, 16)
            for k in range(DC):
                if k >= 2:
                    act.wait_ge(summed, k - 1)
                act.activation(mem_sq[:, k % 2], mem[:, k], ACT.Square).then_inc(squared, 1)
            act.wait_ge(summed, DC)
            act.activation(mem_root, m.ps[:, 0, 0:MEM], ACT.Ln, bias=m.c(C_EPS, 1), scale=1.0 / D).then_inc(logged, 1)
            act.wait_ge(logged, 1)
            act.activation(mem_root, mem_root, ACT.Exp, scale=-0.5).then_inc(rooted, 1)
            for j in range(BT):
                act.wait_ge(r_product, j + 1)
                act.activation(r[:, j], ps[:, 2 * (j % 2)], ACT.Sigmoid, bias=m.p("d_ba", j)).then_inc(r_done, 1)
                act.wait_ge(x_product, j + 1)
                act.activation(ig[:, j], ps[:, 2 * (j % 2) + 1], ACT.Sigmoid, bias=m.p("d_bx", j)).then_inc(i_done, 1)
            act.wait_ge(negated, 1)
            for j in range(BT):
                act.wait_ge(r_done, j + 1)
                act.activation(th[:, j], r[:, j], ACT.Tanh, scale=m.rate[:, j:j + 1]).then_inc(t_done, 1)
            for j in range(BT):
                act.activation(a[:, j], r[:, j], ACT.Exp, scale=neg[:, j:j + 1]).then_inc(a_done, 1)
            act.preload_act_table_set(LN_EXP)
            for j in range(BT):
                act.wait_ge(t_done, j + 1)
                act.wait_ge(weighed, j + 1)
                act.activation(root[:, j], th[:, j], ACT.Ln, bias=1.0).then_inc(ln_done, 1)
            for j in range(BT):
                act.wait_ge(ln_done, j + 1)
                act.activation(root[:, j], root[:, j], ACT.Exp, scale=-0.5).then_inc(inv_root, 1)
            for j in range(BT):
                act.activation(th[:, j], th[:, j], ACT.Sqrt, scale=2.0).then_inc(t_root, 1)
            for j in range(BT):
                act.wait_ge(k_done, j + 1)
                act.activation(mem_k[:, j], m.ps[:, j, 0:MEM], ACT.Copy).then_inc(kv_kept, 1)
            for j in range(MEM // P):
                act.wait_ge(v_done, j + 1)
                act.activation(mem_v[:, j], m.ps[:, BT + j, :], ACT.Copy).then_inc(kv_kept, 1)

        @block.vector
        def _(dve):
            dve.tensor_scalar(neg, m.rate, -1.0, None, ALU.mult).then_inc(negated, 1)
            dve.memset(row[0:8], NEG).then_inc(cleared, 1)
            dve.wait_ge(cleared, 1)
            dve.wait_ge(rel_in, 16)
            for b, lo, hi in ranges:
                dve.tensor_copy(row[0:8, 256 - hi:256 - lo], rel[0:8, b:b + 1].to_broadcast([8, hi - lo])).then_inc(placed, 1)
            dve.memset(bias0[:, :, 0:P], NEG).then_inc(first_done, 1)
            dve.wait_ge(rooted, 1)
            for k in range(DC):
                dve.scalar_tensor_tensor(mem[:, k], mem[:, k], m.p("mem_g", k), mem_root, ALU.mult, ALU.mult).then_inc(scaled, 1)
            for j in range(BT):
                dve.wait_ge(i_done, j + 1)
                dve.tensor_tensor(ig[:, j], ig[:, j], xc[:, j], ALU.mult).then_inc(weighed, 1)
            for j in range(BT):
                dve.wait_ge(inv_root, j + 1)
                dve.tensor_tensor(ig[:, j], ig[:, j], root[:, j], ALU.mult).then_inc(half_b, 1)
            dve.wait_ge(band_in, 128)
            dve.tensor_copy(bias0[:, :, P:2 * P], bias[:, :, P:2 * P]).then_inc(first_done, 1)
            dve.wait_ge(z_in, 16)
            for j in range(BT):
                dve.wait_ge(t_root, j + 1)
                dve.wait_ge(half_b, j + 1)
                dve.tensor_tensor(ig[:, j], ig[:, j], th[:, j], ALU.mult).then_inc(b_done, 1)
                dve.wait_ge(a_done, j + 1)
                dve.wait_ge(b_done, j + 1)
                dve.tensor_tensor_scan(root[:, j], a[:, j], ig[:, j], 0.0, ALU.mult, ALU.add).then_inc(scanned, 1)
                dve.wait_ge(scanned, j + 1)
                dve.tensor_tensor(z[:, j], z[:, j], root[:, j], ALU.mult).then_inc(gated, 1)


def window_phase(nc, m, d, heads_n, scale, q_tiles, gate_tiles, y_tiles, window, biases, sink, place, q_of, k_of, v_of,
                 out_of):
    H, U, N = heads_n, heads_n // 2, NB
    qs, zs, ys = m.take(2, BT, P), m.take(2, BT, P), m.take(2, BT, P)
    win = m.take(2, 3, 2 * P) if window is not None else None
    vt = m.take(2, 2, P)
    sc = m.take(2, H, 2 * P)
    pt = m.take(2, BW)
    mx, nm, rs, ri, dk, es = (m.take(2, H) for _ in range(6))
    scores_ps = m.ps[:, 0:H // 2, :].rearrange("p b (h k) -> p (b h) k", k=2 * P)
    turned = [m.ps[:, 4 + s] for s in range(2)]
    out_ps, v_ps = m.ps[:, 6], m.ps[:, 7, 0:2 * P]
    loads = 1 if window is None else 2
    with phase(nc, "cleared", "staged_a", "staged_b", "z_a", "z_b", "v_turned", "v_kept", "s_done", "s_kept", "max_done", "max_sink",
               "negated", "sink_diff", "p_ready", "sink_exp", "sum_done", "inverted", "p_scaled", "t_done",
               "t_kept_low", "t_kept_high", "o_done", "o_kept", "y_out_a", "y_out_b") as (
            block, cleared, staged_a, staged_b, z_a, z_b, v_turned, v_kept, s_done, s_kept, max_done, max_sink,
            negated, sink_diff, p_ready, sink_exp, sum_done, inverted, p_scaled, t_done,
            t_kept_low, t_kept_high, o_done, o_kept, y_out_a, y_out_b):
        staged, z_in, y_out = (staged_a, staged_b), (z_a, z_b), (y_out_a, y_out_b)

        def rounds(eng, body):
            for n in range(2):
                body(n, n)
            with eng.Fori(1, N // 2 - 1) as i:
                for s in range(2):
                    body(2 * i + s, s)
            for n in range(N - 2, N):
                body(n, n % 2)

        def first(n, below=2):
            return isinstance(n, int) and n < below

        def kept(n, u):
            return (t_kept_low, n * (U // 2) + u + 1) if u < U // 2 else (t_kept_high, n * (U // 2) + u - U // 2 + 1)

        @block.sync
        def _(sp):
            def stage(n, s):
                if not first(n):
                    sp.wait_ge(s_done, n - 1)
                    if window is not None:
                        sp.wait_ge(v_turned, n - 1)
                to = staged[s]
                sp.dma_start(qs[:, s], d["in2"][q_tiles:q_tiles + BT, :, bass.ds(n * P, P)].rearrange("c p t -> p c t")).then_inc(to, 16)
                if window is not None:
                    if first(n, 1):
                        sp.wait_ge(cleared, 1)
                        sp.dma_start(win[:, s, :, P:2 * P], d["in2"][window:window + 3, :, 0:P].rearrange("c p t -> p c t")).then_inc(to, 16)
                    else:
                        sp.dma_start(win[:, s], d["in2"][window:window + 3, :, bass.ds(n * P - P, 2 * P)].rearrange("c p t -> p c t")).then_inc(to, 16)

            def leave(n, s):
                sp.wait_ge(o_kept, n + 1)
                sp.dma_start(d["y"][y_tiles:y_tiles + BT, :, bass.ds(n * P, P)].rearrange("c p t -> p c t"), ys[:, s]).then_inc(y_out[s], 16)

            def body(n, s):
                if not (isinstance(n, int) and n == N - 1):
                    stage(n + 1, 1 - s)
                if not first(n):
                    leave(n - 2, s)
                sp.dma_start(zs[:, s], d["in2"][gate_tiles:gate_tiles + BT, :, bass.ds(n * P, P)].rearrange("c p t -> p c t")).then_inc(z_in[s], 16)
            stage(0, 0)
            rounds(sp, body)
            leave(N - 2, 0)
            leave(N - 1, 1)
            for s in range(2):
                sp.wait_ge(y_out[s], 8 * N)

        @block.tensor
        def _(pe):
            def scores(n, s):
                pe.wait_ge(staged[s], 8 * loads * (n - s) + 16 * loads)
                if not first(n, 1):
                    pe.wait_ge(s_kept, n)
                for u in range(U):
                    for g in range(2):
                        mm = pe.matmul(scores_ps[:, place(u, g)], q_of(qs[:, s], u, g), k_of(win[:, s] if win is not None else None, u, g),
                                       start=True, stop=True)
                mm.then_inc(s_done, 1)
                if window is not None:
                    if not first(n, 1):
                        pe.wait_ge(v_kept, n)
                    for c in range(2):
                        mm = pe.transpose(v_ps[:, c * P:(c + 1) * P], win[:, s, 2, c * P:(c + 1) * P], m.c(C_ID))
                    mm.then_inc(v_turned, 1)

            def values(n, s):
                for t in range(U + 1):
                    if t < U:
                        pe.wait_ge(p_scaled, n + 1)
                        if t >= 2:
                            pe.wait_ge(*kept(n, t - 2))
                        elif not first(n, 1):
                            pe.wait_ge(*kept(n - 1, U + t - 2))
                        for g in range(2):
                            for kb in range(2):
                                c = 2 * g + kb
                                mm = pe.transpose(turned[t % 2][:, c * P:(c + 1) * P], sc[:, s, place(t, g), kb * P:(kb + 1) * P],
                                                  m.c(C_ID))
                        mm.then_inc(t_done, 1)
                    if t >= 1:
                        u = t - 1
                        pe.wait_ge(*kept(n, u))
                        if u == 0:
                            if window is not None:
                                pe.wait_ge(v_kept, n + 1)
                            if not first(n, 1):
                                pe.wait_ge(o_kept, n)
                        for g in range(2):
                            for kb in range(2):
                                c = 2 * g + kb
                                mm = pe.matmul(out_of(out_ps, u, g), v_of(vt[:, s], u, g, kb), pt[:, u % 2, c * P:(c + 1) * P],
                                               start=(kb == 0), stop=(kb == 1))
                        mm.then_inc(o_done, 1)

            def body(n, s):
                if not (isinstance(n, int) and n == N - 1):
                    scores(n + 1, 1 - s)
                values(n, s)
            scores(0, 0)
            rounds(pe, body)

        @block.vector
        def _(dve):
            if window is not None:
                dve.memset(win[:, 0, :, 0:P], 0.0).then_inc(cleared, 1)

            def body(n, s):
                dve.wait_ge(s_done, n + 1)
                if not first(n):
                    dve.wait_ge(t_done, (n - 1) * U)
                if biases is None:
                    dve.tensor_scalar(sc[:, s], scores_ps, scale, None, ALU.mult).then_inc(s_kept, 1)
                else:
                    bias = biases[first(n, 1)]
                    dve.scalar_tensor_tensor(sc[:, s], scores_ps, scale, bias, ALU.mult, ALU.add).then_inc(s_kept, 1)
                dve.wait_ge(s_kept, n + 1)
                if not first(n, 1):
                    dve.wait_ge(negated, n)
                dve.tensor_reduce(mx[:, s], sc[:, s], AX.X, ALU.max).then_inc(max_done, 1)
                dve.wait_ge(max_done, n + 1)
                if sink:
                    dve.tensor_tensor(mx[:, s], mx[:, s], m.p("sinks", 0, H), ALU.max).then_inc(max_sink, 1)
                    dve.wait_ge(max_sink, n + 1)
                    dve.tensor_tensor(dk[:, s], m.p("sinks", 0, H), mx[:, s], ALU.subtract).then_inc(sink_diff, 1)
                dve.tensor_scalar(nm[:, s], mx[:, s], -1.0, None, ALU.mult).then_inc(negated, 1)
                if not first(n, 1):
                    turn_high(n - 1)
                dve.wait_ge(p_ready, H * n + H)
                if sink:
                    dve.wait_ge(sink_exp, n + 1)
                    dve.tensor_tensor(rs[:, s], rs[:, s], es[:, s], ALU.add).then_inc(sum_done, 1)
                    dve.wait_ge(sum_done, n + 1)
                if not first(n, 1):
                    dve.wait_ge(p_scaled, n)
                dve.reciprocal(ri[:, s], rs[:, s]).then_inc(inverted, 1)
                dve.wait_ge(inverted, n + 1)
                dve.tensor_tensor(sc[:, s], sc[:, s], ri[:, s].unsqueeze(2).to_broadcast([P, H, 2 * P]),
                                  ALU.mult).then_inc(p_scaled, 1)
                if not first(n, 1):
                    gate(n - 1, 1 - s)

            def turn_high(n):
                for u in range(U // 2, U):
                    dve.wait_ge(t_done, n * U + u + 1)
                    if not first(n, 1) or u >= 2:
                        dve.wait_ge(o_done, n * U + u - 1)
                    dve.tensor_copy(pt[:, u % 2], turned[u % 2]).then_inc(t_kept_high, 1)

            def gate(n, s):
                dve.wait_ge(o_done, (n + 1) * U)
                dve.wait_ge(z_in[s], 8 * (n - s) + 16)
                if not first(n):
                    dve.wait_ge(y_out[s], 8 * (n - s))
                dve.tensor_tensor(ys[:, s], out_ps.rearrange("p (c t) -> p c t", t=P), zs[:, s], ALU.mult).then_inc(o_kept, 1)
            for n in range(4):
                body(n, n % 2)
            with dve.Fori(2, N // 2) as i:
                for s in range(2):
                    body(2 * i + s, s)
            turn_high(N - 1)
            gate(N - 1, 1)

        @block.scalar
        def _(act):
            def turn(n, u):
                act.wait_ge(t_done, n * U + u + 1)
                if not first(n, 1) or u >= 2:
                    act.wait_ge(o_done, n * U + u - 1)
                act.activation(pt[:, u % 2], turned[u % 2], ACT.Copy).then_inc(t_kept_low, 1)

            def exponentials(n, s):
                act.wait_ge(negated, n + 1)
                for h in range(H):
                    act.activation(sc[:, s, h], sc[:, s, h], ACT.Exp, bias=nm[:, s, h:h + 1],
                                   accum_out=rs[:, s, h:h + 1]).then_inc(p_ready, 1)

            def body(n, s):
                if window is not None:
                    act.wait_ge(v_turned, n + 1)
                    if not first(n):
                        act.wait_ge(o_done, (n - 1) * U)
                    act.activation(vt[:, s], v_ps.rearrange("p (c f) -> p c f", c=2), ACT.Copy).then_inc(v_kept, 1)
                if not first(n, 1):
                    for u in range(U // 2):
                        turn(n - 1, u)
                exponentials(n, s)
                if sink:
                    act.wait_ge(sink_diff, n + 1)
                    act.activation(es[:, s], dk[:, s], ACT.Exp).then_inc(sink_exp, 1)
            for n in range(4):
                body(n, n % 2)
            with act.Fori(2, N // 2) as i:
                for s in range(2):
                    body(2 * i + s, s)
            for u in range(U // 2):
                turn(N - 1, u)


SWA_ORDER = [2 * t + g for g in range(2) for t in range(BT)]


def recurrence_attention_phases(nc, m, d):
    m.clear()
    mem_k, mem_v = m.take(BT, MEM), m.take(MEM // P, BW)
    bias, bias0 = m.take(8, 2 * P), m.take(8, 2 * P)
    base = m.top
    recurrence_keys_phase(nc, m, d, bias, bias0, mem_k, mem_v)
    m.top = base
    window_phase(
        nc, m, d, 8, 64.0 ** -0.5, T_CQ, T_CZ, 2 * BT, T_CK, (bias, bias0), True,
        place=lambda u, g: BT * g + u,
        q_of=lambda q, u, g: q[64 * g:64 * g + 64, u],
        k_of=lambda win, u, g: win[64 * g:64 * g + 64, u // 2],
        v_of=lambda v, u, g, kb: v[:, kb, 64 * (u // 2):64 * (u // 2) + 64],
        out_of=lambda bank, u, g: bank[64 * g:64 * g + 64, u * P:(u + 1) * P])
    m.top = base
    window_phase(
        nc, m, d, 4, float(P) ** -0.5, T_EQ, T_EZ, 4 * BT, None, None, False,
        place=lambda u, g: 2 * u + g,
        q_of=lambda q, u, g: q[:, 2 * u + g],
        k_of=lambda win, u, g: mem_k[:, 2 * u + g],
        v_of=lambda v, u, g, kb: mem_v[:, kb, (2 * u + g) * P:(2 * u + g + 1) * P],
        out_of=lambda bank, u, g: bank[:, (2 * u + g) * P:(2 * u + g + 1) * P])


def merge_phase(nc, m, d, merged):
    raw_y = m.take(BT, S)
    y = m.take_split("y", BT, S)
    raw_g, raw_b = m.take(2, DC, P), m.take(2, BT, P)
    wg, wb = m.take_split("wg", 2, DC, P), m.take_split("wb", 2, BT, P)
    sg = m.take(2, S)
    gate_ps = m.ps[:, 0:4, :].rearrange("p (s h) f -> p s (h f)", s=2)
    br_ps = m.ps[:, 4:8, :].rearrange("p (s h) f -> p s (h f)", s=2)
    gate_bias = m.p("b_gate", 0, 40)
    T = DC
    with phase(nc, "y_in", "y_hi", "y_lo", "wg_a", "wg_b", "wb_a", "wb_b", "w_hi", "w_lo", "gate_done", "branch_done",
               "sig_done", "weighted", "added") as (
            block, y_in, y_hi, y_lo, wg_a, wg_b, wb_a, wb_b, w_hi, w_lo, gate_done, branch_done,
            sig_done, weighted, added):
        g_in, b_in = (wg_a, wg_b), (wb_a, wb_b)

        def start(n, u):
            return isinstance(n, int) and n == 0 and u < 2

        @block.sync
        def _(sp):
            def branch(n):
                for u in range(T):
                    s = u % 2
                    if not start(n, u):
                        sp.wait_ge(w_lo, n * T + u - 1)
                    sp.dma_start(raw_g[:, s].rearrange("p k f -> p (k f)"), d["w_gate"][n * DC + u]).then_inc(g_in[s], 16)
                    sp.dma_start(raw_b[:, s].rearrange("p k f -> p (k f)"), d["w_br"][n, u]).then_inc(b_in[s], 16)
                    if u == 1:
                        if not isinstance(n, int):
                            sp.wait_ge(y_lo, n * BT)
                        sp.dma_start(raw_y, d["y"][bass.ds(n * BT, BT)].rearrange("c p t -> p c t")).then_inc(y_in, 16)
            loop(sp, NBR, branch)

        @block.gpsimd
        def _(pool):
            def branch(n):
                for u in range(T):
                    s = u % 2
                    pool.wait_ge(w_hi, n * T + u + 1)
                    if not start(n, u):
                        pool.wait_ge(branch_done, n * T + u - 1)
                    pool.tensor_tensor(wg.lo[:, s], raw_g[:, s], wg.hi[:, s].bitcast(F32), ALU.subtract)
                    pool.tensor_tensor(wb.lo[:, s], raw_b[:, s], wb.hi[:, s].bitcast(F32), ALU.subtract).then_inc(w_lo, 1)
            loop(pool, NBR, branch)

        @block.tensor
        def _(pe):
            def branch(n):
                for u in range(T):
                    s = u % 2
                    pe.wait_ge(w_lo, n * T + u + 1)
                    if not start(n, u):
                        pe.wait_ge(sig_done, n * T + u - 1)
                    product_of(pe, gate_ps[:, s], wg[:, s], m.split, DC).then_inc(gate_done, 1)
                    if u == 0:
                        pe.wait_ge(y_lo, n * BT + BT)
                    if not start(n, u):
                        pe.wait_ge(weighted, n * T + u - 1)
                    product_of(pe, br_ps[:, s], wb[:, s], y, BT).then_inc(branch_done, 1)
            loop(pe, NBR, branch)

        @block.scalar
        def _(act):
            def high(n, u):
                s = u % 2
                act.wait_ge(g_in[s], 16 * (n * (T // 2) + u // 2) + 16)
                act.wait_ge(b_in[s], 16 * (n * (T // 2) + u // 2) + 16)
                if not start(n, u):
                    act.wait_ge(branch_done, n * T + u - 1)
                act.activation(wg.hi[:, s], raw_g[:, s], ACT.Copy)
                act.activation(wb.hi[:, s], raw_b[:, s], ACT.Copy).then_inc(w_hi, 1)

            def branch(n, products_left=True):
                act.wait_ge(y_in, 16 * n + 16)
                if not start(n, 0):
                    act.wait_ge(branch_done, n * T)
                for k in range(BT):
                    act.activation(y.hi[:, k], raw_y[:, k], ACT.Copy).then_inc(y_hi, 1)
                for u in range(T):
                    s = u % 2
                    act.wait_ge(gate_done, n * T + u + 1)
                    if not start(n, u):
                        act.wait_ge(added, n * T + u - 1)
                    act.activation(sg[:, s], gate_ps[:, s], ACT.Sigmoid,
                                   bias=gate_bias[:, bass.ds(n * DC + u, 1)]).then_inc(sig_done, 1)
                    if products_left or u + 2 < T:
                        high(n, u + 2)
            high(0, 0)
            high(0, 1)
            branch(0)
            with act.Fori(1, NBR - 1) as n:
                branch(n)
            branch(NBR - 1, False)

        @block.vector
        def _(dve):
            def branch(n):
                for k in range(BT):
                    dve.wait_ge(y_hi, n * BT + k + 1)
                    dve.tensor_tensor(y.lo[:, k], raw_y[:, k], y.hi[:, k].bitcast(F32), ALU.subtract).then_inc(y_lo, 1)
                for u in range(T):
                    s = u % 2
                    dve.wait_ge(sig_done, n * T + u + 1)
                    dve.wait_ge(branch_done, n * T + u + 1)
                    if isinstance(n, int):
                        dve.tensor_tensor(merged[:, u], sg[:, s], br_ps[:, s], ALU.mult).then_inc(weighted, 1)
                        dve.wait_ge(weighted, n * T + u + 1).then_inc(added, 1)
                    else:
                        dve.tensor_tensor(sg[:, s], sg[:, s], br_ps[:, s], ALU.mult).then_inc(weighted, 1)
                        dve.wait_ge(weighted, n * T + u + 1)
                        dve.wait_ge(added, n * T + u)
                        dve.tensor_tensor(merged[:, u], merged[:, u], sg[:, s], ALU.add).then_inc(added, 1)
            loop(dve, NBR, branch)


def second_block(nc, m, d):
    m.clear(top=A_WORK)
    norm_phase(nc, m, m.res, m.split, m.p("pre_g", 0, 8), DC, (m.take(2, S), m.take(S)), spill=d["res"])
    m.clear(top=A_WORK)
    y = m.take(BT, S)
    base = m.top
    in2_phase(nc, m, d, y)
    m.top = base
    conformer_phase(nc, m, d, y)
    m.clear(top=A_WORK)
    ab = m.take(NB, 8)
    beta_alpha_phase(nc, m, d, ab)
    small_phase(nc, m, ab)
    delta_phases(nc, m, d)
    recurrence_attention_phases(nc, m, d)
    m.clear(top=A_WORK)
    norm_phase(nc, m, m.res, m.split, m.p("pre_g", 0, 8), DC, (m.take(2, S), m.take(S)))
    m.clear(top=A_WORK)
    merge_phase(nc, m, d, m.res)
    split_phase(nc, m.res, m.split, DC)
    m.clear(top=A_WORK, end=A_ACT)
    gemm_phase(nc, m, d["w_out"], m.split, DC, DC, "keep", dst=m.act, reload=(m.res, d["res"]))
    m.clear(top=A_WORK, end=A_ACT)
    norm_phase(nc, m, m.act, m.act, m.p("post_g", 0, 8), DC, (m.take(2, S), m.take(S)), residual=m.res, out=d["out"])


FF_PARTS = 4
SCRATCH = {
    "rope": (2, P, S), "in1": (13, P, S), "v_sb": (NB, P, BW), "k_rope": (ROPE, S), "q_rope": (2 * P, S),
    "mla_q": (MLA_H, P, S), "mla_k": (MLA_H, P, S), "mla_v": (NB, P, BW),
    "in2": (N_IN2, P, S), "delta": (2 * BT, P, S), "kv_rows": (NB, P, 3 * BW),
    "band": (8, P, 384), "res": (DC, P, S), "mem_v": (MEM // P, P, BW), "y": (NBR * BT, P, S),
}


def first_block(nc, m, d):
    load_phase(nc, m, d)
    m.clear(top=A_WORK)
    norm_phase(nc, m, m.res, m.split, m.p("attn_g", 0, 8), DC, (m.take(2, S), m.take(S)))
    m.clear(top=A_WORK)
    gemm_phase(nc, m, d["w_in1"], m.split, DC, 13, "store", out=d["in1"])
    m.clear(top=A_WORK)
    rows_phase(nc, m, m.split, DC, d["w_v1"], BW, NB, d["v_sb"])
    stick_phase(nc, m, d)
    latent_phases(nc, m, d)
    latent_attention_phase(nc, m, d)
    m.clear(top=A_WORK, end=A_ACT)
    scratch = (m.take(2, S), m.take(S))
    norm_phase(nc, m, m.act[:, 0:4], m.split[:, 0:4], m.p("sb_g", 0, 4), 4, scratch)
    norm_phase(nc, m, m.act[:, 4:8], m.split[:, 4:8], m.p("mla_g", 0, 4), 4, scratch)
    m.clear(top=A_WORK)
    gemm_phase(nc, m, d["w_o"], m.split, DC, DC, "add", dst=m.res)
    m.clear(top=A_WORK)
    norm_phase(nc, m, m.res, m.split, m.p("mlp_g", 0, 8), DC, (m.take(2, S), m.take(S)))
    m.clear(top=A_WORK)
    mlp_phase(nc, m, d["w_mlp"], FF_PARTS)
    m.clear(top=A_WORK)
    norm_phase(nc, m, m.res, m.res, m.p("final_g", 0, 8), DC, (m.take(2, S), m.take(S)))


def program(nc, d):
    for name, shape in SCRATCH.items():
        d[name] = nc.dram_tensor("scratch_" + name, shape, F32).ap()
    m = Mem(nc)
    first_block(nc, m, d)
    second_block(nc, m, d)


def layout(inp):
    g = {k: np.asarray(v) for k, v in inp.items()}

    def tiles(w):
        k, n = w.shape
        return np.ascontiguousarray(w.reshape(k // P, P, n // P, P).transpose(2, 1, 0, 3).reshape(n // P, P, k))

    def rows(w):
        k, n = w.shape
        return np.ascontiguousarray(w.reshape(k // P, P, n).transpose(1, 0, 2))

    def cols(v):
        return v.reshape(-1, P).T

    def swap(w):
        k, n = w.shape
        return w.reshape(k, n // ROPE, 2, ROPE // 2)[:, :, ::-1].reshape(k, n)

    w_in, w_qb, w_kvb = g["w_in"][0], g["w_q_b"][0], g["w_kv_b"][0]
    kr = w_in[:, 1920:1984]
    qb = w_qb.reshape(Q_LORA, MLA_H, NOPE + ROPE)
    qr = qb[:, :, NOPE:].reshape(Q_LORA, MLA_H * ROPE)
    kvb = w_kvb.reshape(KV_LORA, MLA_H, 2 * P)
    out = {
        "x": np.ascontiguousarray(g["x"][0].T),
        "positions": g["positions"],
        "w_in1": tiles(np.concatenate([w_in[:, 0:1024], w_in[:, 1536:1920], kr, kr, swap(kr), swap(kr)], 1)),
        "w_v1": rows(w_in[:, 1024:1536]),
        "w_qn": tiles(qb[:, :, :NOPE].reshape(Q_LORA, -1)),
        "w_qr": tiles(np.concatenate([qr, swap(qr)], 1)),
        "w_kn": tiles(kvb[:, :, :P].reshape(KV_LORA, -1)),
        "w_vm": rows(np.ascontiguousarray(kvb[:, :, P:]).reshape(KV_LORA, -1)),
        "w_o": tiles(g["w_o"][0]),
        "w_mlp": np.concatenate([tiles(part) for up_down in zip(np.split(g["w_up"][0], FF_PARTS, axis=1),
                                                                np.split(g["w_down"][0], FF_PARTS, axis=0))
                                 for part in up_down]),
    }
    w2, b2 = g["w_in_2"][0], g["b_in_2"][0]
    off = np.cumsum([0, 1536, 512, 4, 4, 1024, 512, 512, 256, 512, 512, 512, 512, 512, 5120])
    (qkv, az, be, al, glu, bz, cq, ckv, cz, dx, dz, eq, ez, gate) = [(off[n], off[n + 1]) for n in range(14)]

    def pick(a):
        ck = a[..., ckv[0]:ckv[0] + 128]
        cv = a[..., ckv[0] + 128:ckv[1]]
        k0, k1 = ck[..., :64], ck[..., 64:]
        part = [a[..., lo:hi] for lo, hi in (qkv, dx, glu, az, bz, cz, dz, ez, cq)]
        part += [k0, k0, k1, k1, cv, a[..., eq[0]:eq[1]]]
        return np.concatenate(part, -1)

    wbr = g["w_br_2"][0]

    def diagonal(w):
        t = np.zeros((BT, P, P), w.dtype)
        for n in range(BT):
            t[n, :64, :64] = w[2 * n]
            t[n, 64:, 64:] = w[2 * n + 1]
        return np.ascontiguousarray(t.transpose(1, 0, 2))

    def taps(w):
        k, c = w.shape
        return w.T.reshape(c // P, P, k).transpose(1, 0, 2).reshape(P, -1)

    def spread(v):
        return np.broadcast_to(v.reshape(1, -1), (P, v.size))

    out.update({
        "mem": np.ascontiguousarray(g["mem_2"][0].T),
        "w_in2": tiles(pick(w2)),
        "w_ab": rows(np.concatenate([w2[:, be[0]:be[1]], w2[:, al[0]:al[1]]], 1)),
        "w_gate": tiles(w2[:, gate[0]:]),
        "w_br": np.stack([tiles(wbr[n]) for n in range(NBR)]),
        "w_out": tiles(g["w_out_2"][0]),
        "w_mk": tiles(g["w_mem_kv_2"][0][:, :BW]),
        "w_mv": rows(g["w_mem_kv_2"][0][:, BW:]),
        "w_da": diagonal(g["d_w_a_2"][0]),
        "w_dx": diagonal(g["d_w_x_2"][0]),
        "rel_bias": np.ascontiguousarray(g["rel_bias_2"].T[SWA_ORDER]),
        "consts": constants(),
    })
    vec = {
        "attn_g": cols(g["attn_norm_g"][0]), "q_a_g": cols(g["q_a_norm_g"][0]), "kv_a_g": cols(g["kv_a_norm_g"][0]),
        "sb_g": cols(g["sb_out_norm_g"][0]), "mla_g": cols(g["mla_out_norm_g"][0]), "mlp_g": cols(g["mlp_norm_g"][0]),
        "final_g": cols(g["final_norm_g"]), "pre_g": cols(g["g_pre_2"][0]), "post_g": cols(g["g_post_2"][0]),
        "mem_g": cols(g["g_mem_2"][0]), "b_in": cols(pick(b2)), "b_gate": cols(b2[gate[0]:]),
        "a_conv": taps(g["a_conv_w_2"][0]), "a_norm": cols(g["a_norm_g_2"][0]), "b_conv": taps(g["b_dw_w_2"][0]),
        "b_conv_b": cols(g["b_dw_b_2"][0]), "b_ln_g": cols(g["b_ln_g_2"][0]), "b_ln_b": cols(g["b_ln_b_2"][0]),
        "d_conv": taps(g["d_conv_w_2"][0]), "d_conv_b": cols(g["d_conv_b_2"][0]), "d_ba": cols(g["d_b_a_2"][0]),
        "d_bx": cols(g["d_b_x_2"][0]), "d_lam": cols(g["d_lambda_2"][0]),
        "ab_bias": spread(np.concatenate([b2[be[0]:be[1]], b2[al[0]:al[1]]])),
        "a_log": spread(g["a_log_2"][0]), "a_dt": spread(g["a_dt_bias_2"][0]), "sinks": spread(g["c_sinks_2"][0][SWA_ORDER]),
    }
    for n, w in _PAR:
        assert vec[n].shape == (P, w), (n, vec[n].shape)
    out["params"] = np.ascontiguousarray(np.concatenate([vec[n] for n, _ in _PAR], 1))
    return out


def kernel(**inputs):
    import concourse.bacc as _bacc
    from concourse.bass_utils import run_bass_kernel_spmd as _run

    nc = _bacc.Bacc("TRN2", target_bir_lowering=False, num_devices=1)
    arrays, d = {}, {}
    for name, a in layout(inputs).items():
        arrays["in_" + name] = a
        d[name] = nc.dram_tensor("in_" + name, a.shape, mybir.dt.from_np(a.dtype), kind="ExternalInput").ap()
    d["out"] = nc.dram_tensor("out_x", (D, S), F32, kind="ExternalOutput").ap()
    program(nc, d)
    r = _run(nc, [arrays], core_ids=[0])
    return np.ascontiguousarray(r.results[0]["out_x"].T)[None]
```
